# Optimizing a Trainium2 kernel written in Bass

```python
import math
import jax, jax.numpy as jnp
from jax import lax
import numpy as np

D_MODEL = 1024
BATCH = 1
SEQ = 512
DEPTH = 1

CHUNK = 64
Q_BLOCK = 128
ATT_HEADS = 8
ATT_HEAD_DIM = 64
ATT_WIDTH = ATT_HEADS * ATT_HEAD_DIM
IDX_HEADS = 8
IDX_DIM = 64
TOPK_MAX = 256
REL_BUCKETS = 32
REL_MAX_DIST = 1024
CONV_CH = 512
CONV_WIDTH = 31
N_BRANCH = 2
PEER_HEADS = 8
N_KEYS = 128
N_EXPERTS = N_KEYS * N_KEYS
PEER_QDIM = 256
PEER_HALF = PEER_QDIM // 2
PEER_TOPK = 16
PEER_TOKEN_BLOCK = 128
PLE_DIM = 256
EPS = 1e-6

IN_WIDTHS = (ATT_WIDTH, ATT_WIDTH, ATT_WIDTH, IDX_HEADS * IDX_DIM, IDX_DIM, IDX_HEADS, 2 * CONV_CH, N_BRANCH * D_MODEL)
IN_TOTAL = 3 * ATT_WIDTH + IDX_HEADS * IDX_DIM + IDX_DIM + IDX_HEADS + 2 * CONV_CH + N_BRANCH * D_MODEL


def _split_points():
    pts, acc = [], 0
    for w in IN_WIDTHS[:-1]:
        acc += w
        pts.append(acc)
    return pts

def rms_norm(x, g):
    x32 = x.astype(jnp.float32)
    y = x32 * lax.rsqrt(jnp.mean(x32 * x32, axis=-1, keepdims=True) + EPS)
    return (y * g.astype(jnp.float32)).astype(x.dtype)

def layer_norm(x, g, b):
    x32 = x.astype(jnp.float32)
    mu = jnp.mean(x32, axis=-1, keepdims=True)
    xc = x32 - mu
    y = xc * lax.rsqrt(jnp.mean(xc * xc, axis=-1, keepdims=True) + EPS)
    return (y * g.astype(jnp.float32) + b.astype(jnp.float32)).astype(x.dtype)

def t5_bucket(rel):
    half = REL_BUCKETS // 2
    max_exact = half // 2
    ret = jnp.where(rel > 0, half, 0)
    n = jnp.abs(rel)
    nf = jnp.maximum(n, 1).astype(jnp.float32)
    large = max_exact + (jnp.log(nf / max_exact) / math.log(REL_MAX_DIST / max_exact) * (half - max_exact)).astype(jnp.int32)
    large = jnp.minimum(large, half - 1)
    return ret + jnp.where(n < max_exact, n, large)

def dsa_attention(q, k, v, qi, ki, wi, rel_bias):
    B, S = q.shape[0], q.shape[1]
    topk = min(TOPK_MAX, S // 4)
    nb = S // Q_BLOCK
    key_chunk = jnp.arange(S, dtype=jnp.int32) // CHUNK
    scale = ATT_HEAD_DIM ** -0.5
    idx_scale = (IDX_DIM ** -0.5) * (IDX_HEADS ** -0.5)

    def blockify(a):
        return jnp.moveaxis(a.reshape((B, nb, Q_BLOCK) + a.shape[2:]), 1, 0)

    def one_block(args):
        qb, qib, wib, qpos = args
        qchunk = qpos // CHUNK
        dots = jax.nn.relu(jnp.einsum('bqhd,bsd->bqhs', qib, ki))
        score = jnp.einsum('bqhs,bqh->bqs', dots, wib) * idx_scale
        visible = key_chunk[None, :] <= qchunk[:, None]
        score = jnp.where(visible[None], score, -jnp.inf)
        _, sel = lax.top_k(score, topk)
        kg = jax.vmap(lambda kk, ii: kk[ii])(k, sel)
        vg = jax.vmap(lambda vv, ii: vv[ii])(v, sel)
        logits = jnp.einsum('bqhd,bqkhd->bqhk', qb, kg).astype(jnp.float32) * scale
        bias = rel_bias[t5_bucket(sel - qpos[None, :, None])]
        logits = logits + jnp.transpose(bias, (0, 1, 3, 2)).astype(jnp.float32)
        ok = (sel // CHUNK) <= qchunk[None, :, None]
        logits = jnp.where(ok[:, :, None, :], logits, -jnp.inf)
        probs = jax.nn.softmax(logits, axis=-1).astype(vg.dtype)
        return jnp.einsum('bqhk,bqkhd->bqhd', probs, vg)

    qpos_blocks = jnp.arange(S, dtype=jnp.int32).reshape(nb, Q_BLOCK)
    out = lax.map(one_block, (blockify(q), blockify(qi), blockify(wi), qpos_blocks))
    return jnp.moveaxis(out, 0, 1).reshape(B, S, ATT_WIDTH)

def conformer_conv(glu_in, conv_w, conv_b, ln_g, ln_b, w_proj):
    a, g = jnp.split(glu_in, 2, axis=-1)
    u = a * jax.nn.sigmoid(g)
    y = lax.conv_general_dilated(u, conv_w, window_strides=(1,), padding=[(CONV_WIDTH - 1, 0)],
                                 dimension_numbers=('NWC', 'WIO', 'NWC'), feature_group_count=CONV_CH)
    y = layer_norm(y + conv_b, ln_g, ln_b)
    return jax.nn.silu(y) @ w_proj

def peer(h, w_query, sub_keys, expert_u, expert_v):
    B, S, D = h.shape
    q = (h @ w_query).reshape(B, S, PEER_HEADS, 2, PEER_HALF)
    sc = jnp.einsum('bshcd,hckd->bshck', q, sub_keys)
    sv, si = lax.top_k(sc, PEER_TOPK)
    n_cand = PEER_TOPK * PEER_TOPK
    cand_s = (sv[..., 0, :, None] + sv[..., 1, None, :]).reshape(B, S, PEER_HEADS, n_cand)
    cand_i = (si[..., 0, :, None] * N_KEYS + si[..., 1, None, :]).reshape(B, S, PEER_HEADS, n_cand)
    top_s, top_j = lax.top_k(cand_s, PEER_TOPK)
    eidx = jnp.take_along_axis(cand_i, top_j, axis=-1)
    gate = jax.nn.softmax(top_s.astype(jnp.float32), axis=-1).astype(h.dtype)
    n_sel = PEER_HEADS * PEER_TOPK
    nb = (B * S) // PEER_TOKEN_BLOCK
    hb = h.reshape(nb, PEER_TOKEN_BLOCK, D)
    eb = eidx.reshape(nb, PEER_TOKEN_BLOCK, n_sel)
    gb = gate.reshape(nb, PEER_TOKEN_BLOCK, n_sel)

    def one_block(args):
        xt, et, gt = args
        u = expert_u[et]
        v = expert_v[et]
        act = jax.nn.gelu(jnp.einsum('tnd,td->tn', u, xt)) * gt
        return jnp.einsum('tn,tnd->td', act, v)

    return lax.map(one_block, (hb, eb, gb)).reshape(B, S, D)

def first_inputs(seed: int = 0) -> dict:
    key = jax.random.key(seed)
    ks = jax.random.split(key, 24)
    f = jnp.float32

    def nrm(k, shape, scale):
        return jax.random.normal(k, shape, f) * scale

    def gain(k, shape):
        return 1.0 + 0.05 * jax.random.normal(k, shape, f)

    return {
        'x': nrm(ks[0], (BATCH, SEQ, D_MODEL), 1.0),
        'p': nrm(ks[1], (DEPTH, BATCH, SEQ, PLE_DIM), 1.0),
        'rel_bias': nrm(ks[2], (REL_BUCKETS, ATT_HEADS), 0.1),
        'attn_norm_g': gain(ks[3], (DEPTH, D_MODEL)),
        'w_in': nrm(ks[4], (DEPTH, D_MODEL, IN_TOTAL), D_MODEL ** -0.5),
        'b_gate': nrm(ks[5], (DEPTH, N_BRANCH * D_MODEL), 0.02),
        'q_norm_g': gain(ks[6], (DEPTH, ATT_HEAD_DIM)),
        'k_norm_g': gain(ks[7], (DEPTH, ATT_HEAD_DIM)),
        'w_att_out': nrm(ks[8], (DEPTH, ATT_WIDTH, D_MODEL), ATT_WIDTH ** -0.5),
        'conv_w': nrm(ks[9], (DEPTH, CONV_WIDTH, 1, CONV_CH), CONV_WIDTH ** -0.5),
        'conv_b': nrm(ks[10], (DEPTH, CONV_CH), 0.02),
        'conv_ln_g': gain(ks[11], (DEPTH, CONV_CH)),
        'conv_ln_b': nrm(ks[12], (DEPTH, CONV_CH), 0.02),
        'w_conv_out': nrm(ks[13], (DEPTH, CONV_CH, D_MODEL), CONV_CH ** -0.5),
        'w_out': nrm(ks[14], (DEPTH, D_MODEL, D_MODEL), D_MODEL ** -0.5),
        'ffn_norm_g': gain(ks[15], (DEPTH, D_MODEL)),
        'w_peer_q': nrm(ks[16], (DEPTH, D_MODEL, PEER_HEADS * PEER_QDIM), D_MODEL ** -0.5),
        'peer_sub_keys': nrm(ks[17], (DEPTH, PEER_HEADS, 2, N_KEYS, PEER_HALF), PEER_HALF ** -0.5),
        'peer_u': nrm(ks[18], (DEPTH, N_EXPERTS, D_MODEL), D_MODEL ** -0.5),
        'peer_v': nrm(ks[19], (DEPTH, N_EXPERTS, D_MODEL), PEER_HEADS ** -0.5),
        'ple_norm_g': gain(ks[20], (DEPTH, D_MODEL)),
        'w_ple_gate': nrm(ks[21], (DEPTH, D_MODEL, D_MODEL), D_MODEL ** -0.5),
        'w_ple_proj': nrm(ks[22], (DEPTH, PLE_DIM, D_MODEL), PLE_DIM ** -0.5),
    }

def first_block(x, p, rel_bias, attn_norm_g, w_in, b_gate, q_norm_g, k_norm_g, w_att_out,
              conv_w, conv_b, conv_ln_g, conv_ln_b, w_conv_out, w_out, ffn_norm_g,
              w_peer_q, peer_sub_keys, peer_u, peer_v, ple_norm_g, w_ple_gate, w_ple_proj):
    B, S, D = x.shape
    for i in range(DEPTH):
        h = rms_norm(x, attn_norm_g[i])
        proj = h @ w_in[i]
        q, k, v, qi, ki, wi, glu_in, gates = jnp.split(proj, _split_points(), axis=-1)
        q = rms_norm(q.reshape(B, S, ATT_HEADS, ATT_HEAD_DIM), q_norm_g[i])
        k = rms_norm(k.reshape(B, S, ATT_HEADS, ATT_HEAD_DIM), k_norm_g[i])
        v = v.reshape(B, S, ATT_HEADS, ATT_HEAD_DIM)
        qi = qi.reshape(B, S, IDX_HEADS, IDX_DIM)
        y_att = dsa_attention(q, k, v, qi, ki, wi, rel_bias) @ w_att_out[i]
        y_conv = conformer_conv(glu_in, conv_w[i], conv_b[i], conv_ln_g[i], conv_ln_b[i], w_conv_out[i])
        g = jax.nn.sigmoid(gates + b_gate[i]).reshape(B, S, N_BRANCH, D)
        mixed = g[:, :, 0, :] * y_att + g[:, :, 1, :] * y_conv
        x = x + mixed @ w_out[i]
        h2 = rms_norm(x, ffn_norm_g[i])
        x = x + peer(h2, w_peer_q[i], peer_sub_keys[i], peer_u[i], peer_v[i])
        h3 = rms_norm(x, ple_norm_g[i])
        x = x + jax.nn.sigmoid(h3 @ w_ple_gate[i]) * (p[i] @ w_ple_proj[i])
    return x


CONV_WIDTH_2 = D_MODEL // 2
CONV_GROUPS = 8
CONV_K = 3
ATTN_HEADS = 8
HEAD_DIM = 64
ATTN_WIDTH = ATTN_HEADS * HEAD_DIM
FFN_HIDDEN = 2816
FFN_CONV_K = 3
IN_SPLITS = (CONV_WIDTH_2, CONV_WIDTH_2, CONV_WIDTH_2, ATTN_WIDTH, ATTN_WIDTH, ATTN_WIDTH, ATTN_HEADS, N_BRANCH * D_MODEL)
IN_WIDTH = sum(IN_SPLITS)


def rms_norm_2(x, g):
    x32 = x.astype(jnp.float32)
    y = x32 * lax.rsqrt(jnp.mean(x32 * x32, axis=-1, keepdims=True) + EPS)
    return y.astype(x.dtype) * g

def causal_dwconv(x, w):
    K = w.shape[0]
    S = x.shape[1]
    xp = jnp.pad(x, ((0, 0), (K - 1, 0), (0, 0)))
    y = xp[:, K - 1:K - 1 + S, :] * w[K - 1]
    for k in range(K - 1):
        y = y + xp[:, k:k + S, :] * w[k]
    return y

def forgetting_attention(q, k, v, log_f):
    B, S, H, hd = q.shape
    scale = 1.0 / np.sqrt(hd).astype(np.float32)
    F = jnp.cumsum(log_f, axis=1).transpose(0, 2, 1)
    qh = q.transpose(0, 2, 1, 3).astype(jnp.float32) * scale
    kh = k.transpose(0, 2, 1, 3).astype(jnp.float32)
    vh = v.transpose(0, 2, 1, 3).astype(jnp.float32)
    nb = S // Q_BLOCK
    q_blocks = qh.reshape(B, H, nb, Q_BLOCK, hd).transpose(2, 0, 1, 3, 4)
    fq_blocks = F.reshape(B, H, nb, Q_BLOCK).transpose(2, 0, 1, 3)
    k_pos = jnp.arange(S)

    def one_block(args):
        q_blk, fq_blk, i = args
        q_pos = i * Q_BLOCK + jnp.arange(Q_BLOCK)
        s = jnp.einsum('bhqd,bhkd->bhqk', q_blk, kh) + fq_blk[..., None] - F[:, :, None, :]
        s = jnp.where(k_pos[None, :] <= q_pos[:, None], s, -jnp.inf)
        p = jax.nn.softmax(s, axis=-1)
        return jnp.einsum('bhqk,bhkd->bhqd', p, vh)

    o = lax.map(one_block, (q_blocks, fq_blocks, jnp.arange(nb)))
    o = o.transpose(1, 0, 3, 2, 4).reshape(B, S, H * hd)
    return o.astype(q.dtype)

def second_inputs(seed: int = 0) -> dict:
    key = jax.random.key(seed)
    ks = jax.random.split(key, 16)
    f32 = jnp.float32
    L = DEPTH
    x = jax.random.normal(ks[0], (BATCH, SEQ, D_MODEL), f32)
    norm_mix_g = 1.0 + 0.02 * jax.random.normal(ks[1], (L, D_MODEL), f32)
    w_in = jax.random.normal(ks[2], (L, D_MODEL, IN_WIDTH), f32) * D_MODEL ** -0.5
    b_f = 2.0 + 0.5 * jax.random.normal(ks[3], (L, ATTN_HEADS), f32)
    b_gate = 0.02 * jax.random.normal(ks[4], (L, N_BRANCH * D_MODEL), f32)
    conv_mix_w = jax.random.normal(ks[5], (L, CONV_K, CONV_WIDTH_2), f32) * CONV_K ** -0.5
    w_out_conv = jax.random.normal(ks[6], (L, CONV_WIDTH_2, D_MODEL), f32) * CONV_WIDTH_2 ** -0.5
    w_out_attn = jax.random.normal(ks[7], (L, ATTN_WIDTH, D_MODEL), f32) * ATTN_WIDTH ** -0.5
    w_o = jax.random.normal(ks[8], (L, D_MODEL, D_MODEL), f32) * D_MODEL ** -0.5
    norm_ffn_g = 1.0 + 0.02 * jax.random.normal(ks[9], (L, D_MODEL), f32)
    w_up = jax.random.normal(ks[10], (L, D_MODEL, 2 * FFN_HIDDEN), f32) * D_MODEL ** -0.5
    conv_ffn_w = jax.random.normal(ks[11], (L, FFN_CONV_K, 2 * FFN_HIDDEN), f32) * FFN_CONV_K ** -0.5
    w_down = jax.random.normal(ks[12], (L, FFN_HIDDEN, D_MODEL), f32) * FFN_HIDDEN ** -0.5
    norm_f_g = 1.0 + 0.02 * jax.random.normal(ks[13], (D_MODEL,), f32)
    return {"x": x, "norm_mix_g": norm_mix_g, "w_in": w_in, "b_f": b_f, "b_gate": b_gate,
            "conv_mix_w": conv_mix_w, "w_out_conv": w_out_conv, "w_out_attn": w_out_attn,
            "w_o": w_o, "norm_ffn_g": norm_ffn_g, "w_up": w_up, "conv_ffn_w": conv_ffn_w,
            "w_down": w_down, "norm_f_g": norm_f_g}

def second_block(x, norm_mix_g, w_in, b_f, b_gate, conv_mix_w, w_out_conv, w_out_attn,
              w_o, norm_ffn_g, w_up, conv_ffn_w, w_down, norm_f_g):
    B, S, _ = x.shape
    split_idx = list(np.cumsum(IN_SPLITS)[:-1])
    for l in range(DEPTH):
        h = rms_norm_2(x, norm_mix_g[l])
        proj = h @ w_in[l]
        cb, cc, cin, q, k, v, f_logit, g_logit = jnp.split(proj, split_idx, axis=-1)
        u = causal_dwconv(cc * cin, conv_mix_w[l])
        y_conv = (cb * u) @ w_out_conv[l]
        log_f = jax.nn.log_sigmoid((f_logit + b_f[l]).astype(jnp.float32))
        o = forgetting_attention(q.reshape(B, S, ATTN_HEADS, HEAD_DIM),
                                 k.reshape(B, S, ATTN_HEADS, HEAD_DIM),
                                 v.reshape(B, S, ATTN_HEADS, HEAD_DIM), log_f)
        y_attn = o @ w_out_attn[l]
        gates = jax.nn.sigmoid(g_logit + b_gate[l])
        g_conv, g_attn = jnp.split(gates, 2, axis=-1)
        x = x + (g_conv * y_conv + g_attn * y_attn) @ w_o[l]
        h = rms_norm_2(x, norm_ffn_g[l])
        up = causal_dwconv(h @ w_up[l], conv_ffn_w[l])
        a, b = jnp.split(up, 2, axis=-1)
        x = x + (jax.nn.silu(a) * b) @ w_down[l]
    return rms_norm_2(x, norm_f_g)


def setup_inputs(seed=0):
    out = dict(first_inputs(seed))
    for name, value in second_inputs(seed + 1).items():
        if name != "x":
            out[name + "_2"] = value
    return out


def reference(
    x, p, rel_bias, attn_norm_g, w_in, b_gate, q_norm_g, k_norm_g, w_att_out, conv_w, conv_b,
    conv_ln_g, conv_ln_b, w_conv_out, w_out, ffn_norm_g, w_peer_q, peer_sub_keys, peer_u,
    peer_v, ple_norm_g, w_ple_gate, w_ple_proj, norm_mix_g_2, w_in_2, b_f_2, b_gate_2,
    conv_mix_w_2, w_out_conv_2, w_out_attn_2, w_o_2, norm_ffn_g_2, w_up_2, conv_ffn_w_2,
    w_down_2, norm_f_g_2,
):
    x = first_block(
        x, p, rel_bias, attn_norm_g, w_in, b_gate, q_norm_g, k_norm_g, w_att_out, conv_w,
        conv_b, conv_ln_g, conv_ln_b, w_conv_out, w_out, ffn_norm_g, w_peer_q, peer_sub_keys,
        peer_u, peer_v, ple_norm_g, w_ple_gate, w_ple_proj,
    )
    return second_block(
        x, norm_mix_g_2, w_in_2, b_f_2, b_gate_2, conv_mix_w_2, w_out_conv_2, w_out_attn_2,
        w_o_2, norm_ffn_g_2, w_up_2, conv_ffn_w_2, w_down_2, norm_f_g_2,
    )


_drawn_inputs = setup_inputs


def setup_inputs(seed=0):
    import zlib

    import numpy as np

    out = dict(_drawn_inputs(seed))
    spreads = {}
    factors = {'rel_bias': 3.009,
     'b_gate': 5.193,
     'q_norm_g': 3.77,
     'k_norm_g': 3.953,
     'conv_ln_b': 3.051,
     'ple_norm_g': 5.215,
     'norm_mix_g_2': 3.365,
     'b_gate_2': 8.0,
     'norm_ffn_g_2': 16.644,
     'norm_f_g_2': 7.76,
     'b_f_2': 3.771}
    for name, (base, spread) in spreads.items():
        noise = np.random.default_rng([zlib.crc32(name.encode()), seed]).standard_normal(out[name].shape)
        drawn = base * np.exp(spread * noise) if base else spread * noise
        out[name] = __import__('jax').numpy.asarray(drawn.astype(out[name].dtype))
    for name, factor in factors.items():
        out[name] = (out[name] * factor).astype(out[name].dtype)
    return out
```

```python
import numpy as np
import concourse.bass as bass
from concourse import mybir
from contextlib import ExitStack

P = 128
S, D = 512, 1024
TB = S // P
KT = D // P
H, HD = 8, 64
TOPK = 128
CT = 4
TAPS = 31
PH, PK = 8, 16
NSEL = PH * PK
FT = 22
EPS = 1e-6
MASKED = -1.0e30
TAKEN = -3.0e38
REL = 640

STREAM = [("qi", 4), ("q", 4), ("k", 4), ("v", 4), ("gates", 16), ("glu", 8), ("mix", 8), ("w_out", 8),
          ("peer_q", 16), ("ple_gate", 8),
          ("cc", 4), ("cin", 4), ("cb", 4), ("q2", 4), ("k2", 4), ("v2", 4), ("gates2", 16), ("mix2", 8),
          ("w_o", 8), ("up", 2 * FT), ("down", FT)]
FIRST = {}
NPANEL = 0
for _name, _n in STREAM:
    FIRST[_name] = NPANEL
    NPANEL += _n
RING = 4

VEC = [("attn_g", 8), ("b_gate", 16), ("q_g", 1), ("k_g", 1), ("conv_w", CT * TAPS), ("conv_b", CT), ("ln_g", CT),
       ("ln_b", CT), ("ffn_g", 8), ("ple_g", 8), ("mix_g2", 8), ("b_gate2", 16), ("conv_mix_w", CT * 3),
       ("ffn_g2", 8), ("conv_ffn_w", 2 * FT * 3), ("norm_f_g", 8), ("b_f", 8 * TB)]
VCOL = {}
NVEC = 0
for _name, _n in VEC:
    VCOL[_name] = NVEC
    NVEC += _n


def build(nc, xT_d, pT_d, panels_d, vecs_d, wki_d, wwi_d, wf_d, wpp_d, subk_d, relb_d, onehot_d, u_d, v_d, out_d):
    f32 = mybir.dt.float32
    u32 = mybir.dt.uint32
    ALU = mybir.AluOpType
    ACT = mybir.ActivationFunctionType
    AX = mybir.AxisListType
    ds = bass.ds

    ctx = ExitStack()
    with ctx:
        def sem(name):
            return ctx.enter_context(nc.semaphore(name))

        def sb(name, shape, dt=f32, stack=ctx):
            return stack.enter_context(nc.sbuf_tensor(name, shape, dt))

        bank = [ctx.enter_context(nc.psum_tensor(f"bank{i}", [P, 512], f32)) for i in range(8)]
        rel_tab_d = nc.dram_tensor("rel_tab", (H, REL), f32)

        xT = sb("xT", [P, KT, S])
        hT = sb("hT", [P, KT, S])
        ring = sb("ring", [P, RING, D])
        vec = sb("vec", [P, NVEC])
        ident = sb("ident", [P, P])
        mean_d = sb("mean_d", [P, P])
        mean_h = sb("mean_h", [P, P])
        mean_c = sb("mean_c", [P, P])
        epsc = sb("epsc", [P, 1])
        sq = sb("sq", [P, 2, S])
        rt = sb("rt", [P, 2, S])
        rs = sb("rs", [P, S])

        att = ExitStack()
        gates = sb("gates", [P, 16, S], stack=att)
        vtok = sb("vtok", [P, TB, 512], stack=att)
        oT = sb("oT", [P, CT, S], stack=att)
        lg = sb("lg", [P, 2, S], stack=att)
        ex = sb("ex", [P, 2, S], stack=att)
        pT = sb("pT", [P, 2, S], stack=att)
        nmax = sb("nmax", [P, 4], stack=att)
        esum = sb("esum", [P, 4], stack=att)
        rsum = sb("rsum", [P, 4], stack=att)
        ybr = sb("ybr", [P, CT, S], stack=att)

        one = ExitStack()
        qkiT = sb("qkiT", [P, 12, S], stack=one)
        kiT = sb("kiT", [P, S], stack=one)
        wi = sb("wi", [P, TB * H], stack=one)
        bias = sb("bias", [P, H, S], stack=one)
        MOFF = [0, 128, 384, 768]
        mask = sb("mask", [P, 1280], stack=one)
        upad = sb("upad", [P, CT, TAPS - 1 + S], stack=one)
        score = sb("score", [P, S], stack=one)
        top8 = sb("top8", [P, 8], stack=one)
        onehot = rt[0:32, :, :].rearrange("p a b -> p (a b)")
        reltab = sq[0:8, :, :].rearrange("p a b -> p (a b)")
        relb = sb("relb", [32, H], stack=one)
        wwi = sb("wwi", [P, KT * H], stack=one)
        wki2 = bias[:, 0:2, :].rearrange("p a (k n) -> p (a k) n", n=P)
        one.close()

        two = ExitStack()
        qk2T = sb("qk2T", [P, 8, S], stack=two)
        zpad = sb("zpad", [P, CT, S + 2], stack=two)
        ccT = sb("ccT", [P, CT, S], stack=two)
        wf = sb("wf", [P, KT * H], stack=two)
        tri = sb("tri", [P, TB, S], stack=two)
        nfk = sb("nfk", [P, H, S], stack=two)
        fq = sb("fq", [P, TB * H], stack=two)
        fT = sb("fT", [H, S], stack=two)
        negsel = sb("negsel", [H, H, P], stack=two)
        causal = sb("causal", [P, P], stack=two)
        z = sb("z", [P, 4, TB * H], stack=two)
        two.close()
        att.close()

        pe_ = ExitStack()
        h2tok = sb("h2tok", [P, TB, D], stack=pe_)
        qpT = sb("qpT", [P, 16, S], stack=pe_)
        subk = sb("subk", [P, 16, P], stack=pe_)
        NG = 8
        grows = sb("grows", [P, NG, D], stack=pe_)
        acc = sb("acc", [P, D], stack=pe_)
        sc = sb("sc", [P, 2, 16 * P // 2], stack=pe_)
        sc2 = sb("sc2", [P, P], stack=pe_)
        sv = sb("sv", [P, 16, PK], stack=pe_)
        si = sb("si", [P, 16, PK], u32, stack=pe_)
        sif = sb("sif", [P, 16, PK], stack=pe_)
        cand = sb("cand", [P, PH, PK * PK], stack=pe_)
        cand2 = sb("cand2", [P, PK * PK], stack=pe_)
        tops = sb("tops", [P, PH, PK], stack=pe_)
        topj = sb("topj", [P, PH, PK], u32, stack=pe_)
        tja = sb("tja", [P, 2, PH * PK], u32, stack=pe_)
        tjf = sb("tjf", [P, 2, PH * PK], stack=pe_)
        iota16 = sb("iota16", [P, PK], stack=pe_)
        eqv = sb("eqv", [P, PH, PK * PK], stack=pe_)
        eij = sb("eij", [P, 2, PH * PK], stack=pe_)
        gsum = sb("gsum", [P, 2, PH], stack=pe_)
        gate = sb("gate", [P, 2, NSEL], stack=pe_)
        eidx = sb("eidx", [P, 2, NSEL], u32, stack=pe_)
        idxs = sb("idxs", [P, 2, 8], u32, stack=pe_)
        dots8 = sb("dots8", [P, 2, 8], stack=pe_)
        dots = sb("dots", [P, NSEL], stack=pe_)
        gel = sb("gel", [P, NSEL], stack=pe_)
        act = sb("act", [P, NSEL], stack=pe_)
        act8 = sb("act8", [P, 2, 8], stack=pe_)
        pe_.close()

        ple = ExitStack()
        pT_in = sb("pT_in", [P, 2, S], stack=ple)
        wpp = sb("wpp", [P, 2, D], stack=ple)
        sg = sb("sg", [P, 2, S], stack=ple)
        ple.close()

        ffn = ExitStack()
        actT = sb("actT", [P, FT, S], stack=ffn)
        uppad = sb("uppad", [P, 4, S + 2], stack=ffn)
        upc = sb("upc", [P, 4, S], stack=ffn)
        ffn.close()

        panel_in = [sem(f"panel_in{s}") for s in range(RING)]
        panel_done = sem("panel_done")
        out_free = sem("out_free")
        x_in = sem("x_in")
        vec_in = sem("vec_in")
        small_in = sem("small_in")
        const_ready = sem("const_ready")
        sq_ready, sq_used = sem("sq_ready"), sem("sq_used")
        rt_ready = sem("rt_ready")
        rt_used = sem("rt_used")
        h_ready = sem("h_ready")
        x_ready = sem("x_ready")
        ki_ready, ki_copied = sem("ki_ready"), sem("ki_copied")
        dot_ready, relu_ready, relu_used = sem("dot_ready"), sem("relu_ready"), sem("relu_used")
        qk_ready = sem("qk_ready")
        rel_ready, rel_copied, rel_out, rel_in = sem("rel_ready"), sem("rel_copied"), sem("rel_out"), sem("rel_in")
        lg_ready, lg_done, ex_ready = sem("lg_ready"), sem("lg_done"), sem("ex_ready")
        rsum_ready, prob_ready = sem("rsum_ready"), sem("prob_ready")
        tr_ready, pT_ready, pv_ready, pv_used = sem("tr_ready"), sem("pT_ready"), sem("pv_ready"), sem("pv_used")
        u_sig, br_ready, mixed_ready = sem("u_sig"), sem("br_ready"), sem("mixed_ready")
        cv = sem("cv")
        cm_ready, cx_ready, csq_ready, cvar_ready, csd_ready, cn_ready = (sem(n) for n in (
            "cm_ready", "cx_ready", "csq_ready", "cvar_ready", "csd_ready", "cn_ready"))
        htok_tr, htok_ready = sem("htok_tr"), sem("htok_ready")
        sc_mm, sc_ready, sc_used = sem("sc_mm"), sem("sc_ready"), sem("sc_used")
        g_shift, g_exp, idx_ready = sem("g_shift"), sem("g_exp"), sem("idx_ready")
        idx_staged, idx_seen = sem("idx_staged"), sem("idx_seen")
        gathered = [sem(f"gathered{s}") for s in range(NG)]
        row_used = sem("row_used")
        dots_ready, gel_ready = sem("dots_ready"), sem("gel_ready")
        acc_ready, acc_tr, acc_used = sem("acc_ready"), sem("acc_tr"), sem("acc_used")
        peer_in, ple_in = sem("peer_in"), sem("ple_in")
        sg_ready, sg_used = sem("sg_ready"), sem("sg_used")
        pp_ready = sem("pp_ready")
        cc_ready = sem("cc_ready")
        f_ready, z_ready, sp_ready, logf_ready = sem("f_ready"), sem("z_ready"), sem("sp_ready"), sem("logf_ready")
        fT_mm, fT_ready, nfk_mm, nfk_ready = sem("fT_mm"), sem("fT_ready"), sem("nfk_mm"), sem("nfk_ready")
        two_const, two_in = sem("two_const"), sem("two_in")
        up_copied, up_conv, up_silu, up_used = sem("up_copied"), sem("up_conv"), sem("up_silu"), sem("up_used")
        act_ready = sem("act_ready")
        out_done, y_ready = sem("out_done"), sem("y_ready")
        dve_step, act_step, pool_step = sem("dve_step"), sem("act_step"), sem("pool_step")
        peer_free, ple_free = sem("peer_free"), sem("ple_free")
        qkv_done = sem("qkv_done")
        pads_ready = sem("pads_ready")

        class Steps:

            def __init__(self, eng, s):
                self.eng, self.sem, self.n = eng, s, 0

            def __call__(self, ins):
                ins.then_inc(self.sem, 1)
                self.n = self.n + 1
                self.eng.wait_ge(self.sem, self.n)

        def V(name, i=0, n=1):
            return vec[:, ds(VCOL[name] + i, n)] if not isinstance(i, int) else vec[:, VCOL[name] + i:VCOL[name] + i + n]

        NORMS = ["attn_g", "ffn_g", "ple_g", "mix_g2", "ffn_g2", "norm_f_g"]
        UNITS = [(qb, h) for qb in range(TB) for h in range(H)]

        block = ctx.enter_context(nc.Block())

        @block.sync
        def _(sp):
            sp.dma_start(xT[:, 0:4, :], xT_d[:, 0:4, :]).then_inc(x_in, 16)
            sp.dma_start(xT[:, 4:8, :], xT_d[:, 4:8, :]).then_inc(x_in, 16)
            for s in range(RING):
                sp.dma_start(ring[:, s, :], panels_d[s, :, :]).then_inc(panel_in[s], 16)
            full = NPANEL // RING * RING
            with sp.Fori(1, NPANEL // RING) as i:
                for s in range(RING):
                    sp.wait_ge(panel_done, i * RING + (s + 1 - RING))
                    sp.dma_start(ring[:, s, :], panels_d[ds(i * RING + s, 1), :, :].rearrange("a p n -> (a p) n"))\
                      .then_inc(panel_in[s], 16)
            for n in range(full, NPANEL):
                sp.wait_ge(panel_done, n + 1 - RING)
                sp.dma_start(ring[:, n % RING, :], panels_d[n, :, :]).then_inc(panel_in[n % RING], 16)
            sp.wait_ge(y_ready, 1)
            sp.dma_start(out_d[:, :, :], hT[:, :, :]).then_inc(out_done, 16)
            sp.wait_ge(out_done, 16)

        @block.gpsimd
        def _(pool):
            step = Steps(pool, pool_step)
            g = nc.gpsimd
            g.memset(epsc[:, :], EPS)
            g.memset(mean_d[:, :], 1.0 / D)
            g.memset(mean_c[:, :], 1.0 / 512)
            g.memset(mean_h[:, :], 0.0)
            g.memset(upad[:, :, 0:TAPS - 1], 0.0)
            step(g.memset(ident[:, :], 0.0))
            step(g.memset(mean_h[0:64, 0:64], 1.0 / HD))
            step(g.memset(mean_h[64:128, 64:128], 1.0 / HD))
            g.memset(mask[:, 0:P], 0.0)
            step(g.affine_select(out=ident[:, :], in_=ident[:, :], compare_op=ALU.not_equal, fill=1.0, base=0,
                                 pattern=[[-1, P]], channel_multiplier=1))
            g.memset(mask[0:64, 64:P], MASKED).then_inc(const_ready, 1)

            def probs(first):
                for i in range(len(UNITS)):
                    qb, h = UNITS[i]
                    n = P * (qb + 1)
                    pool.wait_ge(rsum_ready, first + i + 1)
                    g.tensor_scalar(ex[:, i % 2, 0:n], ex[:, i % 2, 0:n], rsum[:, i % 4:i % 4 + 1], None, ALU.mult)\
                     .then_inc(prob_ready, 1)

            probs(0)

            pool.wait_ge(x_ready, 1)
            step(g.iota(iota16[:, :], pattern=[[1, PK]], base=0, channel_multiplier=0,
                        allow_small_or_imprecise_dtypes=True))
            g.memset(sc2[:, 0:1], 0.0).then_inc(peer_free, 1)
            ROUNDS = NSEL // 16
            for tb in range(TB):
                pool.wait_ge(idx_ready, tb + 1)
                for which, table in ((0, u_d), (1, v_d)):
                    turn = (2 * tb + which) * ROUNDS

                    def gather(i, first):
                        for half in range(2):
                            if not (first and half == 0):
                                pool.wait_ge(row_used, i * 16 + (turn * 16 + 8 * half))
                            g.tensor_copy(idxs[:, half, :], eidx[:, tb % 2, ds(i * 16 + 8 * half, 8)])\
                             .then_inc(idx_staged, 1)
                            pool.wait_ge(idx_staged, i * 2 + (2 * turn + half + 1))
                            pool.sem_inc(idx_seen, 1)
                            for u in range(8):
                                g.indirect_dma_start(
                                    out=grows[:, u, :], out_offset=None, in_=table[:, :],
                                    in_offset=bass.IndirectOffsetOnAxis(ap=idxs[:, half, u:u + 1], axis=0),
                                ).then_inc(gathered[u], 16)

                    gather(0, turn == 0)
                    with pool.Fori(1, ROUNDS) as i:
                        gather(i, False)

            pool.wait_ge(x_ready, 3)
            g.memset(tri[:, :, :], 1.0)
            g.memset(causal[:, :], 0.0)
            g.memset(zpad[:, :, 0:2], 0.0)
            step(g.memset(negsel[:, :, :], 0.0))
            g.affine_select(out=tri[:, :, :], in_=tri[:, :, :], compare_op=ALU.is_ge, fill=0.0, base=0,
                            pattern=[[-P, TB], [1, S]], channel_multiplier=-1)
            g.affine_select(out=causal[:, :], in_=causal[:, :], compare_op=ALU.is_ge, fill=MASKED, base=0,
                            pattern=[[-1, P]], channel_multiplier=1)
            g.affine_select(out=negsel[:, :, :], in_=negsel[:, :, :], compare_op=ALU.not_equal, fill=-1.0, base=0,
                            pattern=[[-1, H], [0, P]], channel_multiplier=1).then_inc(two_const, 1)
            probs(len(UNITS))
            pool.wait_ge(x_ready, 4)
            g.memset(uppad[:, :, 0:2], 0.0).then_inc(pads_ready, 1)

        @block.scalar
        def _(act_e):
            step = Steps(act_e, act_step)
            a = nc.scalar
            a.dma_start(vec[:, :], vecs_d).then_inc(vec_in, 16)
            wki_src = wki_d.rearrange("p (k n) -> p k n", k=KT)
            a.dma_start(wki2[:, :, 0:64], wki_src).then_inc(small_in, 16)
            a.dma_start(wki2[:, :, 64:P], wki_src).then_inc(small_in, 16)
            a.dma_start(wwi[:, :], wwi_d).then_inc(small_in, 16)
            a.dma_start(relb[:, :], relb_d).then_inc(small_in, 16)
            a.dma_start(onehot[:, 0:REL], onehot_d).then_inc(small_in, 16)
            nsq = [0]
            nms = [0]
            due = [8] + [8 + c + 1 for c in range(8)] + [16 + 8 * (k + 1) for k in range(5)]
            npan = [0]

            def square(src):
                if nsq[0] >= 2:
                    act_e.wait_ge(sq_used, nsq[0] - 1)
                a.activation(sq[:, nsq[0] % 2, :], src, ACT.Square).then_inc(sq_ready, 1)
                nsq[0] += 1

            def root(ps):
                act_e.wait_ge(sq_used, due[nms[0]])
                if nms[0] >= 2:
                    act_e.wait_ge(rt_used, nms[0] - 1)
                a.activation(rt[:, nms[0] % 2, :], ps, ACT.Sqrt, bias=epsc[:, :]).then_inc(rt_ready, 1)
                nms[0] += 1

            def norm(k):
                act_e.wait_ge(x_ready, k) if k else act_e.wait_ge(x_in, 32)
                for c in range(KT):
                    square(xT[:, c, :])
                root(bank[4][:, :])

            def evac_loop(n_panels, emit):
                n0 = npan[0]
                if n0:
                    act_e.wait_ge(out_free, n0)
                with act_e.Fori(0, n_panels // RING) as i:
                    for s in range(RING):
                        act_e.wait_ge(panel_done, i * RING + (n0 + s + 1))
                        emit(i, s).then_inc(out_free, 1)
                npan[0] += n_panels

            act_e.wait_ge(const_ready, 1)
            act_e.wait_ge(vec_in, 16)
            act_e.wait_ge(rel_ready, 1)
            a.activation(reltab[:, 0:320], bank[6][0:8, 0:320], ACT.Copy)
            a.activation(reltab[:, 320:REL], bank[7][0:8, 0:320], ACT.Copy).then_inc(rel_copied, 1)
            act_e.wait_ge(rel_copied, 1)
            a.dma_start(rel_tab_d.ap(), reltab[:, 0:REL]).then_inc(rel_out, 16)
            act_e.wait_ge(rel_out, 16)
            norm(0)
            evac_loop(4, lambda i, s: a.activation(qkiT[:, ds(i * RING + s, 1), :], bank[s][:, :], ACT.Copy))
            act_e.wait_ge(ki_ready, 1)
            a.activation(kiT[:, :], bank[4][:, :], ACT.Copy).then_inc(ki_copied, 1)
            act_e.wait_ge(ki_ready, 2)
            a.mul(wi[:, :], bank[5][:, 0:TB * H], float(np.float32(HD ** -0.5 * H ** -0.5))).then_inc(ki_copied, 1)
            rel_ap = rel_tab_d.ap()
            diag = bass.AP(tensor=rel_ap.tensor, offset=1, ap=[[1, P], [REL, H], [1, S]])
            a.dma_start(bias[:, :, :], diag).then_inc(rel_in, 16)
            for j in range(3 * H):
                n = P * (j // H + 2)
                act_e.wait_ge(dot_ready, j + 1)
                if j >= 2:
                    act_e.wait_ge(relu_used, j - 1)
                a.activation(lg[:, j % 2, 0:n], bank[4 + j % 2][:, 0:n], ACT.Relu).then_inc(relu_ready, 1)
            evac_loop(8, lambda i, s: a.activation(qkiT[:, ds(i * RING + (s + 4), 1), :], bank[s][:, :], ACT.Copy))
            act_e.wait_ge(panel_done, npan[0] + 4)
            for tb in range(TB):
                a.activation(vtok[:, tb, :], bank[tb][:, :], ACT.Copy).then_inc(out_free, 1)
            npan[0] += 4

            def gate_loop(bname):
                evac_loop(16, lambda i, s: a.activation(gates[:, ds(i * RING + s, 1), :], bank[s][:, :], ACT.Sigmoid,
                                                        bias=V(bname, i * RING + s)))

            gate_loop("b_gate")
            for c in range(8):
                square(qkiT[:, 4 + c, :])
                if c >= 1:
                    root(bank[4 + (c - 1) % 2][:, :])
            root(bank[5][:, :])
            for c in range(CT):
                act_e.wait_ge(panel_done, npan[0] + 2)
                if c >= 2:
                    act_e.wait_ge(out_free, npan[0] - 2)
                a.activation(lg[:, c % 2, :], bank[(2 * c + 1) % 4][:, :], ACT.Sigmoid).then_inc(u_sig, 1)
                npan[0] += 2

            def attend(first):
                for i in range(len(UNITS) + 1):
                    if i < len(UNITS):
                        n = P * (UNITS[i][0] + 1)
                        act_e.wait_ge(lg_done, first + i + 1)
                        if i >= 2:
                            act_e.wait_ge(tr_ready, first + i - 1)
                        a.activation(ex[:, i % 2, 0:n], lg[:, i % 2, 0:n], ACT.Exp, bias=nmax[:, i % 4:i % 4 + 1],
                                     accum_out=esum[:, i % 4:i % 4 + 1]).then_inc(ex_ready, 1)
                    if i >= 1:
                        j = i - 1
                        n = P * (UNITS[j][0] + 1)
                        act_e.wait_ge(tr_ready, first + j + 1)
                        if j >= 2:
                            act_e.wait_ge(pv_ready, first + j - 1)
                        a.activation(pT[:, j % 2, 0:n], bank[6 + j % 2][:, 0:n], ACT.Copy).then_inc(pT_ready, 1)

            attend(0)
            act_e.wait_ge(sq_used, nsq[0])
            for c in range(CT):
                act_e.wait_ge(cx_ready, c + 1)
                if c >= 2:
                    act_e.wait_ge(cvar_ready, c - 1)
                a.activation(sq[:, c % 2, :], ybr[:, c, :], ACT.Square).then_inc(csq_ready, 1)
            act_e.wait_ge(cvar_ready, CT)
            act_e.wait_ge(rt_used, nms[0])
            a.activation(rt[:, 0, :], bank[5][:, :], ACT.Sqrt, bias=epsc[:, :]).then_inc(csd_ready, 1)
            for c in range(CT):
                act_e.wait_ge(cn_ready, c + 1)
                a.activation(ybr[:, c, :], ybr[:, c, :], ACT.Silu, bias=V("ln_b", c), scale=V("ln_g", c))\
                 .then_inc(br_ready, 1)
            npan[0] += 8 + 8
            norm(1)
            act_e.wait_ge(peer_free, 1)
            a.dma_start(subk[:, :, :], subk_d).then_inc(peer_in, 16)
            for j in range(TB * 2):
                act_e.wait_ge(htok_tr, j + 1)
                a.activation(h2tok[:, j // 2, (j % 2) * 512:(j % 2) * 512 + 512], bank[6 + j % 2][:, :], ACT.Copy)\
                 .then_inc(htok_ready, 1)
            evac_loop(16, lambda i, s: a.activation(qpT[:, ds(i * RING + s, 1), :], bank[s][:, :], ACT.Copy))

            def score_copies(tb):
                for q4 in range(4):
                    act_e.wait_ge(sc_mm, tb * 4 + q4 + 1)
                    if tb >= 1 and q4 % 2 == 0:
                        act_e.wait_ge(sc_used, 2 * (tb - 1) + q4 // 2 + 1)
                    a.activation(sc[:, q4 // 2, (q4 % 2) * 512:(q4 % 2) * 512 + 512], bank[4 + q4 % 2][:, :], ACT.Copy)\
                     .then_inc(sc_ready, 1)

            def gate_exp(tb):
                act_e.wait_ge(g_shift, tb + 1)
                a.activation(gate[:, tb % 2, :], gate[:, tb % 2, :], ACT.Exp).then_inc(g_exp, 1)

            score_copies(0)
            gate_exp(0)
            for tb in range(TB):
                if tb + 1 < TB:
                    score_copies(tb + 1)
                act_e.wait_ge(dots_ready, tb + 1)
                a.activation(gel[:, :], dots[:, :], ACT.Gelu_apprx_tanh).then_inc(gel_ready, 1)
                if tb + 1 < TB:
                    gate_exp(tb + 1)
            act_e.wait_ge(x_ready, 2)
            a.dma_start(pT_in[:, :, :], pT_d).then_inc(ple_in, 16)
            a.dma_start(wpp[:, :, :], wpp_d).then_inc(ple_in, 16)
            for c in range(KT):
                square(xT[:, c, :])
            root(bank[4][:, :])
            for c in range(KT):
                act_e.wait_ge(panel_done, npan[0] + 1)
                if c >= 2:
                    act_e.wait_ge(sg_used, c - 1)
                a.activation(sg[:, c % 2, :], bank[2 * (c % 2)][:, :], ACT.Sigmoid).then_inc(sg_ready, 1)
                npan[0] += 1

            act_e.wait_ge(x_ready, 3)
            a.dma_start(wf[:, :], wf_d).then_inc(two_in, 16)
            for c in range(KT):
                square(xT[:, c, :])
            root(bank[4][:, :])
            evac_loop(4, lambda i, s: a.activation(ccT[:, ds(i * RING + s, 1), :], bank[s][:, :], ACT.Copy))
            npan[0] += 8
            evac_loop(4, lambda i, s: a.activation(qk2T[:, ds(i * RING + s, 1), :], bank[s][:, :], ACT.Copy,
                                                   scale=HD ** -0.5))
            evac_loop(4, lambda i, s: a.activation(qk2T[:, ds(i * RING + (s + 4), 1), :], bank[s][:, :], ACT.Copy))
            act_e.wait_ge(panel_done, npan[0] + 4)
            for tb in range(TB):
                a.activation(vtok[:, tb, :], bank[tb][:, :], ACT.Copy).then_inc(out_free, 1)
            npan[0] += 4
            act_e.wait_ge(z_ready, 1)
            step(a.activation(z[:, 1, :], z[:, 0, :], ACT.Abs))
            step(a.activation(z[:, 1, :], z[:, 1, :], ACT.Exp, scale=-1.0))
            a.activation(z[:, 1, :], z[:, 1, :], ACT.Ln, bias=1.0).then_inc(sp_ready, 1)
            act_e.wait_ge(fT_mm, 1)
            a.activation(fT[:, :], bank[5][0:H, :], ACT.Copy).then_inc(fT_ready, 1)
            for h in range(H):
                act_e.wait_ge(nfk_mm, h + 1)
                a.activation(nfk[:, h, :], bank[6 + h % 2][:, :], ACT.Copy).then_inc(nfk_ready, 1)
            gate_loop("b_gate2")
            attend(len(UNITS))
            npan[0] += 8 + 8
            act_e.wait_ge(x_ready, 4)
            for c in range(KT):
                square(xT[:, c, :])
            root(bank[4][:, :])
            act_e.wait_ge(pads_ready, 1)
            n0 = npan[0]
            act_e.wait_ge(out_free, n0)

            def up_step(i, first):
                for s in range(RING):
                    act_e.wait_ge(panel_done, i * RING + (n0 + s + 1))
                    if not first:
                        act_e.wait_ge(up_conv, i * RING + (s + 1 - RING))
                    a.activation(uppad[:, s, 2:S + 2], bank[s][:, :], ACT.Copy).then_inc(out_free, 1)
                for s in (0, 2):
                    act_e.wait_ge(up_conv, i * RING + (s + 1))
                    a.activation(upc[:, s, :], upc[:, s, :], ACT.Silu).then_inc(up_silu, 1)

            up_step(0, True)
            with act_e.Fori(1, 2 * FT // RING) as i:
                up_step(i, False)
            act_e.wait_ge(x_ready, 5)
            for c in range(KT):
                square(xT[:, c, :])
            root(bank[4][:, :])

        @block.tensor
        def _(pe):
            mm = nc.tensor.matmul
            npan = [0]
            nsq = [0]

            def sum_square(bk, weights, first, last):
                pe.wait_ge(sq_ready, nsq[0] + 1)
                mm(bk, weights[:, :], sq[:, nsq[0] % 2, :], start=first, stop=last).then_inc(sq_used, 1)
                nsq[0] += 1

            def norm():
                for c in range(KT):
                    sum_square(bank[4][:, :], mean_d, c == 0, c == KT - 1)

            def gemm_loop(n_panels, src):
                n0 = npan[0]

                def body(i):
                    for s in range(RING):
                        if n0:
                            pe.wait_ge(out_free, i * RING + (n0 + s + 1 - RING))
                        pe.wait_ge(panel_in[s], i * 16 + 16 * (n0 // RING + 1))
                        for kt in range(KT):
                            last = mm(bank[s][:, :], ring[:, s, kt * P:(kt + 1) * P], src[:, kt, :],
                                      start=(kt == 0), stop=(kt == KT - 1))
                        last.then_inc(panel_done, 1)

                if n_panels == RING:
                    body(0)
                else:
                    with pe.Fori(0, n_panels // RING) as i:
                        body(i)
                npan[0] += n_panels

            def values():
                n0 = npan[0]
                pe.wait_ge(out_free, n0)
                for s in range(RING):
                    pe.wait_ge(panel_in[s], 16 * (n0 // RING + 1))
                    for half in range(2):
                        kt = 2 * s + half
                        for tb in range(TB):
                            last = mm(bank[tb][:, :], hT[:, kt, tb * P:(tb + 1) * P],
                                      ring[:, s, half * 512:(half + 1) * 512], start=(kt == 0), stop=(kt == KT - 1),
                                      skip_group_check=True)
                    last.then_inc(panel_done, 1)
                npan[0] += 4

            def mix(a_src, b_src):
                n0 = npan[0]
                for n in range(8):
                    s = n % RING
                    pe.wait_ge(out_free, n0 if n < 2 else n0 + n - 1)
                    pe.wait_ge(panel_in[s], 16 * ((n0 + n) // RING + 1))
                    for kt in range(KT):
                        src = a_src if kt < CT else b_src
                        last = mm(bank[2 * (n % 2) + kt // CT][:, :], ring[:, s, kt * P:(kt + 1) * P],
                                  src[:, kt % CT, :], start=(kt % CT == 0), stop=(kt % CT == CT - 1))
                    last.then_inc(panel_done, 1)
                npan[0] += 8

            def attend(qT, q0, k0, first):
                m = len(UNITS)
                for i in range(m + 2):
                    if i < m:
                        qb, h = UNITS[i]
                        n, r = P * (qb + 1), 64 * (h % 2)
                        if first + i >= 2:
                            pe.wait_ge(lg_done, first + i - 1)
                        mm(bank[4 + i % 2][:, 0:n], qT[r:r + 64, q0 + h // 2, qb * P:(qb + 1) * P],
                           qT[r:r + 64, k0 + h // 2, 0:n], start=True, stop=True).then_inc(lg_ready, 1)
                    if 1 <= i <= m:
                        j = i - 1
                        qb, h = UNITS[j]
                        pe.wait_ge(prob_ready, first + j + 1)
                        if first + j >= 2:
                            pe.wait_ge(pT_ready, first + j - 1)
                        for c in range(qb + 1):
                            last = nc.tensor.transpose(bank[6 + j % 2][:, c * P:(c + 1) * P],
                                                       ex[:, j % 2, c * P:(c + 1) * P], ident[:, :])
                        last.then_inc(tr_ready, 1)
                    if i >= 2:
                        j = i - 2
                        qb, h = UNITS[j]
                        pe.wait_ge(pT_ready, first + j + 1)
                        if first + j >= 2:
                            pe.wait_ge(pv_used, first + j - 1)
                        for c in range(qb + 1):
                            last = mm(bank[j % 2][:, 0:P], vtok[:, c, (h // 2) * P:(h // 2 + 1) * P],
                                      pT[:, j % 2, c * P:(c + 1) * P], start=(c == 0), stop=(c == qb))
                        last.then_inc(pv_ready, 1)

            pe.wait_ge(small_in, 80)
            for j in range(2):
                last = mm(bank[6 + j][0:H, 0:320], relb[:, :], onehot[:, j * 320:(j + 1) * 320], start=True, stop=True)
            last.then_inc(rel_ready, 1)
            pe.wait_ge(const_ready, 1)
            norm()
            pe.wait_ge(h_ready, 1)
            gemm_loop(4, hT)
            for kt in range(KT):
                last = mm(bank[4][:, :], wki2[:, kt, :], hT[:, kt, :], start=(kt == 0), stop=(kt == KT - 1))
            last.then_inc(ki_ready, 1)
            for tb in range(TB):
                for kt in range(KT):
                    last = mm(bank[5][:, tb * H:(tb + 1) * H], hT[:, kt, tb * P:(tb + 1) * P],
                              wwi[:, kt * H:(kt + 1) * H], start=(kt == 0), stop=(kt == KT - 1))
            last.then_inc(ki_ready, 1)
            pe.wait_ge(ki_copied, 2)
            pe.wait_ge(out_free, 4)
            for j in range(3 * H):
                qb, h = j // H + 1, j % H
                r = 64 * (h % 2)
                if j >= 2:
                    pe.wait_ge(relu_ready, j - 1)
                mm(bank[4 + j % 2][:, 0:P * (qb + 1)], qkiT[r:r + 64, h // 2, qb * P:(qb + 1) * P],
                   kiT[r:r + 64, 0:P * (qb + 1)], start=True, stop=True).then_inc(dot_ready, 1)
            gemm_loop(8, hT)
            values()
            gemm_loop(16, hT)
            pe.wait_ge(relu_ready, 3 * H)
            for c in range(8):
                if c >= 2:
                    pe.wait_ge(rt_ready, c)
                sum_square(bank[4 + c % 2][:, :], mean_h, True, True)
            gemm_loop(8, hT)
            pe.wait_ge(qk_ready, 8)
            pe.wait_ge(out_free, npan[0])
            attend(qkiT, 4, 8, 0)
            pe.wait_ge(cv, CT * TAPS)
            for c in range(CT):
                last = mm(bank[4][:, :], mean_c[:, :], ybr[:, c, :], start=(c == 0), stop=(c == CT - 1))
            last.then_inc(cm_ready, 1)
            for c in range(CT):
                pe.wait_ge(csq_ready, c + 1)
                mm(bank[5][:, :], mean_c[:, :], sq[:, c % 2, :], start=(c == 0), stop=(c == CT - 1)).then_inc(cvar_ready, 1)
            pe.wait_ge(br_ready, CT)
            pe.wait_ge(pv_used, len(UNITS))
            mix(oT, ybr)
            pe.wait_ge(mixed_ready, 1)
            gemm_loop(8, hT)
            norm()
            pe.wait_ge(h_ready, 2)
            for j in range(TB * 2):
                if j >= 2:
                    pe.wait_ge(htok_ready, j - 1)
                for c in range(4):
                    last = nc.tensor.transpose(bank[6 + j % 2][:, c * P:(c + 1) * P],
                                               hT[:, (j % 2) * 4 + c, (j // 2) * P:(j // 2 + 1) * P], ident[:, :])
                last.then_inc(htok_tr, 1)
            gemm_loop(16, hT)
            pe.wait_ge(out_free, npan[0])
            pe.wait_ge(peer_in, 16)

            def key_scores(tb):
                for q4 in range(4):
                    if tb * 4 + q4 >= 2:
                        pe.wait_ge(sc_ready, tb * 4 + q4 - 1)
                    for c in range(4):
                        hc = q4 * 4 + c
                        last = mm(bank[4 + q4 % 2][:, c * P:(c + 1) * P], qpT[:, hc, tb * P:(tb + 1) * P],
                                  subk[:, hc, :], start=True, stop=True)
                    last.then_inc(sc_mm, 1)

            key_scores(0)
            for tb in range(TB):
                if tb + 1 < TB:
                    key_scores(tb + 1)
                for j in range(2):
                    pe.wait_ge(acc_ready, tb + 1)
                    if tb >= 1:
                        pe.wait_ge(acc_used, 2 * (tb - 1) + j + 1)
                    for c in range(4):
                        last = nc.tensor.transpose(bank[6 + j][:, c * P:(c + 1) * P],
                                                   acc[:, (4 * j + c) * P:(4 * j + c + 1) * P], ident[:, :])
                    last.then_inc(acc_tr, 1)
            norm()
            pe.wait_ge(h_ready, 3)
            pe.wait_ge(ple_in, 32)
            n0 = npan[0]
            for n in range(8):
                s = n % RING
                pe.wait_ge(out_free, n0 if n < 2 else n0 + n - 1)
                pe.wait_ge(panel_in[s], 16 * ((n0 + n) // RING + 1))
                for kt in range(2):
                    mm(bank[2 * (n % 2) + 1][:, :], wpp[:, kt, n * P:(n + 1) * P], pT_in[:, kt, :],
                       start=(kt == 0), stop=(kt == 1))
                for kt in range(KT):
                    last = mm(bank[2 * (n % 2)][:, :], ring[:, s, kt * P:(kt + 1) * P], hT[:, kt, :],
                              start=(kt == 0), stop=(kt == KT - 1))
                last.then_inc(panel_done, 1)
            npan[0] += 8
            norm()
            pe.wait_ge(h_ready, 4)
            gemm_loop(12, hT)
            pe.wait_ge(two_in, 16)
            for tb in range(TB):
                for kt in range(KT):
                    last = mm(bank[4][:, tb * H:(tb + 1) * H], hT[:, kt, tb * P:(tb + 1) * P],
                              wf[:, kt * H:(kt + 1) * H], start=(kt == 0), stop=(kt == KT - 1))
            last.then_inc(f_ready, 1)
            gemm_loop(8, hT)
            values()
            pe.wait_ge(logf_ready, 1)
            pe.wait_ge(two_const, 1)
            for tc in range(TB):
                last = mm(bank[5][0:H, :], z[:, 2, tc * H:(tc + 1) * H], tri[:, tc, :], start=(tc == 0), stop=(tc == TB - 1))
            last.then_inc(fT_mm, 1)
            for qb in range(TB):
                for tc in range(TB):
                    last = mm(bank[4][:, qb * H:(qb + 1) * H], tri[:, tc, qb * P:(qb + 1) * P],
                              z[:, 2, tc * H:(tc + 1) * H], start=(tc == 0), stop=(tc == TB - 1))
            last.then_inc(fT_mm, 1)
            pe.wait_ge(fT_ready, 2)
            for h in range(H):
                if h >= 2:
                    pe.wait_ge(nfk_ready, h - 1)
                mm(bank[6 + h % 2][:, :], negsel[:, h, :], fT[:, :], start=True, stop=True).then_inc(nfk_mm, 1)
            gemm_loop(16, hT)
            pe.wait_ge(nfk_ready, H)
            pe.wait_ge(out_free, npan[0])
            attend(qk2T, 0, 4, len(UNITS))
            pe.wait_ge(pv_used, 2 * len(UNITS))
            mix(ybr, oT)
            pe.wait_ge(mixed_ready, 2)
            gemm_loop(8, hT)
            norm()
            pe.wait_ge(h_ready, 5)
            gemm_loop(2 * FT, hT)
            n0 = npan[0]
            pe.wait_ge(out_free, n0)
            pe.wait_ge(act_ready, FT)

            def down(kt, s, rounds, rhs, first, last_tile):
                pe.wait_ge(panel_in[s], rounds)
                for nt in range(KT):
                    last = mm(bank[nt][:, :], ring[:, s, nt * P:(nt + 1) * P], rhs, start=first, stop=last_tile,
                              skip_group_check=True)
                last.then_inc(panel_done, 1)

            for kt in range(RING):
                down(kt, kt, 16 * (n0 // RING + 1), actT[:, kt, :], kt == 0, False)
            with pe.Fori(1, FT // RING) as i:
                for s in range(RING):
                    down(None, s, i * 16 + 16 * (n0 // RING + 1), actT[:, ds(i * RING + s, 1), :], False, False)
            for kt in range(FT // RING * RING, FT):
                down(kt, kt % RING, 16 * ((n0 + kt) // RING + 1), actT[:, kt, :], False, kt == FT - 1)
            norm()

        @block.vector
        def _(dve):
            v = nc.vector
            step = Steps(dve, dve_step)
            npan = [0]
            nrt = [0]

            def norm_rs():
                dve.wait_ge(rt_ready, nrt[0] + 1)
                v.reciprocal(rs[:, :], rt[:, nrt[0] % 2, :]).then_inc(rt_used, 1)
                nrt[0] += 1
                dve.wait_ge(rt_used, nrt[0])

            def norm(k):
                norm_rs()
                for c in range(KT):
                    last = v.scalar_tensor_tensor(hT[:, c, :], xT[:, c, :], V(NORMS[k], c), rs[:, :], ALU.mult, ALU.mult)
                return last

            def mix_evac():
                for n in range(8):
                    dve.wait_ge(panel_done, npan[0] + 1)
                    step(v.tensor_tensor(rs[:, :], bank[2 * (n % 2) + 1][:, :], gates[:, 8 + n, :], ALU.mult))
                    v.tensor_tensor(hT[:, n, :], bank[2 * (n % 2)][:, :], gates[:, n, :], ALU.mult).then_inc(out_free, 1)
                    npan[0] += 1
                    dve.wait_ge(out_free, npan[0])
                    last = v.tensor_tensor(hT[:, n, :], hT[:, n, :], rs[:, :], ALU.add)
                    step(last)
                dve.sem_inc(mixed_ready, 1)

            def add_to_x():
                n0 = npan[0]
                with dve.Fori(0, KT // RING) as i:
                    for s in range(RING):
                        dve.wait_ge(panel_done, i * RING + (n0 + s + 1))
                        x = xT[:, ds(i * RING + s, 1), :]
                        v.tensor_tensor(x, x, bank[s][:, :].rearrange("p (a n) -> p a n", a=1), ALU.add)\
                         .then_inc(out_free, 1)
                npan[0] += KT
                dve.wait_ge(out_free, npan[0])
                dve.sem_inc(x_ready, 1)

            def attend(first, logits):
                m = len(UNITS)
                for i in range(m + 2):
                    if i < m:
                        qb, h = UNITS[i]
                        n = P * (qb + 1)
                        dve.wait_ge(lg_ready, first + i + 1)
                        if i >= 2:
                            dve.wait_ge(ex_ready, first + i - 1)
                        logits(i, qb, h, n)
                    if 1 <= i <= m:
                        j = i - 1
                        dve.wait_ge(ex_ready, first + j + 1)
                        if first + j >= 4:
                            dve.wait_ge(prob_ready, first + j - 3)
                        v.reciprocal(rsum[:, j % 4:j % 4 + 1], esum[:, j % 4:j % 4 + 1]).then_inc(rsum_ready, 1)
                    if i >= 2:
                        j = i - 2
                        qb, h = UNITS[j]
                        r = 64 * (h % 2)
                        dve.wait_ge(pv_ready, first + j + 1)
                        v.tensor_copy(oT[r:r + 64, h // 2, qb * P:(qb + 1) * P], bank[j % 2][r:r + 64, 0:P])\
                         .then_inc(pv_used, 1)

            dve.wait_ge(vec_in, 16)
            dve.wait_ge(x_in, 32)
            norm(0).then_inc(h_ready, 1)
            dve.wait_ge(ki_copied, 2)
            j = 0
            for qb in range(1, TB):
                n = P * (qb + 1)
                for h in range(H):
                    dve.wait_ge(relu_ready, j + 1)
                    w = wi[:, qb * H + h:qb * H + h + 1]
                    if h == 0:
                        v.tensor_scalar(score[:, 0:n], lg[:, j % 2, 0:n], w, None, ALU.mult).then_inc(relu_used, 1)
                    else:
                        v.scalar_tensor_tensor(score[:, 0:n], lg[:, j % 2, 0:n], w, score[:, 0:n], ALU.mult, ALU.add)\
                         .then_inc(relu_used, 1)
                    j += 1
                    dve.wait_ge(relu_used, j)
                step(v.memset(score[0:64, n - 64:n], MASKED))
                for rnd in range(TOPK // 8):
                    step(v.max(out=top8[:, :], in_=score[:, 0:n]))
                    step(v.match_replace(out=score[:, 0:n], in_to_replace=top8[:, :], in_values=score[:, 0:n],
                                         imm_value=TAKEN))
                step(v.tensor_scalar(mask[:, MOFF[qb]:MOFF[qb] + n], score[:, 0:n], TAKEN / 2, MASKED, ALU.is_gt, ALU.mult))
            npan[0] += 4 + 8 + 4 + 16
            for c in range(8):
                norm_rs()
                dve.wait_ge(out_free, 12)
                step(v.scalar_tensor_tensor(qkiT[:, 4 + c, :], qkiT[:, 4 + c, :], V("q_g" if c < 4 else "k_g"), rs[:, :],
                                            ALU.mult, ALU.mult))
                dve.sem_inc(qk_ready, 1)
            for c in range(CT):
                dve.wait_ge(u_sig, c + 1)
                npan[0] += 2
                v.tensor_tensor(upad[:, c, TAPS - 1:TAPS - 1 + S], bank[(2 * c) % 4][:, :], lg[:, c % 2, :], ALU.mult)\
                 .then_inc(out_free, 2)
            dve.wait_ge(out_free, npan[0])
            dve.wait_ge(rel_in, 16)
            dve.wait_ge(const_ready, 1)

            def logits_one(i, qb, h, n):
                step(v.scalar_tensor_tensor(lg[:, i % 2, 0:n], bank[4 + i % 2][:, 0:n], HD ** -0.5,
                                            bias[:, h, 0:n][:, ::-1], ALU.mult, ALU.add))
                step(v.tensor_tensor(lg[:, i % 2, 0:n], lg[:, i % 2, 0:n], mask[:, MOFF[qb]:MOFF[qb] + n], ALU.add))
                v.tensor_reduce(nmax[:, i % 4:i % 4 + 1], lg[:, i % 2, 0:n], axis=AX.X, op=ALU.max, negate=True)\
                 .then_inc(lg_done, 1)

            attend(0, logits_one)
            for k in range(TAPS):
                for c in range(CT):
                    w = V("conv_w", c * TAPS + k)
                    src = upad[:, c, k:k + S]
                    if k == 0:
                        v.tensor_scalar(ybr[:, c, :], src, w, V("conv_b", c), ALU.mult, ALU.add).then_inc(cv, 1)
                    else:
                        dve.wait_ge(cv, (k - 1) * CT + c + 1)
                        v.scalar_tensor_tensor(ybr[:, c, :], src, w, ybr[:, c, :], ALU.mult, ALU.add).then_inc(cv, 1)
            dve.wait_ge(cm_ready, 1)
            for c in range(CT):
                v.tensor_tensor(ybr[:, c, :], ybr[:, c, :], bank[4][:, :], ALU.subtract).then_inc(cx_ready, 1)
            dve.wait_ge(csd_ready, 1)
            step(v.reciprocal(rs[:, :], rt[:, 0, :]))
            for c in range(CT):
                v.tensor_tensor(ybr[:, c, :], ybr[:, c, :], rs[:, :], ALU.mult).then_inc(cn_ready, 1)
            dve.wait_ge(cn_ready, CT)
            mix_evac()
            add_to_x()
            norm(1).then_inc(h_ready, 1)
            npan[0] += 16
            dve.wait_ge(peer_free, 1)

            def route(tb):
                for hc in range(16):
                    half, col = hc // 8, (hc % 8) * P
                    src = sc[:, half, col:col + P]
                    dve.wait_ge(sc_ready, tb * 4 + hc // 4 + 1)
                    step(v.max(out=sv[:, hc, 0:8], in_=src))
                    v.max_index(out=si[:, hc, 0:8], in_max=sv[:, hc, 0:8], in_values=src)
                    step(v.match_replace(out=sc2[:, :], in_to_replace=sv[:, hc, 0:8], in_values=src, imm_value=TAKEN))
                    if hc % 8 == 7:
                        dve.sem_inc(sc_used, 1)
                    step(v.max(out=sv[:, hc, 8:16], in_=sc2[:, :]))
                    step(v.max_index(out=si[:, hc, 8:16], in_max=sv[:, hc, 8:16], in_values=sc2[:, :]))
                v.tensor_copy(sif[:, :, :], si[:, :, :])
                s4 = sv[:, :, :].rearrange("p (h c) k -> p h c k", c=2)
                step(v.tensor_tensor(cand[:, :, :].rearrange("p h (a b) -> p h a b", a=PK),
                                     s4[:, :, 0, :].unsqueeze(3).to_broadcast([P, PH, PK, PK]),
                                     s4[:, :, 1, :].unsqueeze(2).to_broadcast([P, PH, PK, PK]), ALU.add))
                for h in range(PH):
                    step(v.max(out=tops[:, h, 0:8], in_=cand[:, h, :]))
                    v.max_index(out=topj[:, h, 0:8], in_max=tops[:, h, 0:8], in_values=cand[:, h, :])
                    step(v.match_replace(out=cand2[:, :], in_to_replace=tops[:, h, 0:8], in_values=cand[:, h, :],
                                         imm_value=TAKEN))
                    step(v.max(out=tops[:, h, 8:16], in_=cand2[:, :]))
                    step(v.max_index(out=topj[:, h, 8:16], in_max=tops[:, h, 8:16], in_values=cand2[:, :]))
                gt = gate[:, tb % 2, :].rearrange("p (h k) -> p h k", h=PH)
                v.tensor_tensor(gt, tops[:, :, :], tops[:, :, 0:1].to_broadcast([P, PH, PK]), ALU.subtract)\
                 .then_inc(g_shift, 1)
                tj = topj[:, :, :].rearrange("p h k -> p (h k)")
                v.tensor_scalar(tja[:, 0, :], tj, 4, None, ALU.logical_shift_right)
                step(v.tensor_scalar(tja[:, 1, :], tj, 15, None, ALU.bitwise_and))
                step(v.tensor_copy(tjf[:, :, :], tja[:, :, :]))
                e4 = eqv[:, :, :].rearrange("p h (k a) -> p h k a", k=PK)
                i4 = sif[:, :, :].rearrange("p (h c) a -> p h c a", c=2)
                for c in range(2):
                    t3 = tjf[:, c, :].rearrange("p (h k) -> p h k", h=PH)
                    step(v.tensor_tensor(e4, t3.unsqueeze(3).to_broadcast([P, PH, PK, PK]),
                                         iota16[:, :].unsqueeze(1).unsqueeze(1).to_broadcast([P, PH, PK, PK]),
                                         ALU.is_equal))
                    step(v.tensor_tensor(e4, e4, i4[:, :, c, :].unsqueeze(2).to_broadcast([P, PH, PK, PK]), ALU.mult))
                    step(v.tensor_reduce(eij[:, c, :].rearrange("p (h k) -> p h k", h=PH), e4, axis=AX.X, op=ALU.add))
                step(v.scalar_tensor_tensor(eij[:, 0, :], eij[:, 0, :], 128.0, eij[:, 1, :], ALU.mult, ALU.add))
                step(v.tensor_copy(eidx[:, tb % 2, :], eij[:, 0, :]))
                dve.sem_inc(idx_ready, 1)
                dve.wait_ge(g_exp, tb + 1)
                step(v.tensor_reduce(gsum[:, 0, :], gt, axis=AX.X, op=ALU.add))
                step(v.reciprocal(gsum[:, 1, :], gsum[:, 0, :]))
                step(v.tensor_tensor(gt, gt, gsum[:, 1, :].unsqueeze(2).to_broadcast([P, PH, PK]), ALU.mult))

            ROUNDS = NSEL // 16

            def rows(turn, per, emit):
                base = step.n
                with dve.Fori(0, ROUNDS) as i:
                    step.n = i * per + base
                    for half in range(2):
                        emit(i, half, turn)
                step.n = base + ROUNDS * per

            def arrived(i, half, u, turn):
                dve.wait_ge(gathered[u], i * 32 + 16 * (2 * turn + half + 1))

            route(0)
            dve.wait_ge(htok_ready, 2 * TB)
            for tb in range(TB):
                def dot_rows(i, half, turn):
                    for u in range(8):
                        arrived(i, half, u, turn)
                        v.tensor_tensor_reduce(out=grows[:, u, :], in0=grows[:, u, :], in1=h2tok[:, tb, :], scale=1.0,
                                               scalar=0.0, op0=ALU.mult, op1=ALU.add,
                                               accum_out=dots8[:, half, u:u + 1]).then_inc(row_used, 1)
                    dve.wait_ge(row_used, i * 16 + (turn * 16 + 8 * (half + 1)))
                    step(v.tensor_copy(dots[:, ds(i * 16 + 8 * half, 8)], dots8[:, half, :]))

                rows(2 * tb * ROUNDS, 2, dot_rows)
                dve.sem_inc(dots_ready, 1)
                if tb + 1 < TB:
                    route(tb + 1)
                dve.wait_ge(gel_ready, tb + 1)
                v.memset(acc[:, :], 0.0)
                step(v.tensor_tensor(act[:, :], gel[:, :], gate[:, tb % 2, :], ALU.mult))

                def add_rows(i, half, turn):
                    step(v.tensor_copy(act8[:, half, :], act[:, ds(i * 16 + 8 * half, 8)]))
                    for u in range(8):
                        arrived(i, half, u, turn)
                        v.scalar_tensor_tensor(acc[:, :], grows[:, u, :], act8[:, half, u:u + 1], acc[:, :],
                                               ALU.mult, ALU.add).then_inc(row_used, 1)
                        dve.wait_ge(row_used, i * 16 + (turn * 16 + 8 * half + u + 1))

                rows((2 * tb + 1) * ROUNDS, 2, add_rows)
                dve.sem_inc(acc_ready, 1)
                for j in range(2):
                    dve.wait_ge(acc_tr, 2 * tb + j + 1)
                    x = xT[:, 4 * j:4 * j + 4, tb * P:(tb + 1) * P]
                    step(v.tensor_tensor(x, x, bank[6 + j][:, :].rearrange("p (c t) -> p c t", c=4), ALU.add))
                    dve.sem_inc(acc_used, 1)
            dve.sem_inc(x_ready, 1)
            norm(2).then_inc(h_ready, 1)
            for n in range(8):
                dve.wait_ge(sg_ready, n + 1)
                npan[0] += 1
                v.tensor_tensor(sg[:, n % 2, :], sg[:, n % 2, :], bank[2 * (n % 2) + 1][:, :], ALU.mult).then_inc(out_free, 1)
                dve.wait_ge(out_free, npan[0])
                step(v.tensor_tensor(xT[:, n, :], xT[:, n, :], sg[:, n % 2, :], ALU.add))
                dve.sem_inc(sg_used, 1)
            dve.sem_inc(x_ready, 1)
            norm(3).then_inc(h_ready, 1)
            npan[0] += 4
            dve.wait_ge(out_free, npan[0])
            dve.wait_ge(two_const, 1)
            for c in range(CT):
                dve.wait_ge(panel_done, npan[0] + 1)
                v.tensor_tensor(zpad[:, c, 2:S + 2], bank[c][:, :], ccT[:, c, :], ALU.mult).then_inc(out_free, 1)
                npan[0] += 1
                dve.wait_ge(out_free, npan[0])
                step(v.tensor_scalar(ybr[:, c, :], zpad[:, c, 2:S + 2], V("conv_mix_w", c * 3 + 2), None, ALU.mult))
                for k in range(2):
                    step(v.scalar_tensor_tensor(ybr[:, c, :], zpad[:, c, k:k + S], V("conv_mix_w", c * 3 + k),
                                                ybr[:, c, :], ALU.mult, ALU.add))
            for c in range(CT):
                dve.wait_ge(panel_done, npan[0] + 1)
                v.tensor_tensor(ybr[:, c, :], ybr[:, c, :], bank[c][:, :], ALU.mult).then_inc(out_free, 1)
                npan[0] += 1
            dve.wait_ge(f_ready, 1)
            step(v.tensor_tensor(z[:, 0, :], bank[4][:, 0:TB * H], V("b_f", 0, TB * H), ALU.add))
            dve.sem_inc(z_ready, 1)
            step(v.tensor_scalar(z[:, 2, :], z[:, 0, :], 0.0, None, ALU.min))
            dve.wait_ge(sp_ready, 1)
            v.tensor_tensor(z[:, 2, :], z[:, 2, :], z[:, 1, :], ALU.subtract).then_inc(logf_ready, 1)
            dve.wait_ge(fT_mm, 2)
            v.tensor_copy(fq[:, :], bank[4][:, 0:TB * H]).then_inc(fT_ready, 1)
            dve.wait_ge(nfk_ready, H)
            dve.wait_ge(fT_ready, 2)
            npan[0] += 8 + 4 + 16

            def logits_two(i, qb, h, n):
                step(v.scalar_tensor_tensor(lg[:, i % 2, 0:n], bank[4 + i % 2][:, 0:n], fq[:, qb * H + h:qb * H + h + 1],
                                            nfk[:, h, 0:n], ALU.add, ALU.add))
                step(v.tensor_tensor(lg[:, i % 2, n - P:n], lg[:, i % 2, n - P:n], causal[:, :], ALU.add))
                v.tensor_reduce(nmax[:, i % 4:i % 4 + 1], lg[:, i % 2, 0:n], axis=AX.X, op=ALU.max, negate=True)\
                 .then_inc(lg_done, 1)

            attend(len(UNITS), logits_two)
            dve.wait_ge(pv_used, 2 * len(UNITS))
            mix_evac()
            add_to_x()
            norm(4).then_inc(h_ready, 1)
            n0 = npan[0]
            base = step.n
            with dve.Fori(0, 2 * FT // RING) as i:
                step.n = i * 8 + base
                for s in range(RING):
                    dve.wait_ge(out_free, i * RING + (n0 + s + 1))
                    step(v.tensor_scalar(upc[:, s, :], uppad[:, s, 2:S + 2], V("conv_ffn_w", i * 12 + (3 * s + 2)), None,
                                         ALU.mult))
                    step(v.scalar_tensor_tensor(upc[:, s, :], uppad[:, s, 0:S], V("conv_ffn_w", i * 12 + 3 * s),
                                                upc[:, s, :], ALU.mult, ALU.add))
                    v.scalar_tensor_tensor(upc[:, s, :], uppad[:, s, 1:S + 1], V("conv_ffn_w", i * 12 + (3 * s + 1)),
                                           upc[:, s, :], ALU.mult, ALU.add).then_inc(up_conv, 1)
                for s in (0, 2):
                    dve.wait_ge(up_conv, i * RING + (s + 2))
                    dve.wait_ge(up_silu, i * 2 + (s // 2 + 1))
                    v.tensor_tensor(actT[:, ds(i * 2 + s // 2, 1), :].rearrange("p a n -> p (a n)"), upc[:, s, :],
                                    upc[:, s + 1, :], ALU.mult).then_inc(act_ready, 1)
                dve.wait_ge(act_ready, i * 2 + 2)
            step.n = base + 8 * (2 * FT // RING)
            npan[0] += 2 * FT + FT
            dve.wait_ge(panel_done, NPANEL)
            for nt in range(KT):
                step(v.tensor_tensor(xT[:, nt, :], xT[:, nt, :], bank[nt][:, :], ALU.add))
            dve.sem_inc(x_ready, 1)
            norm(5).then_inc(y_ready, 1)


def kernel(**inputs):
    import concourse.bacc as bacc
    from concourse.bass_utils import run_bass_kernel_spmd

    a = {k: np.asarray(v) for k, v in inputs.items()}

    def tiles(w):
        kt, n = w.shape[0] // P, w.shape[1] // P
        return w.reshape(kt, P, n, P).transpose(2, 1, 0, 3).reshape(n, P, kt * P)

    def values(w):
        return w.reshape(4, 2, P, 512).transpose(0, 2, 1, 3).reshape(4, P, 2 * 512)

    def pairs(x, y):
        return np.stack([x, y], 1).reshape(-1, *x.shape[1:])

    w1, w2 = a["w_in"][0], a["w_in_2"][0]
    wq, wk, wv, wqi, wki, wwi, wglu, wgates = np.split(w1, np.cumsum([512, 512, 512, 512, 64, 8, 1024]), axis=1)
    cb, cc, cin, q2, k2, v2, wf, gates2 = np.split(w2, np.cumsum([512, 512, 512, 512, 512, 512, 8]), axis=1)
    up = tiles(a["w_up_2"][0])
    panels = np.concatenate([
        tiles(wqi), tiles(wq), tiles(wk), values(wv), tiles(wgates), pairs(tiles(wglu[:, :512]), tiles(wglu[:, 512:])),
        tiles(np.concatenate([a["w_att_out"][0], a["w_conv_out"][0]], 0)), tiles(a["w_out"][0]),
        tiles(a["w_peer_q"][0]), tiles(a["w_ple_gate"][0]),
        tiles(cc), tiles(cin), tiles(cb), tiles(q2), tiles(k2), values(v2), tiles(gates2),
        tiles(np.concatenate([a["w_out_conv_2"][0], a["w_out_attn_2"][0]], 0)), tiles(a["w_o_2"][0]),
        pairs(up[:FT], up[FT:]), a["w_down_2"][0].reshape(FT, P, D)], 0)

    def col(v):
        v = v.reshape(-1, P, *v.shape[1:])
        return np.moveaxis(v, 1, 0).reshape(P, -1)

    ffn_w = col(a["conv_ffn_w_2"][0].T).reshape(P, 2, FT, 3).transpose(0, 2, 1, 3).reshape(P, -1)
    vecs = np.concatenate([
        col(a["attn_norm_g"][0]), col(a["b_gate"][0]), np.tile(a["q_norm_g"][0], 2)[:, None],
        np.tile(a["k_norm_g"][0], 2)[:, None], col(a["conv_w"][0, :, 0, :].T), col(a["conv_b"][0]),
        col(a["conv_ln_g"][0]), col(a["conv_ln_b"][0]), col(a["ffn_norm_g"][0]), col(a["ple_norm_g"][0]),
        col(a["norm_mix_g_2"][0]), col(a["b_gate_2"][0]), col(a["conv_mix_w_2"][0].T), col(a["norm_ffn_g_2"][0]),
        ffn_w, col(a["norm_f_g_2"]), np.tile(a["b_f_2"][0], (P, TB))], 1)

    rel = P - np.arange(REL)
    n = np.abs(rel)
    large = 8 + (np.log(np.maximum(n, 1).astype(np.float32) / np.float32(8)) / np.float32(np.log(1024 / 8)) * 8).astype(np.int32)
    bucket = np.where(rel > 0, 16, 0) + np.where(n < 8, n, np.minimum(large, 15))
    onehot = (bucket[None, :] == np.arange(32)[:, None]).astype(np.float32)

    args = dict(
        xT=np.ascontiguousarray(a["x"][0].T.reshape(KT, P, S).transpose(1, 0, 2)),
        pT=np.ascontiguousarray(a["p"][0, 0].T.reshape(2, P, S).transpose(1, 0, 2)),
        panels=panels, vecs=vecs,
        wki=np.ascontiguousarray(wki.reshape(KT, P, 64).transpose(1, 0, 2).reshape(P, -1)),
        wwi=np.ascontiguousarray(wwi.reshape(KT, P, H).transpose(1, 0, 2).reshape(P, -1)),
        wf=np.ascontiguousarray(wf.reshape(KT, P, H).transpose(1, 0, 2).reshape(P, -1)),
        wpp=np.ascontiguousarray(a["w_ple_proj"][0].reshape(2, P, D).transpose(1, 0, 2)),
        subk=np.ascontiguousarray(a["peer_sub_keys"][0].transpose(3, 0, 1, 2).reshape(P, 16, P)),
        relb=a["rel_bias"], onehot=onehot, peer_u=a["peer_u"][0], peer_v=a["peer_v"][0])
    args = {k: np.ascontiguousarray(v) for k, v in args.items()}
    nc = bacc.Bacc("TRN2", target_bir_lowering=False, num_devices=1)
    aps = [nc.dram_tensor("in_" + k, v.shape, mybir.dt.float32, kind="ExternalInput").ap() for k, v in args.items()]
    out = nc.dram_tensor("y", (P, KT, S), mybir.dt.float32, kind="ExternalOutput").ap()
    build(nc, *aps, out)
    r = run_bass_kernel_spmd(nc, [{"in_" + k: v for k, v in args.items()}], core_ids=[0])
    y = r.results[0]["y"]
    return y.transpose(1, 0, 2).reshape(D, S).T.reshape(1, S, D)
```

```python
import numpy as np
import concourse.bass as bass
from concourse import mybir
from contextlib import ExitStack

P = 128
S, D = 512, 1024
TB = S // P
KT = D // P
H, HD = 8, 64
TOPK = 128
CT = 4
TAPS = 31
PH, PK = 8, 16
NSEL = PH * PK
FT = 22
EPS = 1e-6
MASKED = -1.0e30
TAKEN = -3.0e38
REL = 640

STREAM = [("qi", 4), ("q", 4), ("k", 4), ("v", 4), ("glu", 8), ("gates", 16), ("mix", 8), ("w_out", 8),
          ("peer_q", 16), ("ple_gate", 8),
          ("cc", 4), ("cin", 4), ("cb", 4), ("q2", 4), ("k2", 4), ("v2", 4), ("gates2", 16), ("mix2", 8),
          ("w_o", 8), ("up", 2 * FT), ("down", FT)]
FIRST = {}
NPANEL = 0
for _name, _n in STREAM:
    FIRST[_name] = NPANEL
    NPANEL += _n
RING = 4
RAW = 2

VEC = [("attn_g", 8), ("b_gate", 16), ("q_g", 1), ("k_g", 1), ("conv_w", CT * TAPS), ("conv_b", CT), ("ln_g", CT),
       ("ln_b", CT), ("ffn_g", 8), ("ple_g", 8), ("mix_g2", 8), ("b_gate2", 16), ("conv_mix_w", CT * 3),
       ("ffn_g2", 8), ("conv_ffn_w", 2 * FT * 3), ("norm_f_g", 8), ("b_f", 8 * TB)]
VCOL = {}
NVEC = 0
for _name, _n in VEC:
    VCOL[_name] = NVEC
    NVEC += _n


def build(nc, xT_d, pT_d, panels_d, vecs_d, wki_d, wwi_d, wf_d, wpp_d, subk_d, relb_d, onehot_d, u_d, v_d, out_d):
    f32 = mybir.dt.float32
    u32 = mybir.dt.uint32
    f32r = mybir.dt.float32r
    ALU = mybir.AluOpType
    ACT = mybir.ActivationFunctionType
    AX = mybir.AxisListType
    ds = bass.ds

    ctx = ExitStack()
    with ctx:
        def sem(name):
            return ctx.enter_context(nc.semaphore(name))

        def sb(name, shape, dt=f32, stack=ctx):
            return stack.enter_context(nc.sbuf_tensor(name, shape, dt))

        bank = [ctx.enter_context(nc.psum_tensor(f"bank{i}", [P, 512], f32)) for i in range(8)]
        rel_tab_d = nc.dram_tensor("rel_tab", (H, REL), f32)

        xT = sb("xT", [P, KT, S])
        ring = sb("ring", [P, RAW, D])
        vec = sb("vec", [P, NVEC])
        ident = sb("ident", [P, P])
        mean_d = sb("mean_d", [P, P])
        mean_h = sb("mean_h", [P, P])
        mean_c = sb("mean_c", [P, P])
        epsc = sb("epsc", [P, 1])
        sq = sb("sq", [P, 2, S])
        rt = sb("rt", [P, 2, S])
        rs = sb("rs", [P, S])

        ops = ExitStack()
        wH = sb("wH", [P, RING, D], f32r, stack=ops)
        wL = sb("wL", [P, RING, D], f32r, stack=ops)
        hH = sb("hH", [P, KT, S], f32r, stack=ops)
        hL = sb("hL", [P, KT, S], f32r, stack=ops)

        att = ExitStack()
        gates = sb("gates", [P, 16, S], stack=att)
        vtok = sb("vtok", [P, TB, 512], stack=att)
        oT = sb("oT", [P, CT, S], stack=att)
        lg = sb("lg", [P, 2, S], stack=att)
        pad = sb("pad", [P, CT, TAPS - 1 + S], stack=att)
        padf = pad[:, :, :].rearrange("p a b -> p (a b)")
        ex = padf[:, 0:2 * S].rearrange("p (a b) -> p a b", a=2)
        pT = padf[:, 2 * S:4 * S].rearrange("p (a b) -> p a b", a=2)
        nmax = sb("nmax", [P, 4], stack=att)
        esum = sb("esum", [P, 4], stack=att)
        rsum = sb("rsum", [P, 4], stack=att)

        one = ExitStack()
        qkiT = sb("qkiT", [P, 12, S], stack=one)
        kiT = sq[:, 1, :]
        bias = sb("bias", [P, H, S], stack=one)
        MOFF = [0, 128, 384, 768]
        mask = sb("mask", [P, 1280], stack=one)
        upad = pad
        ybr = qkiT[:, 0:4, :]
        scores = gates[:, 12:15, :]
        top8 = sb("top8", [P, 8 * TB], stack=one)
        onehot = rt[0:32, :, :].rearrange("p a b -> p (a b)")
        reltab = sq[0:8, :, :].rearrange("p a b -> p (a b)")
        relb = sb("relb", [32, H], stack=one)
        wi = sb("wi", [P, TB * H], stack=one)
        wwi = sb("wwi", [P, KT * H], stack=one)
        wki2 = bias[:, 0:2, :].rearrange("p a (k n) -> p (a k) n", n=P)
        one.close()

        two = ExitStack()
        ccT = sb("ccT", [P, CT, S], stack=two)
        qk2T = sb("qk2T", [P, 8, S], stack=two)
        zpad = pad[:, :, TAPS - 3:]
        ybr2 = ccT
        wf = sb("wf", [P, KT * H], stack=two)
        tri = oT
        nfk = sb("nfk", [P, H, S], stack=two)
        fq = sb("fq", [P, TB * H], stack=two)
        fT = rs[0:H, :]
        negsel = lg[0:H, :, :].rearrange("p a (b n) -> p (a b) n", n=P)
        causal = sb("causal", [P, P], stack=two)
        z = sb("z", [P, 4, TB * H], stack=two)
        two.close()

        branch = ExitStack()
        oL, yH, yL, oH = (sb(n, [P, CT, S], f32r, stack=branch) for n in ("oL", "yH", "yL", "oH"))
        branch.close()
        att.close()
        ops.close()

        pe_ = ExitStack()
        NG = 16
        grows = sb("grows", [P, NG, D], stack=pe_)
        h2tok = sb("h2tok", [P, TB, D], stack=pe_)
        qpT = sb("qpT", [P, 16, S], stack=pe_)
        subk = sb("subk", [P, 16, P], stack=pe_)
        acc = sb("acc", [P, D], stack=pe_)
        sc = sb("sc", [P, 2, D], stack=pe_)
        sc2 = sb("sc2", [P, P], stack=pe_)
        sv = sb("sv", [P, 16, PK], stack=pe_)
        si = sb("si", [P, 16, PK], u32, stack=pe_)
        sif = sb("sif", [P, 16, PK], stack=pe_)
        cand = sb("cand", [P, PH, PK * PK], stack=pe_)
        cand2 = sb("cand2", [P, PK * PK], stack=pe_)
        tops = sb("tops", [P, PH, PK], stack=pe_)
        topj = sb("topj", [P, PH, PK], u32, stack=pe_)
        tja = sb("tja", [P, 2, PH * PK], u32, stack=pe_)
        spare = sb("spare", [P, 7 * NSEL], stack=pe_)
        dots, gel, act = (spare[:, j * NSEL:(j + 1) * NSEL] for j in range(3))
        tjf, eij = (spare[:, j:j + 2 * NSEL].rearrange("p (a b) -> p a b", a=2) for j in (3 * NSEL, 5 * NSEL))
        iota16 = sb("iota16", [P, PK], stack=pe_)
        eqv = sb("eqv", [P, PH, PK * PK], stack=pe_)
        gsum = sb("gsum", [P, 2, PH], stack=pe_)
        gate = sb("gate", [P, 2, NSEL], stack=pe_)
        eidx = sb("eidx", [P, 2, NSEL], u32, stack=pe_)
        idxs = sb("idxs", [P, 2, 8], u32, stack=pe_)
        dots8 = sb("dots8", [P, 2, 8], stack=pe_)
        act8 = sb("act8", [P, 2, 8], stack=pe_)
        pe_.close()

        ple = ExitStack()
        sb("ple_below", [P, 16 * D], stack=ple)
        pT_in = sb("pT_in", [P, 2, S], stack=ple)
        wpp = sb("wpp", [P, 2, D], stack=ple)
        sg = sb("sg", [P, 2, S], stack=ple)
        ple.close()

        ffn = ExitStack()
        sb("ffn_below", [P, 16 * D], stack=ffn)
        actH = sb("actH", [P, FT, S], f32r, stack=ffn)
        actL = sb("actL", [P, FT, S], f32r, stack=ffn)
        uppad = sb("uppad", [P, 4, S + 2], stack=ffn)
        upc = [sq[:, 0, :], sq[:, 1, :], rt[:, 0, :], rt[:, 1, :]]
        ffn.close()

        panel_in = [sem(f"panel_in{s}") for s in range(RAW)]
        panel_done = sem("panel_done")
        out_free = sem("out_free")
        hi_ready, lo_ready = sem("hi_ready"), sem("lo_ready")
        x_in = sem("x_in")
        vec_in = sem("vec_in")
        small_in = sem("small_in")
        const_ready = sem("const_ready")
        sq_ready, sq_used = sem("sq_ready"), sem("sq_used")
        rt_ready = sem("rt_ready")
        rt_used = sem("rt_used")
        h_ready = sem("h_ready")
        x_ready = sem("x_ready")
        ki_ready, ki_copied = sem("ki_ready"), sem("ki_copied")
        dot_ready, relu_ready, relu_used = sem("dot_ready"), sem("relu_ready"), sem("relu_used")
        qk_ready = sem("qk_ready")
        rel_ready, rel_copied, rel_out, rel_in = sem("rel_ready"), sem("rel_copied"), sem("rel_out"), sem("rel_in")
        lg_ready, lg_done, ex_ready = sem("lg_ready"), sem("lg_done"), sem("ex_ready")
        rsum_ready, prob_ready = sem("rsum_ready"), sem("prob_ready")
        tr_ready, pT_ready, pv_ready, pv_used = sem("tr_ready"), sem("pT_ready"), sem("pv_ready"), sem("pv_used")
        u_sig, br_ready, mixed_ready = sem("u_sig"), sem("br_ready"), sem("mixed_ready")
        cv = sem("cv")
        cm_ready, cx_ready, csq_ready, cvar_ready, csd_ready, cn_ready = (sem(n) for n in (
            "cm_ready", "cx_ready", "csq_ready", "cvar_ready", "csd_ready", "cn_ready"))
        htok_tr, htok_ready = sem("htok_tr"), sem("htok_ready")
        sc_mm, sc_ready, sc_used = sem("sc_mm"), sem("sc_ready"), sem("sc_used")
        g_shift, g_exp, idx_ready = sem("g_shift"), sem("g_exp"), sem("idx_ready")
        idx_staged, idx_seen = sem("idx_staged"), sem("idx_seen")
        gathered = [sem(f"gathered{s}") for s in range(NG)]
        row_used = sem("row_used")
        dots_ready, gel_ready = sem("dots_ready"), sem("gel_ready")
        acc_ready, acc_tr, acc_used = sem("acc_ready"), sem("acc_tr"), sem("acc_used")
        peer_in, ple_in = sem("peer_in"), sem("ple_in")
        sg_ready, sg_used = sem("sg_ready"), sem("sg_used")
        pp_ready = sem("pp_ready")
        cc_ready = sem("cc_ready")
        f_ready, z_ready, sp_ready, logf_ready = sem("f_ready"), sem("z_ready"), sem("sp_ready"), sem("logf_ready")
        fT_mm, fT_ready, nfk_mm, nfk_ready = sem("fT_mm"), sem("fT_ready"), sem("nfk_mm"), sem("nfk_ready")
        two_const, two_in = sem("two_const"), sem("two_in")
        up_copied, up_conv, up_silu, up_used = sem("up_copied"), sem("up_conv"), sem("up_silu"), sem("up_used")
        act_ready = sem("act_ready")
        act_hi = sem("act_hi")
        wf_ready, br_split, h_whole = sem("wf_ready"), sem("br_split"), sem("h_whole")
        small_ready = sem("small_ready")
        out_done, y_ready = sem("out_done"), sem("y_ready")
        dve_step, act_step, pool_step = sem("dve_step"), sem("act_step"), sem("pool_step")
        peer_free, ple_free = sem("peer_free"), sem("ple_free")
        qkv_done = sem("qkv_done")
        pads_ready = sem("pads_ready")

        class Steps:

            def __init__(self, eng, s):
                self.eng, self.sem, self.n = eng, s, 0

            def __call__(self, ins):
                ins.then_inc(self.sem, 1)
                self.n = self.n + 1
                self.eng.wait_ge(self.sem, self.n)

        def V(name, i=0, n=1):
            return vec[:, ds(VCOL[name] + i, n)] if not isinstance(i, int) else vec[:, VCOL[name] + i:VCOL[name] + i + n]

        NORMS = ["attn_g", "ffn_g", "ple_g", "mix_g2", "ffn_g2", "norm_f_g"]
        UNITS = [(qb, h) for qb in range(TB) for h in range(H)]

        block = ctx.enter_context(nc.Block())

        @block.sync
        def _(sp):
            sp.dma_start(xT[:, 0:4, :], xT_d[:, 0:4, :]).then_inc(x_in, 16)
            sp.dma_start(xT[:, 4:8, :], xT_d[:, 4:8, :]).then_inc(x_in, 16)
            for s in range(RAW):
                sp.dma_start(ring[:, s, :], panels_d[s, :, :]).then_inc(panel_in[s], 16)
            with sp.Fori(1, NPANEL // RAW) as i:
                for s in range(RAW):
                    sp.wait_ge(lo_ready, i * RAW + (s + 1 - RAW))
                    sp.dma_start(ring[:, s, :], panels_d[ds(i * RAW + s, 1), :, :].rearrange("a p n -> (a p) n"))\
                      .then_inc(panel_in[s], 16)
            sp.wait_ge(y_ready, 1)
            sp.dma_start(out_d[:, :, :], xT[:, :, :]).then_inc(out_done, 16)
            sp.wait_ge(out_done, 16)

        @block.gpsimd
        def _(pool):
            step = Steps(pool, pool_step)
            g = nc.gpsimd
            g.memset(epsc[:, :], EPS)
            g.memset(mean_d[:, :], 1.0 / D)
            g.memset(mean_c[:, :], 1.0 / 512)
            g.memset(mean_h[:, :], 0.0)
            g.memset(upad[:, :, 0:TAPS - 1], 0.0)
            step(g.memset(ident[:, :], 0.0))
            step(g.memset(mean_h[0:64, 0:64], 1.0 / HD))
            step(g.memset(mean_h[64:128, 64:128], 1.0 / HD))
            g.memset(mask[:, 0:P], 0.0)
            step(g.affine_select(out=ident[:, :], in_=ident[:, :], compare_op=ALU.not_equal, fill=1.0, base=0,
                                 pattern=[[-1, P]], channel_multiplier=1))
            g.memset(mask[0:64, 64:P], MASKED).then_inc(const_ready, 1)

            def probs(first):
                for i in range(len(UNITS)):
                    qb, h = UNITS[i]
                    n = P * (qb + 1)
                    pool.wait_ge(rsum_ready, first + i + 1)
                    g.tensor_scalar(ex[:, i % 2, 0:n], ex[:, i % 2, 0:n], rsum[:, i % 4:i % 4 + 1], None, ALU.mult)\
                     .then_inc(prob_ready, 1)

            npan = [0]

            def rests(m):
                n0 = npan[0]

                def rest(s, count):
                    pool.wait_ge(hi_ready, count)
                    g.tensor_tensor(wL[:, s, :], ring[:, s % RAW, :], wH[:, s, :].bitcast(f32), ALU.subtract).then_inc(lo_ready, 1)

                assert n0 % RING == 0
                if m >= RING:
                    with pool.Fori(0, m // RING) as i:
                        for s in range(RING):
                            rest(s, i * RING + (n0 + s + 1))
                for n in range(n0 + m // RING * RING, n0 + m):
                    rest(n % RING, n + 1)
                npan[0] += m

            rests(FIRST["mix"] + RING)
            probs(0)
            rests(FIRST["peer_q"] - npan[0])

            pool.wait_ge(x_ready, 1)
            step(g.iota(iota16[:, :], pattern=[[1, PK]], base=0, channel_multiplier=0,
                        allow_small_or_imprecise_dtypes=True))
            g.memset(sc2[:, 0:1], 0.0).then_inc(peer_free, 1)
            rests(FIRST["ple_gate"] - npan[0])
            ROUNDS = NSEL // 16
            for tb in range(TB):
                pool.wait_ge(idx_ready, tb + 1)
                for which, table in ((0, u_d), (1, v_d)):
                    turn = (2 * tb + which) * ROUNDS

                    def gather(i, first):
                        for half in range(2):
                            if not first:
                                pool.wait_ge(row_used, i * 16 + (turn * 16 + 8 * half - 8))
                            g.tensor_copy(idxs[:, half, :], eidx[:, tb % 2, ds(i * 16 + 8 * half, 8)])\
                             .then_inc(idx_staged, 1)
                            pool.wait_ge(idx_staged, i * 2 + (2 * turn + half + 1))
                            pool.sem_inc(idx_seen, 1)
                            for u in range(8):
                                g.indirect_dma_start(
                                    out=grows[:, 8 * half + u, :], out_offset=None, in_=table[:, :],
                                    in_offset=bass.IndirectOffsetOnAxis(ap=idxs[:, half, u:u + 1], axis=0),
                                ).then_inc(gathered[8 * half + u], 16)

                    gather(0, turn == 0)
                    with pool.Fori(1, ROUNDS) as i:
                        gather(i, False)

            rests(FIRST["cc"] + RING - npan[0])
            pool.wait_ge(x_ready, 3)
            g.memset(tri[:, :, :], 1.0)
            g.memset(causal[:, :], 0.0)
            g.memset(zpad[:, :, 0:2], 0.0)
            step(g.memset(negsel[:, :, :], 0.0))
            g.affine_select(out=tri[:, :, :], in_=tri[:, :, :], compare_op=ALU.is_ge, fill=0.0, base=0,
                            pattern=[[-P, TB], [1, S]], channel_multiplier=-1)
            g.affine_select(out=causal[:, :], in_=causal[:, :], compare_op=ALU.is_ge, fill=MASKED, base=0,
                            pattern=[[-1, P]], channel_multiplier=1)
            g.affine_select(out=negsel[:, :, :], in_=negsel[:, :, :], compare_op=ALU.not_equal, fill=-1.0, base=0,
                            pattern=[[-1, H], [0, P]], channel_multiplier=1).then_inc(two_const, 1)
            rests(FIRST["mix2"] + RING - npan[0])
            probs(len(UNITS))
            rests(FIRST["up"] + RING - npan[0])
            pool.wait_ge(x_ready, 4)
            g.memset(uppad[:, :, 0:2], 0.0).then_inc(pads_ready, 1)
            rests(NPANEL - npan[0])

        @block.scalar
        def _(act_e):
            step = Steps(act_e, act_step)
            a = nc.scalar
            a.dma_start(vec[:, :], vecs_d).then_inc(vec_in, 16)
            wki_src = wki_d.rearrange("p (k n) -> p k n", k=KT)
            a.dma_start(wki2[:, :, 0:64], wki_src).then_inc(small_in, 16)
            a.dma_start(wki2[:, :, 64:P], wki_src).then_inc(small_in, 16)
            a.dma_start(wwi[:, :], wwi_d).then_inc(small_in, 16)
            a.dma_start(relb[:, :], relb_d).then_inc(small_in, 16)
            a.dma_start(onehot[:, 0:REL], onehot_d).then_inc(small_in, 16)
            nsq = [0]
            nms = [0]
            due = [8] + [8 + c + 1 for c in range(8)] + [16 + 8 * (k + 1) for k in range(5)]
            npan = [0]

            def square(src):
                if nsq[0] >= 2:
                    act_e.wait_ge(sq_used, nsq[0] - 1)
                a.activation(sq[:, nsq[0] % 2, :], src, ACT.Square).then_inc(sq_ready, 1)
                nsq[0] += 1

            def root(ps):
                act_e.wait_ge(sq_used, due[nms[0]])
                if nms[0] >= 2:
                    act_e.wait_ge(rt_used, nms[0] - 1)
                a.activation(rt[:, nms[0] % 2, :], ps, ACT.Sqrt, bias=epsc[:, :]).then_inc(rt_ready, 1)
                nms[0] += 1

            def norm(k):
                act_e.wait_ge(x_ready, k) if k else act_e.wait_ge(x_in, 32)
                for c in range(KT):
                    square(xT[:, c, :])
                root(bank[4][:, :])

            def upper(s, loads, done):
                act_e.wait_ge(panel_in[s % RAW], loads)
                if done is not None:
                    act_e.wait_ge(panel_done, done)
                a.activation(wH[:, s, :], ring[:, s % RAW, :], ACT.Copy).then_inc(hi_ready, 1)

            nup = [0]

            def uppers(m):
                for n in range(nup[0], nup[0] + m):
                    upper(n % RING, 16 * (n // RAW + 1), n + 1 - RING if n >= RING else None)
                nup[0] += m

            def evac_loop(n_panels, emit, ahead=True):
                n0 = npan[0]
                if n0 and emit is not None:
                    act_e.wait_ge(out_free, n0)
                assert not ahead or nup[0] == n0 + RING
                with act_e.Fori(0, n_panels // RING) as i:
                    for s in range(RING):
                        if emit is not None:
                            act_e.wait_ge(panel_done, i * RING + (n0 + s + 1))
                            emit(i, s).then_inc(out_free, 1)
                        if ahead:
                            upper(s, i * 32 + 16 * ((n0 + RING + s) // RAW + 1), i * RING + (n0 + s + 1))
                npan[0] += n_panels
                if ahead:
                    nup[0] += n_panels

            act_e.wait_ge(const_ready, 1)
            act_e.wait_ge(vec_in, 16)
            act_e.wait_ge(rel_ready, 1)
            a.activation(reltab[:, 0:320], bank[6][0:8, 0:320], ACT.Copy)
            a.activation(reltab[:, 320:REL], bank[7][0:8, 0:320], ACT.Copy).then_inc(rel_copied, 1)
            act_e.wait_ge(rel_copied, 1)
            a.dma_start(rel_tab_d.ap(), reltab[:, 0:REL]).then_inc(rel_out, 16)
            act_e.wait_ge(rel_out, 16)
            norm(0)
            uppers(RING)
            evac_loop(4, lambda i, s: a.activation(qkiT[:, ds(i * RING + s, 1), :], bank[s][:, :], ACT.Copy))
            act_e.wait_ge(ki_ready, 1)
            a.activation(kiT[:, :], bank[4][:, :], ACT.Copy).then_inc(ki_copied, 1)
            act_e.wait_ge(ki_ready, 2)
            a.mul(wi[:, :], bank[5][:, 0:TB * H], float(np.float32(HD ** -0.5 * H ** -0.5))).then_inc(ki_copied, 1)
            rel_ap = rel_tab_d.ap()
            diag = bass.AP(tensor=rel_ap.tensor, offset=1, ap=[[1, P], [REL, H], [1, S]])
            a.dma_start(bias[:, :, :], diag).then_inc(rel_in, 16)
            for j in range(3 * H):
                n = P * (j // H + 2)
                act_e.wait_ge(dot_ready, j + 1)
                if j >= 2:
                    act_e.wait_ge(relu_used, j - 1)
                a.activation(lg[:, j % 2, 0:n], bank[4 + j % 2][:, 0:n], ACT.Relu).then_inc(relu_ready, 1)
            evac_loop(8, lambda i, s: a.activation(qkiT[:, ds(i * RING + (s + 4), 1), :], bank[s][:, :], ACT.Copy))
            uppers(RING)
            act_e.wait_ge(panel_done, npan[0] + 4)
            for tb in range(TB):
                a.activation(vtok[:, tb, :], bank[tb][:, :], ACT.Copy).then_inc(out_free, 1)
            npan[0] += 4

            def gate_loop(bname):
                evac_loop(16, lambda i, s: a.activation(gates[:, ds(i * RING + s, 1), :], bank[s][:, :], ACT.Sigmoid,
                                                        bias=V(bname, i * RING + s)))

            act_e.wait_ge(relu_used, 3 * H)
            for c in range(CT):
                act_e.wait_ge(panel_done, npan[0] + 2)
                if c >= 2:
                    act_e.wait_ge(out_free, npan[0] - 2)
                a.activation(lg[:, c % 2, :], bank[(2 * c + 1) % 4][:, :], ACT.Sigmoid).then_inc(u_sig, 1)
                npan[0] += 2
                uppers(2)
            for c in range(8):
                square(qkiT[:, 4 + c, :])
                if c >= 1:
                    root(bank[4 + (c - 1) % 2][:, :])
            root(bank[5][:, :])
            gate_loop("b_gate")

            def attend(first):
                for i in range(len(UNITS) + 1):
                    if i < len(UNITS):
                        n = P * (UNITS[i][0] + 1)
                        act_e.wait_ge(lg_done, first + i + 1)
                        if i >= 2:
                            act_e.wait_ge(tr_ready, first + i - 1)
                        a.activation(ex[:, i % 2, 0:n], lg[:, i % 2, 0:n], ACT.Exp, bias=nmax[:, i % 4:i % 4 + 1],
                                     accum_out=esum[:, i % 4:i % 4 + 1]).then_inc(ex_ready, 1)
                    if i >= 1:
                        j = i - 1
                        n = P * (UNITS[j][0] + 1)
                        act_e.wait_ge(tr_ready, first + j + 1)
                        if j >= 2:
                            act_e.wait_ge(pv_ready, first + j - 1)
                        a.activation(pT[:, j % 2, 0:n], bank[6 + j % 2][:, 0:n], ACT.Copy).then_inc(pT_ready, 1)

            attend(0)
            act_e.wait_ge(sq_used, nsq[0])
            for c in range(CT):
                act_e.wait_ge(cx_ready, c + 1)
                if c >= 2:
                    act_e.wait_ge(cvar_ready, c - 1)
                a.activation(sq[:, c % 2, :], ybr[:, c, :], ACT.Square).then_inc(csq_ready, 1)
            act_e.wait_ge(cvar_ready, CT)
            act_e.wait_ge(rt_used, nms[0])
            a.activation(rt[:, 0, :], bank[5][:, :], ACT.Sqrt, bias=epsc[:, :]).then_inc(csd_ready, 1)
            for c in range(CT):
                act_e.wait_ge(cn_ready, c + 1)
                a.activation(ybr[:, c, :], ybr[:, c, :], ACT.Silu, bias=V("ln_b", c), scale=V("ln_g", c))\
                 .then_inc(br_ready, 1)
            evac_loop(8 + 8, None)
            norm(1)
            act_e.wait_ge(peer_free, 1)
            a.dma_start(subk[:, :, :], subk_d).then_inc(peer_in, 16)
            evac_loop(12, lambda i, s: a.activation(qpT[:, ds(i * RING + s, 1), :], bank[s][:, :], ACT.Copy))
            evac_loop(4, lambda i, s: a.activation(qpT[:, ds(i * RING + (s + 12), 1), :], bank[s][:, :], ACT.Copy), False)
            for j in range(TB * 2):
                act_e.wait_ge(htok_tr, j + 1)
                a.activation(h2tok[:, j // 2, (j % 2) * 512:(j % 2) * 512 + 512], bank[6 + j % 2][:, :], ACT.Copy)\
                 .then_inc(htok_ready, 1)

            def score_copies(tb):
                for q4 in range(4):
                    act_e.wait_ge(sc_mm, tb * 4 + q4 + 1)
                    if tb >= 1 and q4 % 2 == 0:
                        act_e.wait_ge(sc_used, 2 * (tb - 1) + q4 // 2 + 1)
                    a.activation(sc[:, q4 // 2, (q4 % 2) * 512:(q4 % 2) * 512 + 512], bank[4 + q4 % 2][:, :], ACT.Copy)\
                     .then_inc(sc_ready, 1)

            def gate_exp(tb):
                act_e.wait_ge(g_shift, tb + 1)
                a.activation(gate[:, tb % 2, :], gate[:, tb % 2, :], ACT.Exp).then_inc(g_exp, 1)

            score_copies(0)
            gate_exp(0)
            for tb in range(TB):
                if tb + 1 < TB:
                    score_copies(tb + 1)
                act_e.wait_ge(dots_ready, tb + 1)
                a.activation(gel[:, :], dots[:, :], ACT.Gelu_apprx_tanh).then_inc(gel_ready, 1)
                if tb + 1 < TB:
                    gate_exp(tb + 1)
            act_e.wait_ge(x_ready, 2)
            a.dma_start(pT_in[:, :, :], pT_d).then_inc(ple_in, 16)
            a.dma_start(wpp[:, :, :], wpp_d).then_inc(ple_in, 16)
            uppers(RING)
            for c in range(KT):
                square(xT[:, c, :])
            root(bank[4][:, :])
            for c in range(KT):
                act_e.wait_ge(panel_done, npan[0] + 1)
                if c >= 2:
                    act_e.wait_ge(sg_used, c - 1)
                a.activation(sg[:, c % 2, :], bank[2 * (c % 2)][:, :], ACT.Sigmoid).then_inc(sg_ready, 1)
                npan[0] += 1
                uppers(1)

            act_e.wait_ge(x_ready, 3)
            a.dma_start(wf[:, :], wf_d).then_inc(two_in, 16)
            for c in range(KT):
                square(xT[:, c, :])
            root(bank[4][:, :])
            evac_loop(4, lambda i, s: a.activation(ccT[:, ds(i * RING + s, 1), :], bank[s][:, :], ACT.Copy))
            evac_loop(8, None)
            act_e.wait_ge(z_ready, 1)
            step(a.activation(z[:, 1, :], z[:, 0, :], ACT.Abs))
            step(a.activation(z[:, 1, :], z[:, 1, :], ACT.Exp, scale=-1.0))
            a.activation(z[:, 1, :], z[:, 1, :], ACT.Ln, bias=1.0).then_inc(sp_ready, 1)
            evac_loop(4, lambda i, s: a.activation(qk2T[:, ds(i * RING + s, 1), :], bank[s][:, :], ACT.Copy,
                                                   scale=HD ** -0.5))
            evac_loop(4, lambda i, s: a.activation(qk2T[:, ds(i * RING + (s + 4), 1), :], bank[s][:, :], ACT.Copy))
            uppers(RING)
            act_e.wait_ge(panel_done, npan[0] + 4)
            for tb in range(TB):
                a.activation(vtok[:, tb, :], bank[tb][:, :], ACT.Copy).then_inc(out_free, 1)
            npan[0] += 4
            act_e.wait_ge(fT_mm, 1)
            a.activation(fT[:, :], bank[5][0:H, :], ACT.Copy).then_inc(fT_ready, 1)
            for h in range(H):
                act_e.wait_ge(nfk_mm, h + 1)
                a.activation(nfk[:, h, :], bank[6 + h % 2][:, :], ACT.Copy).then_inc(nfk_ready, 1)
            gate_loop("b_gate2")
            attend(len(UNITS))
            evac_loop(8 + 8, None)
            act_e.wait_ge(x_ready, 4)
            for c in range(KT):
                square(xT[:, c, :])
            root(bank[4][:, :])
            act_e.wait_ge(pads_ready, 1)
            n0 = npan[0]
            act_e.wait_ge(out_free, n0)

            def up_step(i, first):
                for s in range(RING):
                    act_e.wait_ge(panel_done, i * RING + (n0 + s + 1))
                    if not first:
                        act_e.wait_ge(up_conv, i * RING + (s + 1 - RING))
                    a.activation(uppad[:, s, 2:S + 2], bank[s][:, :], ACT.Copy).then_inc(out_free, 1)
                    upper(s, i * 32 + 16 * ((n0 + RING + s) // RAW + 1), i * RING + (n0 + s + 1))
                for s in (0, 2):
                    act_e.wait_ge(up_conv, i * RING + (s + 1))
                    a.activation(upc[s], upc[s], ACT.Silu).then_inc(up_silu, 1)

            up_step(0, True)
            with act_e.Fori(1, 2 * FT // RING) as i:
                up_step(i, False)
            npan[0] += 2 * FT
            nup[0] += 2 * FT
            evac_loop((FT - RING) // RING * RING, None)
            uppers(NPANEL - nup[0])
            act_e.wait_ge(x_ready, 5)
            for c in range(KT):
                square(xT[:, c, :])
            root(bank[4][:, :])

        @block.tensor
        def _(pe):
            mm = nc.tensor.matmul
            npan = [0]
            nsq = [0]

            def mm3(bk, w_hi, w_lo, x_hi, x_lo, start, stop, **kw):
                mm(bk, w_hi, x_hi, start=start, stop=False, **kw)
                mm(bk, w_hi, x_lo, start=False, stop=False, **kw)
                return mm(bk, w_lo, x_hi, start=False, stop=stop, **kw)

            def sum_square(bk, weights, first, last):
                pe.wait_ge(sq_ready, nsq[0] + 1)
                mm(bk, weights[:, :], sq[:, nsq[0] % 2, :], start=first, stop=last).then_inc(sq_used, 1)
                nsq[0] += 1

            def norm():
                for c in range(KT):
                    sum_square(bank[4][:, :], mean_d, c == 0, c == KT - 1)

            def gemm_loop(n_panels):
                n0 = npan[0]

                def body(i):
                    for s in range(RING):
                        if n0:
                            pe.wait_ge(out_free, i * RING + (n0 + s + 1 - RING))
                        pe.wait_ge(lo_ready, i * RING + (n0 + s + 1))
                        for kt in range(KT):
                            k = slice(kt * P, (kt + 1) * P)
                            last = mm3(bank[s][:, :], wH[:, s, k], wL[:, s, k], hH[:, kt, :], hL[:, kt, :],
                                       kt == 0, kt == KT - 1)
                        last.then_inc(panel_done, 1)

                if n_panels == RING:
                    body(0)
                else:
                    with pe.Fori(0, n_panels // RING) as i:
                        body(i)
                npan[0] += n_panels

            def values():
                n0 = npan[0]
                pe.wait_ge(out_free, n0)
                for s in range(RING):
                    pe.wait_ge(lo_ready, n0 + s + 1)
                    for half in range(2):
                        kt = 2 * s + half
                        for tb in range(TB):
                            t, k = slice(tb * P, (tb + 1) * P), slice(half * 512, (half + 1) * 512)
                            last = mm3(bank[tb][:, :], hH[:, kt, t], hL[:, kt, t], wH[:, s, k], wL[:, s, k],
                                       kt == 0, kt == KT - 1, skip_group_check=True)
                    last.then_inc(panel_done, 1)
                npan[0] += 4

            def mix(a_hi, a_lo, b_hi, b_lo):
                n0 = npan[0]
                for n in range(8):
                    s = n % RING
                    pe.wait_ge(out_free, n0 if n < 2 else n0 + n - 1)
                    pe.wait_ge(lo_ready, n0 + n + 1)
                    for kt in range(KT):
                        hi, lo = (a_hi, a_lo) if kt < CT else (b_hi, b_lo)
                        k, c = slice(kt * P, (kt + 1) * P), kt % CT
                        last = mm3(bank[2 * (n % 2) + kt // CT][:, :], wH[:, s, k], wL[:, s, k],
                                   hi[:, c, :], lo[:, c, :], c == 0, c == CT - 1)
                    last.then_inc(panel_done, 1)
                npan[0] += 8

            def attend(qT, q0, k0, first):
                m = len(UNITS)
                for i in range(m + 2):
                    if i < m:
                        qb, h = UNITS[i]
                        n, r = P * (qb + 1), 64 * (h % 2)
                        if first + i >= 2:
                            pe.wait_ge(lg_done, first + i - 1)
                        mm(bank[4 + i % 2][:, 0:n], qT[r:r + 64, q0 + h // 2, qb * P:(qb + 1) * P],
                           qT[r:r + 64, k0 + h // 2, 0:n], start=True, stop=True).then_inc(lg_ready, 1)
                    if 1 <= i <= m:
                        j = i - 1
                        qb, h = UNITS[j]
                        pe.wait_ge(prob_ready, first + j + 1)
                        if first + j >= 2:
                            pe.wait_ge(pT_ready, first + j - 1)
                        for c in range(qb + 1):
                            last = nc.tensor.transpose(bank[6 + j % 2][:, c * P:(c + 1) * P],
                                                       ex[:, j % 2, c * P:(c + 1) * P], ident[:, :])
                        last.then_inc(tr_ready, 1)
                    if i >= 2:
                        j = i - 2
                        qb, h = UNITS[j]
                        pe.wait_ge(pT_ready, first + j + 1)
                        if first + j >= 2:
                            pe.wait_ge(pv_used, first + j - 1)
                        for c in range(qb + 1):
                            last = mm(bank[j % 2][:, 0:P], vtok[:, c, (h // 2) * P:(h // 2 + 1) * P],
                                      pT[:, j % 2, c * P:(c + 1) * P], start=(c == 0), stop=(c == qb))
                        last.then_inc(pv_ready, 1)

            pe.wait_ge(small_in, 80)
            for j in range(2):
                last = mm(bank[6 + j][0:H, 0:320], relb[:, :], onehot[:, j * 320:(j + 1) * 320], start=True, stop=True)
            last.then_inc(rel_ready, 1)
            pe.wait_ge(const_ready, 1)
            norm()
            pe.wait_ge(h_ready, 1)
            gemm_loop(4)
            for kt in range(KT):
                for part in (hH, hL):
                    last = mm(bank[4][:, :], wki2[:, kt, :], part[:, kt, :].bitcast(f32),
                              start=(kt == 0 and part is hH), stop=(kt == KT - 1 and part is hL))
            last.then_inc(ki_ready, 1)
            for tb in range(TB):
                for kt in range(KT):
                    for part in (hH, hL):
                        last = mm(bank[5][:, tb * H:(tb + 1) * H], part[:, kt, tb * P:(tb + 1) * P].bitcast(f32),
                                  wwi[:, kt * H:(kt + 1) * H], start=(kt == 0 and part is hH),
                                  stop=(kt == KT - 1 and part is hL))
            last.then_inc(ki_ready, 1)
            pe.wait_ge(ki_copied, 2)
            pe.wait_ge(out_free, 4)
            for j in range(3 * H):
                qb, h = j // H + 1, j % H
                r = 64 * (h % 2)
                if j >= 2:
                    pe.wait_ge(relu_ready, j - 1)
                mm(bank[4 + j % 2][:, 0:P * (qb + 1)], qkiT[r:r + 64, h // 2, qb * P:(qb + 1) * P],
                   kiT[r:r + 64, 0:P * (qb + 1)], start=True, stop=True).then_inc(dot_ready, 1)
            gemm_loop(8)
            values()
            gemm_loop(8)
            pe.wait_ge(relu_ready, 3 * H)
            for c in range(8):
                if c >= 2:
                    pe.wait_ge(rt_ready, c)
                sum_square(bank[4 + c % 2][:, :], mean_h, True, True)
            gemm_loop(16)
            pe.wait_ge(qk_ready, 8)
            pe.wait_ge(out_free, npan[0])
            attend(qkiT, 4, 8, 0)
            pe.wait_ge(cv, CT * TAPS)
            for c in range(CT):
                last = mm(bank[4][:, :], mean_c[:, :], ybr[:, c, :], start=(c == 0), stop=(c == CT - 1))
            last.then_inc(cm_ready, 1)
            for c in range(CT):
                pe.wait_ge(csq_ready, c + 1)
                mm(bank[5][:, :], mean_c[:, :], sq[:, c % 2, :], start=(c == 0), stop=(c == CT - 1)).then_inc(cvar_ready, 1)
            pe.wait_ge(br_split, 1)
            mix(oH, oL, yH, yL)
            pe.wait_ge(mixed_ready, 1)
            gemm_loop(8)
            norm()
            pe.wait_ge(h_ready, 2)
            gemm_loop(16)
            for j in range(TB * 2):
                if j >= 2:
                    pe.wait_ge(htok_ready, j - 1)
                for c in range(4):
                    for part in (hH, hL):
                        last = mm(bank[6 + j % 2][:, c * P:(c + 1) * P],
                                  part[:, (j % 2) * 4 + c, (j // 2) * P:(j // 2 + 1) * P].bitcast(f32), ident[:, :],
                                  start=(part is hH), stop=(part is hL))
                last.then_inc(htok_tr, 1)
            pe.wait_ge(out_free, npan[0])
            pe.wait_ge(peer_in, 16)

            def key_scores(tb):
                for q4 in range(4):
                    if tb * 4 + q4 >= 2:
                        pe.wait_ge(sc_ready, tb * 4 + q4 - 1)
                    for c in range(4):
                        hc = q4 * 4 + c
                        last = mm(bank[4 + q4 % 2][:, c * P:(c + 1) * P], qpT[:, hc, tb * P:(tb + 1) * P],
                                  subk[:, hc, :], start=True, stop=True)
                    last.then_inc(sc_mm, 1)

            key_scores(0)
            for tb in range(TB):
                if tb + 1 < TB:
                    key_scores(tb + 1)
                for j in range(2):
                    pe.wait_ge(acc_ready, tb + 1)
                    if tb >= 1:
                        pe.wait_ge(acc_used, 2 * (tb - 1) + j + 1)
                    for c in range(4):
                        last = nc.tensor.transpose(bank[6 + j][:, c * P:(c + 1) * P],
                                                   acc[:, (4 * j + c) * P:(4 * j + c + 1) * P], ident[:, :])
                    last.then_inc(acc_tr, 1)
            norm()
            pe.wait_ge(h_ready, 3)
            pe.wait_ge(ple_in, 32)
            n0 = npan[0]
            for n in range(8):
                s = n % RING
                pe.wait_ge(out_free, n0 if n < 2 else n0 + n - 1)
                pe.wait_ge(lo_ready, n0 + n + 1)
                for kt in range(2):
                    mm(bank[2 * (n % 2) + 1][:, :], wpp[:, kt, n * P:(n + 1) * P], pT_in[:, kt, :],
                       start=(kt == 0), stop=(kt == 1))
                for kt in range(KT):
                    k = slice(kt * P, (kt + 1) * P)
                    last = mm3(bank[2 * (n % 2)][:, :], wH[:, s, k], wL[:, s, k], hH[:, kt, :], hL[:, kt, :],
                               kt == 0, kt == KT - 1)
                last.then_inc(panel_done, 1)
            npan[0] += 8
            norm()
            pe.wait_ge(h_ready, 4)
            gemm_loop(12)
            pe.wait_ge(two_in, 16)
            for tb in range(TB):
                for kt in range(KT):
                    for part in (hH, hL):
                        last = mm(bank[4][:, tb * H:(tb + 1) * H], part[:, kt, tb * P:(tb + 1) * P].bitcast(f32),
                                  wf[:, kt * H:(kt + 1) * H], start=(kt == 0 and part is hH),
                                  stop=(kt == KT - 1 and part is hL))
            last.then_inc(f_ready, 1)
            gemm_loop(8)
            values()
            pe.wait_ge(logf_ready, 1)
            pe.wait_ge(two_const, 1)
            for tc in range(TB):
                last = mm(bank[5][0:H, :], z[:, 2, tc * H:(tc + 1) * H], tri[:, tc, :], start=(tc == 0), stop=(tc == TB - 1))
            last.then_inc(fT_mm, 1)
            for qb in range(TB):
                for tc in range(TB):
                    last = mm(bank[4][:, qb * H:(qb + 1) * H], tri[:, tc, qb * P:(qb + 1) * P],
                              z[:, 2, tc * H:(tc + 1) * H], start=(tc == 0), stop=(tc == TB - 1))
            last.then_inc(fT_mm, 1)
            pe.wait_ge(fT_ready, 2)
            for h in range(H):
                if h >= 2:
                    pe.wait_ge(nfk_ready, h - 1)
                mm(bank[6 + h % 2][:, :], negsel[:, h, :], fT[:, :], start=True, stop=True).then_inc(nfk_mm, 1)
            gemm_loop(16)
            pe.wait_ge(nfk_ready, H)
            pe.wait_ge(out_free, npan[0])
            attend(qk2T, 0, 4, len(UNITS))
            pe.wait_ge(br_split, 2)
            mix(yH, yL, oH, oL)
            pe.wait_ge(mixed_ready, 2)
            gemm_loop(8)
            norm()
            pe.wait_ge(h_ready, 5)
            gemm_loop(2 * FT)
            n0 = npan[0]
            pe.wait_ge(out_free, n0)
            pe.wait_ge(act_ready, FT)

            def down(s, count, hi, lo, first, last_tile):
                pe.wait_ge(lo_ready, count)
                for nt in range(KT):
                    k = slice(nt * P, (nt + 1) * P)
                    last = mm3(bank[nt][:, :], wH[:, s, k], wL[:, s, k], hi, lo, first, last_tile,
                               skip_group_check=True)
                last.then_inc(panel_done, 1)

            for kt in range(RING):
                down(kt, n0 + kt + 1, actH[:, kt, :], actL[:, kt, :], kt == 0, False)
            with pe.Fori(1, FT // RING) as i:
                for s in range(RING):
                    down(s, i * RING + (n0 + s + 1), actH[:, ds(i * RING + s, 1), :], actL[:, ds(i * RING + s, 1), :],
                         False, False)
            for kt in range(FT // RING * RING, FT):
                down(kt % RING, n0 + kt + 1, actH[:, kt, :], actL[:, kt, :], False, kt == FT - 1)
            norm()

        @block.vector
        def _(dve):
            v = nc.vector
            step = Steps(dve, dve_step)
            npan = [0]
            nrt = [0]

            def split(hi, lo, x):
                step(v.tensor_copy(hi, x))
                return v.tensor_tensor(lo, x, hi.bitcast(f32), ALU.subtract)

            def norm_rs():
                dve.wait_ge(rt_ready, nrt[0] + 1)
                v.reciprocal(rs[:, :], rt[:, nrt[0] % 2, :]).then_inc(rt_used, 1)
                nrt[0] += 1
                dve.wait_ge(rt_used, nrt[0])

            def norm(k):
                norm_rs()
                for c in range(KT):
                    if k == 5:
                        last = v.scalar_tensor_tensor(xT[:, c, :], xT[:, c, :], V(NORMS[k], c), rs[:, :],
                                                      ALU.mult, ALU.mult)
                    else:
                        step(v.scalar_tensor_tensor(sq[:, c % 2, :], xT[:, c, :], V(NORMS[k], c), rs[:, :],
                                                    ALU.mult, ALU.mult))
                        last = split(hH[:, c, :], hL[:, c, :], sq[:, c % 2, :])
                return last

            def mix_evac():
                for n in range(8):
                    dve.wait_ge(panel_done, npan[0] + 1)
                    step(v.tensor_tensor(rs[:, :], bank[2 * (n % 2) + 1][:, :], gates[:, 8 + n, :], ALU.mult))
                    m = sq[:, n % 2, :]
                    v.tensor_tensor(m, bank[2 * (n % 2)][:, :], gates[:, n, :], ALU.mult).then_inc(out_free, 1)
                    npan[0] += 1
                    dve.wait_ge(out_free, npan[0])
                    step(v.tensor_tensor(m, m, rs[:, :], ALU.add))
                    step(split(hH[:, n, :], hL[:, n, :], m))
                dve.sem_inc(mixed_ready, 1)

            def add_to_x():
                n0 = npan[0]
                with dve.Fori(0, KT // RING) as i:
                    for s in range(RING):
                        dve.wait_ge(panel_done, i * RING + (n0 + s + 1))
                        x = xT[:, ds(i * RING + s, 1), :]
                        v.tensor_tensor(x, x, bank[s][:, :].rearrange("p (a n) -> p a n", a=1), ALU.add)\
                         .then_inc(out_free, 1)
                npan[0] += KT
                dve.wait_ge(out_free, npan[0])
                dve.sem_inc(x_ready, 1)

            def attend(first, logits):
                m = len(UNITS)
                for i in range(m + 2):
                    if i < m:
                        qb, h = UNITS[i]
                        n = P * (qb + 1)
                        dve.wait_ge(lg_ready, first + i + 1)
                        if i >= 2:
                            dve.wait_ge(ex_ready, first + i - 1)
                        logits(i, qb, h, n)
                    if 1 <= i <= m:
                        j = i - 1
                        dve.wait_ge(ex_ready, first + j + 1)
                        if first + j >= 4:
                            dve.wait_ge(prob_ready, first + j - 3)
                        v.reciprocal(rsum[:, j % 4:j % 4 + 1], esum[:, j % 4:j % 4 + 1]).then_inc(rsum_ready, 1)
                    if i >= 2:
                        j = i - 2
                        qb, h = UNITS[j]
                        r = 64 * (h % 2)
                        dve.wait_ge(pv_ready, first + j + 1)
                        v.tensor_copy(oT[r:r + 64, h // 2, qb * P:(qb + 1) * P], bank[j % 2][r:r + 64, 0:P])\
                         .then_inc(pv_used, 1)

            dve.wait_ge(vec_in, 16)
            dve.wait_ge(x_in, 32)
            norm(0).then_inc(h_ready, 1)
            dve.wait_ge(ki_copied, 2)
            j = 0
            for qb in range(1, TB):
                n = P * (qb + 1)
                score = scores[:, qb - 1, 0:n]
                for h in range(H):
                    dve.wait_ge(relu_ready, j + 1)
                    w = wi[:, qb * H + h:qb * H + h + 1]
                    if h == 0:
                        v.tensor_scalar(score, lg[:, j % 2, 0:n], w, None, ALU.mult).then_inc(relu_used, 1)
                    else:
                        v.scalar_tensor_tensor(score, lg[:, j % 2, 0:n], w, score, ALU.mult, ALU.add)\
                         .then_inc(relu_used, 1)
                    j += 1
                    dve.wait_ge(relu_used, j)
                step(v.memset(score[0:64, n - 64:n], MASKED))
            blocks = [(qb, scores[:, qb - 1, 0:P * (qb + 1)], top8[:, 8 * qb:8 * qb + 8]) for qb in range(1, TB)]
            for rnd in range(TOPK // 8):
                for qb, score, best in blocks:
                    last = v.max(out=best, in_=score)
                step(last)
                for qb, score, best in blocks:
                    last = v.match_replace(out=score, in_to_replace=best, in_values=score, imm_value=TAKEN)
                step(last)
            for qb, score, best in blocks:
                last = v.tensor_scalar(mask[:, MOFF[qb]:MOFF[qb] + P * (qb + 1)], score, TAKEN / 2, MASKED,
                                       ALU.is_gt, ALU.mult)
            step(last)
            npan[0] += 4 + 8 + 4
            for c in range(CT):
                dve.wait_ge(u_sig, c + 1)
                npan[0] += 2
                v.tensor_tensor(upad[:, c, TAPS - 1:TAPS - 1 + S], bank[(2 * c) % 4][:, :], lg[:, c % 2, :], ALU.mult)\
                 .then_inc(out_free, 2)
            npan[0] += 16
            for c in range(8):
                norm_rs()
                dve.wait_ge(out_free, 12)
                step(v.scalar_tensor_tensor(qkiT[:, 4 + c, :], qkiT[:, 4 + c, :], V("q_g" if c < 4 else "k_g"), rs[:, :],
                                            ALU.mult, ALU.mult))
                dve.sem_inc(qk_ready, 1)
            dve.wait_ge(out_free, FIRST["gates"])
            dve.wait_ge(const_ready, 1)
            for k in range(TAPS):
                for c in range(CT):
                    w = V("conv_w", c * TAPS + k)
                    src = upad[:, c, k:k + S]
                    if k == 0:
                        v.tensor_scalar(ybr[:, c, :], src, w, V("conv_b", c), ALU.mult, ALU.add).then_inc(cv, 1)
                    else:
                        dve.wait_ge(cv, (k - 1) * CT + c + 1)
                        v.scalar_tensor_tensor(ybr[:, c, :], src, w, ybr[:, c, :], ALU.mult, ALU.add).then_inc(cv, 1)
            dve.wait_ge(rel_in, 16)
            dve.wait_ge(const_ready, 1)

            def logits_one(i, qb, h, n):
                step(v.scalar_tensor_tensor(lg[:, i % 2, 0:n], bank[4 + i % 2][:, 0:n], HD ** -0.5,
                                            bias[:, h, 0:n][:, ::-1], ALU.mult, ALU.add))
                step(v.tensor_tensor(lg[:, i % 2, 0:n], lg[:, i % 2, 0:n], mask[:, MOFF[qb]:MOFF[qb] + n], ALU.add))
                v.tensor_reduce(nmax[:, i % 4:i % 4 + 1], lg[:, i % 2, 0:n], axis=AX.X, op=ALU.max, negate=True)\
                 .then_inc(lg_done, 1)

            attend(0, logits_one)
            dve.wait_ge(cm_ready, 1)
            for c in range(CT):
                v.tensor_tensor(ybr[:, c, :], ybr[:, c, :], bank[4][:, :], ALU.subtract).then_inc(cx_ready, 1)
            dve.wait_ge(csd_ready, 1)
            step(v.reciprocal(rs[:, :], rt[:, 0, :]))
            for c in range(CT):
                v.tensor_tensor(ybr[:, c, :], ybr[:, c, :], rs[:, :], ALU.mult).then_inc(cn_ready, 1)
            dve.wait_ge(br_ready, CT)
            dve.wait_ge(pv_used, len(UNITS))
            step(split(yH[:, :, :], yL[:, :, :], ybr))
            step(split(oH[:, :, :], oL[:, :, :], oT[:, :, :]))
            dve.sem_inc(br_split, 1)
            mix_evac()
            add_to_x()
            norm(1).then_inc(h_ready, 1)
            npan[0] += 16
            dve.wait_ge(peer_free, 1)

            def route(tb):
                for hc in range(16):
                    half, col = hc // 8, (hc % 8) * P
                    src = sc[:, half, col:col + P]
                    dve.wait_ge(sc_ready, tb * 4 + hc // 4 + 1)
                    step(v.max(out=sv[:, hc, 0:8], in_=src))
                    v.max_index(out=si[:, hc, 0:8], in_max=sv[:, hc, 0:8], in_values=src)
                    step(v.match_replace(out=sc2[:, :], in_to_replace=sv[:, hc, 0:8], in_values=src, imm_value=TAKEN))
                    if hc % 8 == 7:
                        dve.sem_inc(sc_used, 1)
                    step(v.max(out=sv[:, hc, 8:16], in_=sc2[:, :]))
                    step(v.max_index(out=si[:, hc, 8:16], in_max=sv[:, hc, 8:16], in_values=sc2[:, :]))
                v.tensor_copy(sif[:, :, :], si[:, :, :])
                s4 = sv[:, :, :].rearrange("p (h c) k -> p h c k", c=2)
                step(v.tensor_tensor(cand[:, :, :].rearrange("p h (a b) -> p h a b", a=PK),
                                     s4[:, :, 0, :].unsqueeze(3).to_broadcast([P, PH, PK, PK]),
                                     s4[:, :, 1, :].unsqueeze(2).to_broadcast([P, PH, PK, PK]), ALU.add))
                for h in range(PH):
                    step(v.max(out=tops[:, h, 0:8], in_=cand[:, h, :]))
                    v.max_index(out=topj[:, h, 0:8], in_max=tops[:, h, 0:8], in_values=cand[:, h, :])
                    step(v.match_replace(out=cand2[:, :], in_to_replace=tops[:, h, 0:8], in_values=cand[:, h, :],
                                         imm_value=TAKEN))
                    step(v.max(out=tops[:, h, 8:16], in_=cand2[:, :]))
                    step(v.max_index(out=topj[:, h, 8:16], in_max=tops[:, h, 8:16], in_values=cand2[:, :]))
                gt = gate[:, tb % 2, :].rearrange("p (h k) -> p h k", h=PH)
                v.tensor_tensor(gt, tops[:, :, :], tops[:, :, 0:1].to_broadcast([P, PH, PK]), ALU.subtract)\
                 .then_inc(g_shift, 1)
                tj = topj[:, :, :].rearrange("p h k -> p (h k)")
                v.tensor_scalar(tja[:, 0, :], tj, 4, None, ALU.logical_shift_right)
                step(v.tensor_scalar(tja[:, 1, :], tj, 15, None, ALU.bitwise_and))
                step(v.tensor_copy(tjf[:, :, :], tja[:, :, :]))
                e4 = eqv[:, :, :].rearrange("p h (k a) -> p h k a", k=PK)
                i4 = sif[:, :, :].rearrange("p (h c) a -> p h c a", c=2)
                for c in range(2):
                    t3 = tjf[:, c, :].rearrange("p (h k) -> p h k", h=PH)
                    step(v.tensor_tensor(e4, t3.unsqueeze(3).to_broadcast([P, PH, PK, PK]),
                                         iota16[:, :].unsqueeze(1).unsqueeze(1).to_broadcast([P, PH, PK, PK]),
                                         ALU.is_equal))
                    step(v.tensor_tensor(e4, e4, i4[:, :, c, :].unsqueeze(2).to_broadcast([P, PH, PK, PK]), ALU.mult))
                    step(v.tensor_reduce(eij[:, c, :].rearrange("p (h k) -> p h k", h=PH), e4, axis=AX.X, op=ALU.add))
                step(v.scalar_tensor_tensor(eij[:, 0, :], eij[:, 0, :], 128.0, eij[:, 1, :], ALU.mult, ALU.add))
                step(v.tensor_copy(eidx[:, tb % 2, :], eij[:, 0, :]))
                dve.sem_inc(idx_ready, 1)
                dve.wait_ge(g_exp, tb + 1)
                step(v.tensor_reduce(gsum[:, 0, :], gt, axis=AX.X, op=ALU.add))
                step(v.reciprocal(gsum[:, 1, :], gsum[:, 0, :]))
                step(v.tensor_tensor(gt, gt, gsum[:, 1, :].unsqueeze(2).to_broadcast([P, PH, PK]), ALU.mult))

            ROUNDS = NSEL // 16

            def rows(turn, per, emit):
                base = step.n
                with dve.Fori(0, ROUNDS) as i:
                    step.n = i * per + base
                    for half in range(2):
                        emit(i, half, turn)
                step.n = base + ROUNDS * per

            def arrived(i, half, u, turn):
                dve.wait_ge(gathered[8 * half + u], i * 16 + 16 * (turn + 1))

            dve.wait_ge(htok_ready, 2 * TB)
            route(0)
            for tb in range(TB):
                def dot_rows(i, half, turn):
                    for u in range(8):
                        arrived(i, half, u, turn)
                        v.tensor_tensor_reduce(out=grows[:, 8 * half + u, :], in0=grows[:, 8 * half + u, :], in1=h2tok[:, tb, :], scale=1.0,
                                               scalar=0.0, op0=ALU.mult, op1=ALU.add,
                                               accum_out=dots8[:, half, u:u + 1]).then_inc(row_used, 1)
                    dve.wait_ge(row_used, i * 16 + (turn * 16 + 8 * (half + 1)))
                    step(v.tensor_copy(dots[:, ds(i * 16 + 8 * half, 8)], dots8[:, half, :]))

                rows(2 * tb * ROUNDS, 2, dot_rows)
                dve.sem_inc(dots_ready, 1)
                if tb + 1 < TB:
                    route(tb + 1)
                dve.wait_ge(gel_ready, tb + 1)
                v.memset(acc[:, :], 0.0)
                step(v.tensor_tensor(act[:, :], gel[:, :], gate[:, tb % 2, :], ALU.mult))

                def add_rows(i, half, turn):
                    step(v.tensor_copy(act8[:, half, :], act[:, ds(i * 16 + 8 * half, 8)]))
                    for u in range(8):
                        arrived(i, half, u, turn)
                        v.scalar_tensor_tensor(acc[:, :], grows[:, 8 * half + u, :], act8[:, half, u:u + 1], acc[:, :],
                                               ALU.mult, ALU.add).then_inc(row_used, 1)
                        dve.wait_ge(row_used, i * 16 + (turn * 16 + 8 * half + u + 1))

                rows((2 * tb + 1) * ROUNDS, 2, add_rows)
                dve.sem_inc(acc_ready, 1)
                for j in range(2):
                    dve.wait_ge(acc_tr, 2 * tb + j + 1)
                    x = xT[:, 4 * j:4 * j + 4, tb * P:(tb + 1) * P]
                    step(v.tensor_tensor(x, x, bank[6 + j][:, :].rearrange("p (c t) -> p c t", c=4), ALU.add))
                    dve.sem_inc(acc_used, 1)
            dve.sem_inc(x_ready, 1)
            norm(2).then_inc(h_ready, 1)
            for n in range(8):
                dve.wait_ge(sg_ready, n + 1)
                npan[0] += 1
                v.tensor_tensor(sg[:, n % 2, :], sg[:, n % 2, :], bank[2 * (n % 2) + 1][:, :], ALU.mult).then_inc(out_free, 1)
                dve.wait_ge(out_free, npan[0])
                step(v.tensor_tensor(xT[:, n, :], xT[:, n, :], sg[:, n % 2, :], ALU.add))
                dve.sem_inc(sg_used, 1)
            dve.sem_inc(x_ready, 1)
            norm(3).then_inc(h_ready, 1)
            npan[0] += 4
            dve.wait_ge(out_free, npan[0])
            dve.wait_ge(two_const, 1)
            for c in range(CT):
                dve.wait_ge(panel_done, npan[0] + 1)
                v.tensor_tensor(zpad[:, c, 2:S + 2], bank[c][:, :], ccT[:, c, :], ALU.mult).then_inc(out_free, 1)
                npan[0] += 1
                dve.wait_ge(out_free, npan[0])
                step(v.tensor_scalar(ybr2[:, c, :], zpad[:, c, 2:S + 2], V("conv_mix_w", c * 3 + 2), None, ALU.mult))
                for k in range(2):
                    step(v.scalar_tensor_tensor(ybr2[:, c, :], zpad[:, c, k:k + S], V("conv_mix_w", c * 3 + k),
                                                ybr2[:, c, :], ALU.mult, ALU.add))
            for c in range(CT):
                dve.wait_ge(panel_done, npan[0] + 1)
                v.tensor_tensor(ybr2[:, c, :], ybr2[:, c, :], bank[c][:, :], ALU.mult).then_inc(out_free, 1)
                npan[0] += 1
            dve.wait_ge(f_ready, 1)
            step(v.tensor_tensor(z[:, 0, :], bank[4][:, 0:TB * H], V("b_f", 0, TB * H), ALU.add))
            dve.sem_inc(z_ready, 1)
            step(v.tensor_scalar(z[:, 2, :], z[:, 0, :], 0.0, None, ALU.min))
            dve.wait_ge(sp_ready, 1)
            v.tensor_tensor(z[:, 2, :], z[:, 2, :], z[:, 1, :], ALU.subtract).then_inc(logf_ready, 1)
            dve.wait_ge(fT_mm, 2)
            v.tensor_copy(fq[:, :], bank[4][:, 0:TB * H]).then_inc(fT_ready, 1)
            dve.wait_ge(nfk_ready, H)
            dve.wait_ge(fT_ready, 2)
            npan[0] += 8 + 4 + 16

            def logits_two(i, qb, h, n):
                step(v.scalar_tensor_tensor(lg[:, i % 2, 0:n], bank[4 + i % 2][:, 0:n], fq[:, qb * H + h:qb * H + h + 1],
                                            nfk[:, h, 0:n], ALU.add, ALU.add))
                step(v.tensor_tensor(lg[:, i % 2, n - P:n], lg[:, i % 2, n - P:n], causal[:, :], ALU.add))
                v.tensor_reduce(nmax[:, i % 4:i % 4 + 1], lg[:, i % 2, 0:n], axis=AX.X, op=ALU.max, negate=True)\
                 .then_inc(lg_done, 1)

            attend(len(UNITS), logits_two)
            dve.wait_ge(pv_used, 2 * len(UNITS))
            dve.wait_ge(out_free, FIRST["q2"])
            step(split(yH[:, :, :], yL[:, :, :], ybr2[:, :, :]))
            step(split(oH[:, :, :], oL[:, :, :], oT[:, :, :]))
            dve.sem_inc(br_split, 1)
            mix_evac()
            add_to_x()
            norm(4).then_inc(h_ready, 1)
            n0 = npan[0]
            base = step.n
            with dve.Fori(0, 2 * FT // RING) as i:
                step.n = i * 10 + base
                for s in range(RING):
                    dve.wait_ge(out_free, i * RING + (n0 + s + 1))
                    step(v.tensor_scalar(upc[s], uppad[:, s, 2:S + 2], V("conv_ffn_w", i * 12 + (3 * s + 2)), None,
                                         ALU.mult))
                    step(v.scalar_tensor_tensor(upc[s], uppad[:, s, 0:S], V("conv_ffn_w", i * 12 + 3 * s),
                                                upc[s], ALU.mult, ALU.add))
                    v.scalar_tensor_tensor(upc[s], uppad[:, s, 1:S + 1], V("conv_ffn_w", i * 12 + (3 * s + 1)),
                                           upc[s], ALU.mult, ALU.add).then_inc(up_conv, 1)
                for s in (0, 2):
                    dve.wait_ge(up_conv, i * RING + (s + 2))
                    dve.wait_ge(up_silu, i * 2 + (s // 2 + 1))
                    step(v.tensor_tensor(upc[s], upc[s], upc[s + 1], ALU.mult))
                    tile = ds(i * 2 + s // 2, 1)
                    hi = actH[:, tile, :].rearrange("p a n -> p (a n)")
                    v.tensor_copy(hi, upc[s]).then_inc(act_hi, 1)
                    dve.wait_ge(act_hi, i * 2 + (s // 2 + 1))
                    v.tensor_tensor(actL[:, tile, :].rearrange("p a n -> p (a n)"), upc[s], hi.bitcast(f32), ALU.subtract)\
                     .then_inc(act_ready, 1)
                dve.wait_ge(act_ready, i * 2 + 2)
            step.n = base + 10 * (2 * FT // RING)
            npan[0] += 2 * FT + FT
            dve.wait_ge(panel_done, NPANEL)
            for nt in range(KT):
                step(v.tensor_tensor(xT[:, nt, :], xT[:, nt, :], bank[nt][:, :], ALU.add))
            dve.sem_inc(x_ready, 1)
            norm(5).then_inc(y_ready, 1)


def kernel(**inputs):
    import concourse.bacc as bacc
    from concourse.bass_utils import run_bass_kernel_spmd

    a = {k: np.asarray(v) for k, v in inputs.items()}

    def tiles(w):
        kt, n = w.shape[0] // P, w.shape[1] // P
        return w.reshape(kt, P, n, P).transpose(2, 1, 0, 3).reshape(n, P, kt * P)

    def values(w):
        return w.reshape(4, 2, P, 512).transpose(0, 2, 1, 3).reshape(4, P, 2 * 512)

    def pairs(x, y):
        return np.stack([x, y], 1).reshape(-1, *x.shape[1:])

    w1, w2 = a["w_in"][0], a["w_in_2"][0]
    wq, wk, wv, wqi, wki, wwi, wglu, wgates = np.split(w1, np.cumsum([512, 512, 512, 512, 64, 8, 1024]), axis=1)
    cb, cc, cin, q2, k2, v2, wf, gates2 = np.split(w2, np.cumsum([512, 512, 512, 512, 512, 512, 8]), axis=1)
    up = tiles(a["w_up_2"][0])
    panels = np.concatenate([
        tiles(wqi), tiles(wq), tiles(wk), values(wv), pairs(tiles(wglu[:, :512]), tiles(wglu[:, 512:])), tiles(wgates),
        tiles(np.concatenate([a["w_att_out"][0], a["w_conv_out"][0]], 0)), tiles(a["w_out"][0]),
        tiles(a["w_peer_q"][0]), tiles(a["w_ple_gate"][0]),
        tiles(cc), tiles(cin), tiles(cb), tiles(q2), tiles(k2), values(v2), tiles(gates2),
        tiles(np.concatenate([a["w_out_conv_2"][0], a["w_out_attn_2"][0]], 0)), tiles(a["w_o_2"][0]),
        pairs(up[:FT], up[FT:]), a["w_down_2"][0].reshape(FT, P, D)], 0)

    def col(v):
        v = v.reshape(-1, P, *v.shape[1:])
        return np.moveaxis(v, 1, 0).reshape(P, -1)

    ffn_w = col(a["conv_ffn_w_2"][0].T).reshape(P, 2, FT, 3).transpose(0, 2, 1, 3).reshape(P, -1)
    vecs = np.concatenate([
        col(a["attn_norm_g"][0]), col(a["b_gate"][0]), np.tile(a["q_norm_g"][0], 2)[:, None],
        np.tile(a["k_norm_g"][0], 2)[:, None], col(a["conv_w"][0, :, 0, :].T), col(a["conv_b"][0]),
        col(a["conv_ln_g"][0]), col(a["conv_ln_b"][0]), col(a["ffn_norm_g"][0]), col(a["ple_norm_g"][0]),
        col(a["norm_mix_g_2"][0]), col(a["b_gate_2"][0]), col(a["conv_mix_w_2"][0].T), col(a["norm_ffn_g_2"][0]),
        ffn_w, col(a["norm_f_g_2"]), np.tile(a["b_f_2"][0], (P, TB))], 1)

    rel = P - np.arange(REL)
    n = np.abs(rel)
    large = 8 + (np.log(np.maximum(n, 1).astype(np.float32) / np.float32(8)) / np.float32(np.log(1024 / 8)) * 8).astype(np.int32)
    bucket = np.where(rel > 0, 16, 0) + np.where(n < 8, n, np.minimum(large, 15))
    onehot = (bucket[None, :] == np.arange(32)[:, None]).astype(np.float32)

    args = dict(
        xT=np.ascontiguousarray(a["x"][0].T.reshape(KT, P, S).transpose(1, 0, 2)),
        pT=np.ascontiguousarray(a["p"][0, 0].T.reshape(2, P, S).transpose(1, 0, 2)),
        panels=panels, vecs=vecs,
        wki=np.ascontiguousarray(wki.reshape(KT, P, 64).transpose(1, 0, 2).reshape(P, -1)),
        wwi=np.ascontiguousarray(wwi.reshape(KT, P, H).transpose(1, 0, 2).reshape(P, -1)),
        wf=np.ascontiguousarray(wf.reshape(KT, P, H).transpose(1, 0, 2).reshape(P, -1)),
        wpp=np.ascontiguousarray(a["w_ple_proj"][0].reshape(2, P, D).transpose(1, 0, 2)),
        subk=np.ascontiguousarray(a["peer_sub_keys"][0].transpose(3, 0, 1, 2).reshape(P, 16, P)),
        relb=a["rel_bias"], onehot=onehot, peer_u=a["peer_u"][0], peer_v=a["peer_v"][0])
    args = {k: np.ascontiguousarray(v) for k, v in args.items()}
    nc = bacc.Bacc("TRN2", target_bir_lowering=False, num_devices=1)
    aps = [nc.dram_tensor("in_" + k, v.shape, mybir.dt.float32, kind="ExternalInput").ap() for k, v in args.items()]
    out = nc.dram_tensor("y", (P, KT, S), mybir.dt.float32, kind="ExternalOutput").ap()
    build(nc, *aps, out)
    r = run_bass_kernel_spmd(nc, [{"in_" + k: v for k, v in args.items()}], core_ids=[0])
    y = r.results[0]["y"]
    return y.transpose(1, 0, 2).reshape(D, S).T.reshape(1, S, D)
```

```python
import numpy as np
import concourse.bass as bass
from concourse import mybir
from contextlib import ExitStack

P = 128
S, D = 512, 1024
TB = S // P
KT = D // P
H, HD = 8, 64
TOPK = 128
CT = 4
TAPS = 31
PH, PK = 8, 16
NSEL = PH * PK
NEXP = 128
GT = 32
GV = NEXP // 4
UCUT = [20, 20, 20, 20]
UMID = 8
ULAST = 8
FT = 22
EPS = 1e-6
MASKED = -1.0e30
TAKEN = -3.0e38
REL = 640

STREAM = [("qi", 4), ("q", 4), ("k", 4), ("v", 4), ("glu", 8), ("gates", 16), ("mix", 8), ("w_out", 8),
          ("peer_q", 16), ("peer_u", NEXP), ("peer_v", NEXP), ("ple_gate", 8),
          ("cc", 4), ("cin", 4), ("cb", 4), ("q2", 4), ("k2", 4), ("v2", 4), ("gates2", 16), ("mix2", 8),
          ("w_o", 8), ("up", 2 * FT), ("down", FT)]
FIRST = {}
NPANEL = 0
for _name, _n in STREAM:
    FIRST[_name] = NPANEL
    NPANEL += _n
RING = 4
RAW = 2

VEC = [("attn_g", 8), ("b_gate", 16), ("q_g", 1), ("k_g", 1), ("conv_w", CT * TAPS), ("conv_b", CT), ("ln_g", CT),
       ("ln_b", CT), ("ffn_g", 8), ("ple_g", 8), ("mix_g2", 8), ("b_gate2", 16), ("conv_mix_w", CT * 3),
       ("ffn_g2", 8), ("conv_ffn_w", 2 * FT * 3), ("norm_f_g", 8), ("b_f", 8 * TB)]
VCOL = {}
NVEC = 0
for _name, _n in VEC:
    VCOL[_name] = NVEC
    NVEC += _n




def build(nc, xT_d, pT_d, panels_d, vecs_d, wki_d, wwi_d, wf_d, wpp_d, subk_d, relb_d, onehot_d, out_d):
    f32 = mybir.dt.float32
    u32 = mybir.dt.uint32
    f32r = mybir.dt.float32r
    ALU = mybir.AluOpType
    ACT = mybir.ActivationFunctionType
    AX = mybir.AxisListType
    ds = bass.ds

    ctx = ExitStack()
    with ctx:
        def sem(name):
            return ctx.enter_context(nc.semaphore(name))

        def sb(name, shape, dt=f32, stack=ctx):
            return stack.enter_context(nc.sbuf_tensor(name, shape, dt))

        bank = [ctx.enter_context(nc.psum_tensor(f"bank{i}", [P, 512], f32)) for i in range(8)]
        rel_tab_d = nc.dram_tensor("rel_tab", (H, REL), f32)
        gelu_d = nc.dram_tensor("gelu_d", (GV, P, 4, S), f32).ap()
        gates_d = nc.dram_tensor("gates_d", (S // GT, P, P, GT), f32).ap()

        xT = sb("xT", [P, KT, S])
        ring = sb("ring", [P, RAW, D])
        vec = sb("vec", [P, NVEC])
        ident = sb("ident", [P, P])
        mean_d = sb("mean_d", [P, P])
        mean_h = sb("mean_h", [P, P])
        mean_c = sb("mean_c", [P, P])
        epsc = sb("epsc", [P, 1])
        sq = sb("sq", [P, 2, S])
        rt = sb("rt", [P, 2, S])
        rs = sb("rs", [P, S])

        ops = ExitStack()
        wH = sb("wH", [P, RING, D], f32r, stack=ops)
        wL = sb("wL", [P, RING, D], f32r, stack=ops)
        hH = sb("hH", [P, KT, S], f32r, stack=ops)
        hL = sb("hL", [P, KT, S], f32r, stack=ops)

        att = ExitStack()
        gates = sb("gates", [P, 16, S], stack=att)
        vtok = sb("vtok", [P, TB, 512], stack=att)
        oT = sb("oT", [P, CT, S], stack=att)
        lg = sb("lg", [P, 2, S], stack=att)
        pad = sb("pad", [P, CT, TAPS - 1 + S], stack=att)
        ex = sq
        pT = rt
        nmax = sb("nmax", [P, 4], stack=att)
        esum = sb("esum", [P, 4], stack=att)
        rsum = sb("rsum", [P, 4], stack=att)

        one = ExitStack()
        qkiT = sb("qkiT", [P, 12, S], stack=one)
        kiT = sq[:, 1, :]
        early = ExitStack()
        wki2 = sb("wki2", [P, KT, P], stack=early)
        wkiH, wkiL = (sb(n, [P, KT, P], f32r, stack=early) for n in ("wkiH", "wkiL"))
        wwi = sb("wwi", [P, KT * H], stack=early)
        wwiH, wwiL = (sb(n, [P, KT * H], f32r, stack=early) for n in ("wwiH", "wwiL"))
        early.close()
        bias = sb("bias", [P, H, S], stack=one)
        MOFF = [0, 128, 384, 768]
        mask = sb("mask", [P, 1280], stack=one)
        upad = pad
        ybr = qkiT[:, 0:4, :]
        scores = gates[:, 12:15, :]
        top8 = sb("top8", [P, 8 * TB], stack=one)
        onehot = rt[0:32, :, :].rearrange("p a b -> p (a b)")
        reltab = sq[0:8, :, :].rearrange("p a b -> p (a b)")
        relb = sb("relb", [32, H], stack=one)
        wi = sb("wi", [P, TB * H], stack=one)
        wiT = rt[0:H, 0, :]
        one.close()

        two = ExitStack()
        ccT = sb("ccT", [P, CT, S], stack=two)
        qk2T = sb("qk2T", [P, 8, S], stack=two)
        zpad = pad[:, :, TAPS - 3:]
        ybr2 = ccT
        wf = sb("wf", [P, KT * H], stack=two)
        wfH, wfL = (sb(n, [P, KT * H], f32r, stack=two) for n in ("wfH", "wfL"))
        zT = rs[0:H, :]
        tri = oT
        nfk = sb("nfk", [P, H, S], stack=two)
        fq = sb("fq", [P, TB * H], stack=two)
        fT = rs[0:H, :]
        negsel = lg[0:H, :, :].rearrange("p a (b n) -> p (a b) n", n=P)
        causal = sb("causal", [P, P], stack=two)
        z = sb("z", [P, 4, TB * H], stack=two)
        two.close()

        branch = ExitStack()
        oL, yH, yL, oH = (sb(n, [P, CT, S], f32r, stack=branch) for n in ("oL", "yH", "yL", "oH"))
        branch.close()
        att.close()
        ops.close()

        pe_ = ExitStack()
        sb("pe_below", [P, 16 * D], stack=pe_)
        qpT = sb("qpT", [P, 16, S], stack=pe_)
        spread = sb("spread", [P, 2, P, GT], stack=pe_)
        subk = sb("subk", [P, 16, P], stack=pe_)
        sc = sb("sc", [P, 2, D], stack=pe_)
        eqv = sc[:, :, :].rearrange("p a n -> p (a n)").rearrange("p (h n) -> p h n", h=PH)
        sv = sb("sv", [P, 16, PK], stack=pe_)
        si = sb("si", [P, 16, PK], u32, stack=pe_)
        sif = sb("sif", [P, 16, PK], stack=pe_)
        cand = sb("cand", [P, PH, PK * PK], stack=pe_)
        cand2 = sb("cand2", [P, PK * PK], stack=pe_)
        sc2 = cand2[:, 0:P]
        tops = sb("tops", [P, PH, PK], stack=pe_)
        topj = sb("topj", [P, PH, PK], u32, stack=pe_)
        tjf = sb("tjf", [P, 2, NSEL], stack=pe_)
        eij = sb("eij", [P, 2, NSEL], stack=pe_)
        tja = eij[:, :, :].bitcast(u32)
        iota16 = sb("iota16", [P, PK], stack=pe_)
        gsum = sb("gsum", [P, 2, PH], stack=pe_)
        gate = sb("gate", [P, NSEL], stack=pe_)
        chosen = sb("chosen", [P, 3, P], stack=pe_)
        iota = sb("iota", [P, P], stack=pe_)
        hot1 = sb("hot1", [P, 8, P], stack=pe_)
        hot2 = sb("hot2", [P, 8, P], stack=pe_)
        pe_.close()
        gelu = [sq[:, 0, :], sq[:, 1, :], rt[:, 0, :], rt[:, 1, :]]

        pv_ = ExitStack()
        sb("pv_below", [P, 16 * D], stack=pv_)
        gin = sb("gin", [P, 2, 4, S], stack=pv_)
        din = sb("din", [P, 2, S // GT, 4, GT], stack=pv_)
        wgtH = sb("wgtH", [P, 4, S], f32r, stack=pv_)
        wgtL = sb("wgtL", [P, 4, S], f32r, stack=pv_)
        pv_.close()
        pe_.close()

        ple = ExitStack()
        sb("ple_below", [P, 16 * D], stack=ple)
        pT_in = sb("pT_in", [P, 2, S], stack=ple)
        wpp = sb("wpp", [P, 2, D], stack=ple)
        sg = sb("sg", [P, 2, S], stack=ple)
        ple.close()

        ffn = ExitStack()
        sb("ffn_below", [P, 16 * D], stack=ffn)
        actH = sb("actH", [P, FT, S], f32r, stack=ffn)
        actL = sb("actL", [P, FT, S], f32r, stack=ffn)
        uppad = sb("uppad", [P, 4, S + 2], stack=ffn)
        upc = [sq[:, 0, :], sq[:, 1, :], rt[:, 0, :], rt[:, 1, :]]
        ffn.close()

        panel_in = [sem(f"panel_in{s}") for s in range(RAW)]
        hi_ready, lo_ready = sem("hi_ready"), sem("lo_ready")
        panel_done = sem("panel_done")
        out_free = sem("out_free")
        x_in, vec_in, small_in = sem("x_in"), sem("vec_in"), sem("small_in")
        peer_in, ple_in, two_in = sem("peer_in"), sem("ple_in"), sem("two_in")
        const_ready, two_const, pads_ready = sem("const_ready"), sem("two_const"), sem("pads_ready")
        small_ready, wf_ready = sem("small_ready"), sem("wf_ready")
        sq_ready, sq_used = sem("sq_ready"), sem("sq_used")
        rt_ready, rt_used = sem("rt_ready"), sem("rt_used")
        norm_ready, norm_hi = sem("norm_ready"), sem("norm_hi")
        h_ready = sem("h_ready")
        x_ready = sem("x_ready")
        ki_ready, ki_copied = sem("ki_ready"), sem("ki_copied")
        dot_ready, relu_ready, relu_used = sem("dot_ready"), sem("relu_ready"), sem("relu_used")
        qk_ready = sem("qk_ready")
        rel_ready, rel_copied, rel_out, rel_in = sem("rel_ready"), sem("rel_copied"), sem("rel_out"), sem("rel_in")
        lg_ready, lg_done, ex_ready = sem("lg_ready"), sem("lg_done"), sem("ex_ready")
        rsum_ready, prob_ready = sem("rsum_ready"), sem("prob_ready")
        tr_ready, pT_ready, pv_ready, pv_used = sem("tr_ready"), sem("pT_ready"), sem("pv_ready"), sem("pv_used")
        u_sig, cv = sem("u_sig"), sem("cv")
        cm_ready, cx_ready, csq_ready, cvar_ready, csd_ready, cn_ready = (sem(n) for n in (
            "cm_ready", "cx_ready", "csq_ready", "cvar_ready", "csd_ready", "cn_ready"))
        br_ready, br_split = sem("br_ready"), sem("br_split")
        gate_sig, mixed_ready = sem("gate_sig"), sem("mixed_ready")
        peer_free = sem("peer_free")
        sc_mm, sc_ready, sc_used = sem("sc_mm"), sem("sc_ready"), sem("sc_used")
        g_shift, g_exp = sem("g_shift"), sem("g_exp")
        keys_ready, keys_tr = sem("keys_ready"), sem("keys_tr")
        hot_ready, spread_mm, spread_copied = sem("hot_ready"), sem("spread_mm"), sem("spread_copied")
        spread_out = [sem(f"spread_out{b}") for b in range(2)]
        gelu_out = [sem(f"gelu_out{s}") for s in range(4)]
        pair_in = [sem(f"pair_in{b}") for b in range(2)]
        wgt_hi, wgt_ready = sem("wgt_hi"), sem("wgt_ready")
        sg_ready, sg_used = sem("sg_ready"), sem("sg_used")
        zT_ready = sem("zT_ready")
        f_ready, z_ready, sp_ready, logf_ready = sem("f_ready"), sem("z_ready"), sem("sp_ready"), sem("logf_ready")
        fT_mm, fT_ready, nfk_mm, nfk_ready = sem("fT_mm"), sem("fT_ready"), sem("nfk_mm"), sem("nfk_ready")
        up_conv, up_silu = sem("up_conv"), sem("up_silu")
        act_hi, act_ready = sem("act_hi"), sem("act_ready")
        y_tile, y_ready, out_done = sem("y_tile"), sem("y_ready"), sem("out_done")
        dve_step, act_step, pool_step = sem("dve_step"), sem("act_step"), sem("pool_step")

        class Steps:

            def __init__(self, eng, s):
                self.eng, self.sem, self.n = eng, s, 0

            def __call__(self, ins):
                ins.then_inc(self.sem, 1)
                self.n = self.n + 1
                self.eng.wait_ge(self.sem, self.n)

        def V(name, i=0, n=1):
            return vec[:, ds(VCOL[name] + i, n)] if not isinstance(i, int) else vec[:, VCOL[name] + i:VCOL[name] + i + n]

        NORMS = ["attn_g", "ffn_g", "ple_g", "mix_g2", "ffn_g2", "norm_f_g"]
        UNITS = [(qb, h) for qb in range(TB) for h in range(H)]

        block = ctx.enter_context(nc.Block())

        @block.sync
        def _(sp):
            sp.dma_start(xT[:, 0:4, :], xT_d[:, 0:4, :]).then_inc(x_in, 16)
            sp.dma_start(xT[:, 4:8, :], xT_d[:, 4:8, :]).then_inc(x_in, 16)
            for s in range(RAW):
                sp.dma_start(ring[:, s, :], panels_d[s, :, :]).then_inc(panel_in[s], 16)
            with sp.Fori(1, NPANEL // RAW) as i:
                for s in range(RAW):
                    sp.wait_ge(lo_ready, i * RAW + (s + 1 - RAW))
                    sp.dma_start(ring[:, s, :], panels_d[ds(i * RAW + s, 1), :, :].rearrange("a p n -> (a p) n"))\
                      .then_inc(panel_in[s], 16)
            sp.wait_ge(y_ready, 1)
            sp.dma_start(out_d[:, :, :], xT[:, :, :]).then_inc(out_done, 16)
            sp.wait_ge(out_done, 16)

        @block.gpsimd
        def _(pool):
            step = Steps(pool, pool_step)
            g = nc.gpsimd
            g.memset(epsc[:, :], EPS)
            g.memset(mean_d[:, :], 1.0 / D)
            g.memset(mean_c[:, :], 1.0 / 512)
            g.memset(mean_h[:, :], 0.0)
            g.memset(upad[:, :, 0:TAPS - 1], 0.0)
            step(g.memset(ident[:, :], 0.0))
            step(g.memset(mean_h[0:64, 0:64], 1.0 / HD))
            step(g.memset(mean_h[64:128, 64:128], 1.0 / HD))
            g.memset(mask[:, 0:P], 0.0)
            step(g.affine_select(out=ident[:, :], in_=ident[:, :], compare_op=ALU.not_equal, fill=1.0, base=0,
                                 pattern=[[-1, P]], channel_multiplier=1))
            g.memset(mask[0:64, 64:P], MASKED).then_inc(const_ready, 1)

            def rest(s, count):
                pool.wait_ge(hi_ready, count)
                g.tensor_tensor(wL[:, s, :], ring[:, s % RAW, :], wH[:, s, :].bitcast(f32), ALU.subtract).then_inc(lo_ready, 1)

            def probs(first):
                for i in range(len(UNITS)):
                    qb, h = UNITS[i]
                    n = P * (qb + 1)
                    pool.wait_ge(rsum_ready, first + i + 1)
                    g.tensor_scalar(ex[:, i % 2, 0:n], ex[:, i % 2, 0:n], rsum[:, i % 4:i % 4 + 1], None, ALU.mult)\
                     .then_inc(prob_ready, 1)
                    if i % 2:
                        rest(npan[0] % RING, npan[0] + 1)
                        npan[0] += 1

            npan = [0]

            def rests(m):
                n0 = npan[0]
                assert n0 % RING == 0
                if m >= RING:
                    with pool.Fori(0, m // RING) as i:
                        for s in range(RING):
                            rest(s, i * RING + (n0 + s + 1))
                for n in range(n0 + m // RING * RING, n0 + m):
                    rest(n % RING, n + 1)
                npan[0] += m

            rests(FIRST["gates"] + RING)
            probs(0)
            rests(FIRST["peer_q"] - npan[0])

            pool.wait_ge(x_ready, 1)
            step(g.iota(iota16[:, :], pattern=[[1, PK]], base=0, channel_multiplier=0,
                        allow_small_or_imprecise_dtypes=True))
            g.iota(iota[:, :], pattern=[[1, P]], base=0, channel_multiplier=0,
                   allow_small_or_imprecise_dtypes=True).then_inc(peer_free, 1)
            rests(FIRST["cc"] + RING - npan[0])
            pool.wait_ge(x_ready, 3)
            g.memset(tri[:, :, :], 1.0)
            g.memset(causal[:, :], 0.0)
            g.memset(zpad[:, :, 0:2], 0.0)
            step(g.memset(negsel[:, :, :], 0.0))
            g.affine_select(out=tri[:, :, :], in_=tri[:, :, :], compare_op=ALU.is_ge, fill=0.0, base=0,
                            pattern=[[-P, TB], [1, S]], channel_multiplier=-1)
            g.affine_select(out=causal[:, :], in_=causal[:, :], compare_op=ALU.is_ge, fill=MASKED, base=0,
                            pattern=[[-1, P]], channel_multiplier=1)
            g.affine_select(out=negsel[:, :, :], in_=negsel[:, :, :], compare_op=ALU.not_equal, fill=-1.0, base=0,
                            pattern=[[-1, H], [0, P]], channel_multiplier=1).then_inc(two_const, 1)
            rests(FIRST["gates2"] + RING - npan[0])
            probs(len(UNITS))
            rests(FIRST["up"] + RING - npan[0])
            pool.wait_ge(x_ready, 4)
            g.memset(uppad[:, :, 0:2], 0.0).then_inc(pads_ready, 1)
            rests(NPANEL - npan[0])

        @block.scalar
        def _(act_e):
            step = Steps(act_e, act_step)
            a = nc.scalar
            a.dma_start(vec[:, :], vecs_d).then_inc(vec_in, 16)
            wki_src = wki_d.rearrange("p (k n) -> p k n", k=KT)
            a.dma_start(wki2[:, :, 0:64], wki_src).then_inc(small_in, 16)
            a.dma_start(wki2[:, :, 64:P], wki_src).then_inc(small_in, 16)
            a.dma_start(wwi[:, :], wwi_d).then_inc(small_in, 16)
            a.dma_start(relb[:, :], relb_d).then_inc(small_in, 16)
            a.dma_start(onehot[:, 0:REL], onehot_d).then_inc(small_in, 16)
            nsq = [0]
            nms = [0]
            due = [8] + [8 + c + 1 for c in range(8)] + [16 + 8 * (k + 1) for k in range(5)]
            npan = [0]

            def square(src):
                if nsq[0] >= 2:
                    act_e.wait_ge(sq_used, nsq[0] - 1)
                a.activation(sq[:, nsq[0] % 2, :], src, ACT.Square).then_inc(sq_ready, 1)
                nsq[0] += 1

            def root(ps):
                act_e.wait_ge(sq_used, due[nms[0]])
                if nms[0] >= 2:
                    act_e.wait_ge(rt_used, nms[0] - 1)
                a.activation(rt[:, nms[0] % 2, :], ps, ACT.Sqrt, bias=epsc[:, :]).then_inc(rt_ready, 1)
                nms[0] += 1

            nhi = [0]

            def norm_end(split=True, bk=4):
                root(bank[bk][:, :])
                for c in range(KT if split else 0):
                    nhi[0] += 1
                    act_e.wait_ge(norm_ready, nhi[0])
                    a.activation(hH[:, c, :], sq[:, c % 2, :], ACT.Copy).then_inc(norm_hi, 1)

            def norm(tile_ready, split=True, bk=4):
                for c in range(KT):
                    tile_ready(c)
                    square(xT[:, c, :])
                norm_end(split, bk)

            def upper(s, loads, done):
                act_e.wait_ge(panel_in[s % RAW], loads)
                if done is not None:
                    act_e.wait_ge(panel_done, done)
                a.activation(wH[:, s, :], ring[:, s % RAW, :], ACT.Copy).then_inc(hi_ready, 1)

            def residual_norm():
                n0 = npan[0]
                for c in range(KT + 1):
                    if c < KT:
                        uppers(1)
                    if c >= 1:
                        act_e.wait_ge(out_free, n0 + c)
                        square(xT[:, c - 1, :])
                npan[0] += KT
                norm_end()

            nup = [0]

            def uppers(m):
                for n in range(nup[0], nup[0] + m):
                    upper(n % RING, 16 * (n // RAW + 1), n + 1 - RING if n >= RING else None)
                nup[0] += m

            def evac_loop(n_panels, emit, ahead=True):
                n0 = npan[0]
                if n0 and emit is not None:
                    act_e.wait_ge(out_free, n0)
                assert not ahead or nup[0] == n0 + RING
                with act_e.Fori(0, n_panels // RING) as i:
                    for s in range(RING):
                        if emit is not None:
                            act_e.wait_ge(panel_done, i * RING + (n0 + s + 1))
                            emit(i, s).then_inc(out_free, 1)
                        if ahead:
                            upper(s, i * 32 + 16 * ((n0 + RING + s) // RAW + 1), i * RING + (n0 + s + 1))
                npan[0] += n_panels
                if ahead:
                    nup[0] += n_panels

            act_e.wait_ge(const_ready, 1)
            act_e.wait_ge(vec_in, 16)
            act_e.wait_ge(rel_ready, 1)
            a.activation(reltab[:, 0:320], bank[6][0:8, 0:320], ACT.Copy)
            a.activation(reltab[:, 320:REL], bank[7][0:8, 0:320], ACT.Copy).then_inc(rel_copied, 1)
            act_e.wait_ge(rel_copied, 1)
            a.dma_start(rel_tab_d.ap(), reltab[:, 0:REL]).then_inc(rel_out, 16)
            act_e.wait_ge(rel_out, 16)
            act_e.wait_ge(x_in, 32)
            norm(lambda c: None)
            uppers(RING)
            evac_loop(4, lambda i, s: a.activation(qkiT[:, ds(i * RING + s, 1), :], bank[s][:, :], ACT.Copy))
            act_e.wait_ge(ki_ready, 1)
            a.activation(wiT, bank[5][0:H, :], ACT.Copy).then_inc(ki_copied, 1)
            act_e.wait_ge(ki_ready, 2)
            a.activation(kiT[:, :], bank[4][:, :], ACT.Copy).then_inc(ki_copied, 1)
            act_e.wait_ge(ki_ready, 3)
            a.mul(wi[:, :], bank[5][:, 0:TB * H], float(np.float32(HD ** -0.5 * H ** -0.5))).then_inc(ki_copied, 1)
            rel_ap = rel_tab_d.ap()
            diag = bass.AP(tensor=rel_ap.tensor, offset=1, ap=[[1, P], [REL, H], [1, S]])
            a.dma_start(bias[:, :, :], diag).then_inc(rel_in, 16)
            for j in range(3 * H):
                n = P * (j // H + 2)
                act_e.wait_ge(dot_ready, j + 1)
                if j >= 2:
                    act_e.wait_ge(relu_used, j - 1)
                a.activation(lg[:, j % 2, 0:n], bank[4 + j % 2][:, 0:n], ACT.Relu).then_inc(relu_ready, 1)
            evac_loop(8, lambda i, s: a.activation(qkiT[:, ds(i * RING + (s + 4), 1), :], bank[s][:, :], ACT.Copy))
            uppers(RING)
            act_e.wait_ge(panel_done, npan[0] + 4)
            for tb in range(TB):
                a.activation(vtok[:, tb, :], bank[tb][:, :], ACT.Copy).then_inc(out_free, 1)
            npan[0] += 4

            def sigmoids(bname):
                act_e.wait_ge(out_free, npan[0])
                for n in range(8):
                    for c in (n, 8 + n):
                        a.activation(gates[:, c, :], gates[:, c, :], ACT.Sigmoid, bias=V(bname, c)).then_inc(gate_sig, 1)

            act_e.wait_ge(relu_used, 3 * H)
            for c in range(CT):
                square(qkiT[:, 4 + 2 * c, :])
                square(qkiT[:, 5 + 2 * c, :])
                act_e.wait_ge(panel_done, npan[0] + 2)
                if c >= 2:
                    act_e.wait_ge(out_free, npan[0] - 2)
                a.activation(lg[:, c % 2, :], bank[(2 * c + 1) % 4][:, :], ACT.Sigmoid).then_inc(u_sig, 1)
                npan[0] += 2
                uppers(2)
                root(bank[4][:, :])
                root(bank[5][:, :])
            def attend(first):
                for i in range(len(UNITS) + 1):
                    if i < len(UNITS):
                        n = P * (UNITS[i][0] + 1)
                        act_e.wait_ge(lg_done, first + i + 1)
                        if i >= 2:
                            act_e.wait_ge(tr_ready, first + i - 1)
                        a.activation(ex[:, i % 2, 0:n], lg[:, i % 2, 0:n], ACT.Exp, bias=nmax[:, i % 4:i % 4 + 1],
                                     accum_out=esum[:, i % 4:i % 4 + 1]).then_inc(ex_ready, 1)
                    if i >= 1:
                        j = i - 1
                        n = P * (UNITS[j][0] + 1)
                        act_e.wait_ge(tr_ready, first + j + 1)
                        if j >= 2:
                            act_e.wait_ge(pv_ready, first + j - 1)
                        a.activation(pT[:, j % 2, 0:n], bank[6 + j % 2][:, 0:n], ACT.Copy).then_inc(pT_ready, 1)
                    if i >= 2 and i % 2 == 0:
                        act_e.wait_ge(panel_done, npan[0] + 1)
                        a.activation(gates[:, i // 2 - 1, :], bank[2 + (i // 2 - 1) % 2][:, :], ACT.Copy).then_inc(out_free, 1)
                        npan[0] += 1
                        uppers(1)

            attend(0)
            act_e.wait_ge(sq_used, nsq[0])
            for c in range(CT):
                act_e.wait_ge(cx_ready, c + 1)
                if c >= 2:
                    act_e.wait_ge(cvar_ready, c - 1)
                a.activation(sq[:, c % 2, :], ybr[:, c, :], ACT.Square).then_inc(csq_ready, 1)
            act_e.wait_ge(cvar_ready, CT)
            act_e.wait_ge(rt_used, nms[0])
            a.activation(rt[:, 0, :], bank[5][:, :], ACT.Sqrt, bias=epsc[:, :]).then_inc(csd_ready, 1)
            for c in range(CT):
                act_e.wait_ge(cn_ready, c + 1)
                a.activation(ybr[:, c, :], ybr[:, c, :], ACT.Silu, bias=V("ln_b", c), scale=V("ln_g", c))\
                 .then_inc(br_ready, 1)
            sigmoids("b_gate")
            evac_loop(8, None)
            residual_norm()
            act_e.wait_ge(peer_free, 1)
            a.dma_start(subk[:, :, :], subk_d).then_inc(peer_in, 16)
            evac_loop(16, lambda i, s: a.activation(qpT[:, ds(i * RING + s, 1), :], bank[s][:, :], ACT.Copy))

            def score_copies(tb):
                for q4 in range(4):
                    act_e.wait_ge(sc_mm, tb * 4 + q4 + 1)
                    if tb >= 1 and q4 == 0:
                        act_e.wait_ge(sc_used, tb)
                    a.activation(sc[:, q4 // 2, (q4 % 2) * 512:(q4 % 2) * 512 + 512], bank[4 + q4 % 2][:, :], ACT.Copy)\
                     .then_inc(sc_ready, 1)

            nu = [0]

            def gelu_panel(i, s, n0, u0, first):
                act_e.wait_ge(panel_done, i * RING + (n0 + s + 1))
                if not first:
                    act_e.wait_ge(gelu_out[s], i * 16 + 16 * (u0 // RING))
                a.activation(gelu[s], bank[s][:, :], ACT.Gelu_apprx_tanh).then_inc(out_free, 1)
                upper(s, i * 32 + 16 * ((n0 + RING + s) // RAW + 1), i * RING + (n0 + s + 1))
                act_e.wait_ge(out_free, i * RING + (n0 + s + 1))
                a.dma_start(gelu_d[ds(i + u0 // RING, 1), :, s, :].rearrange("a p n -> (a p) n"), gelu[s])\
                 .then_inc(gelu_out[s], 16)

            def counted(m):
                npan[0] += m
                nup[0] += m
                nu[0] += m

            def gelu_loop(m):
                n0, u0 = npan[0], nu[0]
                start = 0
                if u0 == 0:
                    for s in range(RING):
                        gelu_panel(0, s, n0, u0, True)
                    start = 1
                with act_e.Fori(start, m // RING) as i:
                    for s in range(RING):
                        gelu_panel(i, s, n0, u0, False)
                counted(m)

            def gate_exp(tb):
                act_e.wait_ge(g_shift, tb + 1)
                a.activation(gate[:, :], gate[:, :], ACT.Exp).then_inc(g_exp, 1)

            def spread_copies(tb):
                n0, u0, t0 = npan[0], nu[0], tb * P

                def body(i, first):
                    for j in range(8):
                        grp = j // 4
                        if j % 4 == 0 and not first:
                            act_e.wait_ge(spread_out[grp], i * 16 + 32 * tb)
                        for b in range(2):
                            at = 8 * (j % 4) + 4 * b
                            act_e.wait_ge(spread_mm, i * 64 + (t0 + 8 * j + 4 * b + 4))
                            a.activation(spread[:, grp, :, at:at + 4].rearrange("p k t -> p t k"),
                                         bank[6 + b][:, :].rearrange("p (t k) -> p t k", t=4), ACT.Copy)\
                             .then_inc(spread_copied, 1)
                        if j % 4 == 3:
                            act_e.wait_ge(spread_copied, i * 16 + (t0 // 4 + 2 * (j + 1)))
                            a.dma_start(gates_d[ds(i * 2 + (tb * (P // GT) + grp), 1), :, :, :]
                                        .rearrange("a p k t -> (a p) k t"), spread[:, grp, :, :])\
                             .then_inc(spread_out[grp], 16)
                        if j % 2:
                            gelu_panel(i, j // 2, n0, u0, False)

                if tb == 0:
                    body(0, True)
                    body(1, False)
                else:
                    with act_e.Fori(0, UMID // RING) as i:
                        body(i, False)
                counted(UMID)

            score_copies(0)
            for tb in range(TB):
                gelu_loop(UCUT[tb])
                gate_exp(tb)
                spread_copies(tb)
                if tb + 1 < TB:
                    score_copies(tb + 1)
            gelu_loop(NEXP - sum(UCUT) - TB * UMID - ULAST)

            def pair_load(grp, b):
                a.dma_start(gin[:, b, :, :], gelu_d[ds(grp, 1), :, :, :].rearrange("a p s n -> (a p) s n"))\
                 .then_inc(pair_in[b], 16)
                a.dma_start(din[:, b, :, :, :].rearrange("p g s t -> p g (s t)"),
                            gates_d.rearrange("g p k t -> p g (k t)")[:, :, ds(grp * (4 * GT), 4 * GT)])\
                 .then_inc(pair_in[b], 16)

            for b in range(2):
                act_e.wait_ge(spread_out[b], 16 * (S // GT // 2))
            for b in range(2):
                pair_load(b, b)
            gelu_loop(ULAST)
            for s in range(RING):
                act_e.wait_ge(gelu_out[s], 16 * GV)
            n0 = npan[0]

            def second_pass(i, more):
                for b in range(2):
                    for s in range(RING):
                        upper(s, i * 64 + 16 * ((n0 + 4 * b + RING + s) // RAW + 1), i * 8 + (n0 + 4 * b + s + 1))
                    if more:
                        act_e.wait_ge(wgt_ready, i * 8 + 4 * (b + 1))
                        pair_load(i * 2 + (2 + b), b)

            with act_e.Fori(0, GV // 2 - 1) as i:
                second_pass(i, True)
            second_pass(GV // 2 - 1, False)
            npan[0] += NEXP
            nup[0] += NEXP
            act_e.wait_ge(panel_done, npan[0])
            a.dma_start(pT_in[:, :, :], pT_d).then_inc(ple_in, 16)
            a.dma_start(wpp[:, :, :], wpp_d).then_inc(ple_in, 16)
            norm(lambda c: act_e.wait_ge(out_free, FIRST["peer_v"] + (c + 1) * (NEXP // KT)), bk=0)
            for c in range(KT):
                act_e.wait_ge(panel_done, npan[0] + 1)
                if c >= 2:
                    act_e.wait_ge(sg_used, c - 1)
                a.activation(sg[:, c % 2, :], bank[2 * (c % 2)][:, :], ACT.Sigmoid).then_inc(sg_ready, 1)
                npan[0] += 1
                uppers(1)

            a.dma_start(wf[:, :], wf_d).then_inc(two_in, 16)
            norm(lambda c: act_e.wait_ge(sg_used, c + 1))
            evac_loop(4, lambda i, s: a.activation(ccT[:, ds(i * RING + s, 1), :], bank[s][:, :], ACT.Copy))
            evac_loop(8, None)
            act_e.wait_ge(f_ready, 1)
            a.activation(zT, bank[4][0:H, :], ACT.Copy).then_inc(zT_ready, 1)
            act_e.wait_ge(z_ready, 1)
            step(a.activation(z[:, 1, :], z[:, 0, :], ACT.Abs))
            step(a.activation(z[:, 1, :], z[:, 1, :], ACT.Exp, scale=-1.0))
            a.activation(z[:, 1, :], z[:, 1, :], ACT.Ln, bias=1.0).then_inc(sp_ready, 1)
            evac_loop(4, lambda i, s: a.activation(qk2T[:, ds(i * RING + s, 1), :], bank[s][:, :], ACT.Copy,
                                                   scale=HD ** -0.5))
            evac_loop(4, lambda i, s: a.activation(qk2T[:, ds(i * RING + (s + 4), 1), :], bank[s][:, :], ACT.Copy))
            uppers(RING)
            act_e.wait_ge(panel_done, npan[0] + 4)
            for tb in range(TB):
                a.activation(vtok[:, tb, :], bank[tb][:, :], ACT.Copy).then_inc(out_free, 1)
            npan[0] += 4
            act_e.wait_ge(fT_mm, 1)
            a.activation(fT[:, :], bank[5][0:H, :], ACT.Copy).then_inc(fT_ready, 1)
            for h in range(H):
                act_e.wait_ge(nfk_mm, h + 1)
                a.activation(nfk[:, h, :], bank[6 + h % 2][:, :], ACT.Copy).then_inc(nfk_ready, 1)
            attend(len(UNITS))
            sigmoids("b_gate2")
            evac_loop(8, None)
            residual_norm()
            act_e.wait_ge(pads_ready, 1)
            n0 = npan[0]
            act_e.wait_ge(out_free, n0)

            def up_step(i, first):
                for s in range(RING):
                    act_e.wait_ge(panel_done, i * RING + (n0 + s + 1))
                    if not first:
                        act_e.wait_ge(up_conv, i * RING + (s + 1 - RING))
                    a.activation(uppad[:, s, 2:S + 2], bank[s][:, :], ACT.Copy).then_inc(out_free, 1)
                    upper(s, i * 32 + 16 * ((n0 + RING + s) // RAW + 1), i * RING + (n0 + s + 1))
                for s in (0, 2):
                    act_e.wait_ge(up_conv, i * RING + (s + 1))
                    a.activation(upc[s], upc[s], ACT.Silu).then_inc(up_silu, 1)

            up_step(0, True)
            with act_e.Fori(1, 2 * FT // RING) as i:
                up_step(i, False)
            npan[0] += 2 * FT
            nup[0] += 2 * FT
            evac_loop((FT - RING) // RING * RING, None)
            uppers(NPANEL - nup[0])
            norm(lambda c: act_e.wait_ge(y_tile, c + 1), split=False, bk=0)

        @block.tensor
        def _(pe):
            mm = nc.tensor.matmul
            npan = [0]
            nsq = [0]

            def mm3(bk, w_hi, w_lo, x_hi, x_lo, start, stop, **kw):
                mm(bk, w_hi, x_hi, start=start, stop=False, **kw)
                mm(bk, w_hi, x_lo, start=False, stop=False, **kw)
                return mm(bk, w_lo, x_hi, start=False, stop=stop, **kw)

            def sum_square(bk, weights, first, last):
                pe.wait_ge(sq_ready, nsq[0] + 1)
                mm(bk, weights[:, :], sq[:, nsq[0] % 2, :], start=first, stop=last).then_inc(sq_used, 1)
                nsq[0] += 1

            def norm(bk=4):
                for c in range(KT):
                    sum_square(bank[bk][:, :], mean_d, c == 0, c == KT - 1)

            def gemm_loop(n_panels, h_tiles=None):
                n0 = npan[0]

                def body(i, first=False):
                    for s in range(RING):
                        if n0:
                            pe.wait_ge(out_free, i * RING + (n0 + s + 1 - RING))
                        pe.wait_ge(lo_ready, i * RING + (n0 + s + 1))
                        for kt in range(KT):
                            if first and s == 0:
                                pe.wait_ge(h_ready, h_tiles + kt + 1)
                            k = slice(kt * P, (kt + 1) * P)
                            last = mm3(bank[s][:, :], wH[:, s, k], wL[:, s, k], hH[:, kt, :], hL[:, kt, :],
                                       kt == 0, kt == KT - 1)
                        last.then_inc(panel_done, 1)

                first = h_tiles is not None
                if first or n_panels == RING:
                    body(0, first)
                    n_panels -= RING
                    npan[0] += RING
                if n_panels:
                    with pe.Fori(1 if first else 0, n_panels // RING + (1 if first else 0)) as i:
                        body(i)
                npan[0] += n_panels

            def residual_gemm():
                n0 = npan[0]
                for c in range(KT + 2):
                    if c < KT:
                        s = c % RING
                        pe.wait_ge(out_free, n0 + c + 1 - RING)
                        pe.wait_ge(lo_ready, n0 + c + 1)
                        for kt in range(KT):
                            k = slice(kt * P, (kt + 1) * P)
                            last = mm3(bank[s][:, :], wH[:, s, k], wL[:, s, k], hH[:, kt, :], hL[:, kt, :],
                                       kt == 0, kt == KT - 1)
                        last.then_inc(panel_done, 1)
                    if c >= 2:
                        sum_square(bank[4][:, :], mean_d, c == 2, c == KT + 1)
                npan[0] += KT

            def values():
                n0 = npan[0]
                pe.wait_ge(out_free, n0)
                for s in range(RING):
                    pe.wait_ge(lo_ready, n0 + s + 1)
                    for half in range(2):
                        kt = 2 * s + half
                        for tb in range(TB):
                            t, k = slice(tb * P, (tb + 1) * P), slice(half * 512, (half + 1) * 512)
                            last = mm3(bank[tb][:, :], hH[:, kt, t], hL[:, kt, t], wH[:, s, k], wL[:, s, k],
                                       kt == 0, kt == KT - 1, skip_group_check=True)
                    last.then_inc(panel_done, 1)
                npan[0] += 4

            def mix(a_hi, a_lo, b_hi, b_lo):
                n0 = npan[0]
                for n in range(8):
                    s = n % RING
                    pe.wait_ge(out_free, n0 if n < 2 else n0 + n - 1)
                    pe.wait_ge(lo_ready, n0 + n + 1)
                    for kt in range(KT):
                        hi, lo = (a_hi, a_lo) if kt < CT else (b_hi, b_lo)
                        k, c = slice(kt * P, (kt + 1) * P), kt % CT
                        last = mm3(bank[2 * (n % 2) + kt // CT][:, :], wH[:, s, k], wL[:, s, k],
                                   hi[:, c, :], lo[:, c, :], c == 0, c == CT - 1)
                    last.then_inc(panel_done, 1)
                npan[0] += 8

            def attend(qT, q0, k0, first):
                m = len(UNITS)
                n0 = npan[0]
                for i in range(m + 2):
                    if i < m:
                        qb, h = UNITS[i]
                        n, r = P * (qb + 1), 64 * (h % 2)
                        if first + i >= 2:
                            pe.wait_ge(lg_done, first + i - 1)
                        mm(bank[4 + i % 2][:, 0:n], qT[r:r + 64, q0 + h // 2, qb * P:(qb + 1) * P],
                           qT[r:r + 64, k0 + h // 2, 0:n], start=True, stop=True).then_inc(lg_ready, 1)
                        g, s = i // 2, (i // 2) % RING
                        if i % 2 == 0:
                            pe.wait_ge(out_free, n0 if g < 2 else n0 + g - 1)
                            pe.wait_ge(lo_ready, n0 + g + 1)
                        for kt in range(4 * (i % 2), 4 * (i % 2) + 4):
                            k = slice(kt * P, (kt + 1) * P)
                            last = mm3(bank[2 + g % 2][:, :], wH[:, s, k], wL[:, s, k], hH[:, kt, :], hL[:, kt, :],
                                       kt == 0, kt == KT - 1)
                        if i % 2:
                            last.then_inc(panel_done, 1)
                    if 1 <= i <= m:
                        j = i - 1
                        qb, h = UNITS[j]
                        pe.wait_ge(prob_ready, first + j + 1)
                        if first + j >= 2:
                            pe.wait_ge(pT_ready, first + j - 1)
                        for c in range(qb + 1):
                            last = nc.tensor.transpose(bank[6 + j % 2][:, c * P:(c + 1) * P],
                                                       ex[:, j % 2, c * P:(c + 1) * P], ident[:, :])
                        last.then_inc(tr_ready, 1)
                    if i >= 2:
                        j = i - 2
                        qb, h = UNITS[j]
                        pe.wait_ge(pT_ready, first + j + 1)
                        if first + j >= 2:
                            pe.wait_ge(pv_used, first + j - 1)
                        for c in range(qb + 1):
                            last = mm(bank[j % 2][:, 0:P], vtok[:, c, (h // 2) * P:(h // 2 + 1) * P],
                                      pT[:, j % 2, c * P:(c + 1) * P], start=(c == 0), stop=(c == qb))
                        last.then_inc(pv_ready, 1)
                npan[0] += 16

            pe.wait_ge(small_in, 80)
            for j in range(2):
                last = mm(bank[6 + j][0:H, 0:320], relb[:, :], onehot[:, j * 320:(j + 1) * 320], start=True, stop=True)
            last.then_inc(rel_ready, 1)
            pe.wait_ge(const_ready, 1)
            norm()
            gemm_loop(4, 0)
            pe.wait_ge(small_ready, 1)
            for kt in range(KT):
                last = mm3(bank[5][0:H, :], wwiH[:, kt * H:(kt + 1) * H], wwiL[:, kt * H:(kt + 1) * H],
                           hH[:, kt, :], hL[:, kt, :], kt == 0, kt == KT - 1)
            last.then_inc(ki_ready, 1)
            for kt in range(KT):
                last = mm3(bank[4][:, :], wkiH[:, kt, :], wkiL[:, kt, :], hH[:, kt, :], hL[:, kt, :],
                           kt == 0, kt == KT - 1)
            last.then_inc(ki_ready, 1)
            pe.wait_ge(ki_copied, 1)
            for tb in range(TB):
                last = mm(bank[5][:, tb * H:(tb + 1) * H], wiT[:, tb * P:(tb + 1) * P], ident[0:H, 0:H],
                          start=True, stop=True)
            last.then_inc(ki_ready, 1)
            pe.wait_ge(ki_copied, 3)
            pe.wait_ge(out_free, 4)
            for j in range(3 * H):
                qb, h = j // H + 1, j % H
                r = 64 * (h % 2)
                if j >= 2:
                    pe.wait_ge(relu_ready, j - 1)
                mm(bank[4 + j % 2][:, 0:P * (qb + 1)], qkiT[r:r + 64, h // 2, qb * P:(qb + 1) * P],
                   kiT[r:r + 64, 0:P * (qb + 1)], start=True, stop=True).then_inc(dot_ready, 1)
            gemm_loop(8)
            values()
            pe.wait_ge(relu_ready, 3 * H)
            for c in range(8):
                n0, s = npan[0], c % RING
                pe.wait_ge(out_free, n0 + 1 - RING)
                pe.wait_ge(lo_ready, n0 + 1)
                for kt in range(KT):
                    k = slice(kt * P, (kt + 1) * P)
                    last = mm3(bank[s][:, :], wH[:, s, k], wL[:, s, k], hH[:, kt, :], hL[:, kt, :],
                               kt == 0, kt == KT - 1)
                last.then_inc(panel_done, 1)
                npan[0] += 1
                if c % 2:
                    for e in (c - 1, c):
                        if e >= 2:
                            pe.wait_ge(rt_ready, e)
                        sum_square(bank[4 + e % 2][:, :], mean_h, True, True)
            pe.wait_ge(qk_ready, 8)
            pe.wait_ge(out_free, npan[0])
            attend(qkiT, 4, 8, 0)
            pe.wait_ge(cv, CT * TAPS)
            for c in range(CT):
                last = mm(bank[4][:, :], mean_c[:, :], ybr[:, c, :], start=(c == 0), stop=(c == CT - 1))
            last.then_inc(cm_ready, 1)
            for c in range(CT):
                pe.wait_ge(csq_ready, c + 1)
                mm(bank[5][:, :], mean_c[:, :], sq[:, c % 2, :], start=(c == 0), stop=(c == CT - 1)).then_inc(cvar_ready, 1)
            pe.wait_ge(br_split, 1)
            mix(oH, oL, yH, yL)
            pe.wait_ge(mixed_ready, 1)
            residual_gemm()
            gemm_loop(16, 8)
            pe.wait_ge(out_free, npan[0])
            pe.wait_ge(peer_in, 16)

            def key_scores(tb):
                for q4 in range(4):
                    if tb * 4 + q4 >= 2:
                        pe.wait_ge(sc_ready, tb * 4 + q4 - 1)
                    for c in range(4):
                        hc = q4 * 4 + c
                        last = mm(bank[4 + q4 % 2][:, c * P:(c + 1) * P], qpT[:, hc, tb * P:(tb + 1) * P],
                                  subk[:, hc, :], start=True, stop=True)
                    last.then_inc(sc_mm, 1)

            def spread_gates(tb):
                pe.wait_ge(keys_ready, tb + 1)
                for j, src in enumerate((gate[:, :], eij[:, 0, :], eij[:, 1, :])):
                    last = nc.tensor.transpose(bank[4][:, j * P:(j + 1) * P], src, ident[:, :])
                last.then_inc(keys_tr, 1)
                t0, n0 = tb * P, npan[0]

                def body(i, first):
                    for j in range(8):
                        s, half = j // 2, j % 2
                        for b in range(2):
                            for u in range(4 * b, 4 * b + 4):
                                pe.wait_ge(hot_ready, i * 64 + (t0 + 8 * j + u + 1))
                                if u == 4 * b and not (first and j == 0):
                                    pe.wait_ge(spread_copied, i * 16 + (t0 // 4 + 2 * j + b - 1))
                                mm(bank[6 + b][:, (u % 4) * P:(u % 4 + 1) * P], hot2[:, u, :], hot1[:, u, :],
                                   start=True, stop=True).then_inc(spread_mm, 1)
                        if half == 0:
                            pe.wait_ge(out_free, i * RING + (n0 + s + 1 - RING))
                            pe.wait_ge(lo_ready, i * RING + (n0 + s + 1))
                        for kt in range(4 * half, 4 * half + 4):
                            k = slice(kt * P, (kt + 1) * P)
                            last = mm3(bank[s][:, :], wH[:, s, k], wL[:, s, k], hH[:, kt, :], hL[:, kt, :],
                                       kt == 0, kt == KT - 1)
                        if half:
                            last.then_inc(panel_done, 1)

                if tb == 0:
                    body(0, True)
                    body(1, False)
                else:
                    with pe.Fori(0, UMID // RING) as i:
                        body(i, False)
                npan[0] += UMID

            key_scores(0)
            for tb in range(TB):
                gemm_loop(UCUT[tb])
                spread_gates(tb)
                if tb + 1 < TB:
                    key_scores(tb + 1)
            gemm_loop(NEXP - sum(UCUT) - TB * UMID)
            n0 = npan[0]
            pe.wait_ge(out_free, n0)
            pe.wait_ge(spread_copied, S // 4)

            def experts(i, edge):
                for s in range(RING):
                    pe.wait_ge(lo_ready, i * RING + (n0 + s + 1))
                    pe.wait_ge(wgt_ready, i * RING + (s + 1))
                    for nt in range(KT):
                        k = slice(nt * P, (nt + 1) * P)
                        last = mm3(bank[nt][:, :], wH[:, s, k], wL[:, s, k], wgtH[:, s, :], wgtL[:, s, :],
                                   edge == "first" and s == 0, edge == "last" and s == RING - 1, skip_group_check=True)
                    last.then_inc(panel_done, 1)

            experts(0, "first")
            with pe.Fori(1, GV - 1) as i:
                experts(i, None)
            experts(GV - 1, "last")
            npan[0] += NEXP
            norm(0)
            pe.wait_ge(ple_in, 32)
            n0 = npan[0]
            for n in range(8):
                s = n % RING
                pe.wait_ge(out_free, n0 if n < 2 else n0 + n - 1)
                pe.wait_ge(lo_ready, n0 + n + 1)
                for kt in range(2):
                    mm(bank[2 * (n % 2) + 1][:, :], wpp[:, kt, n * P:(n + 1) * P], pT_in[:, kt, :],
                       start=(kt == 0), stop=(kt == 1))
                for kt in range(KT):
                    if n == 0:
                        pe.wait_ge(h_ready, 16 + kt + 1)
                    k = slice(kt * P, (kt + 1) * P)
                    last = mm3(bank[2 * (n % 2)][:, :], wH[:, s, k], wL[:, s, k], hH[:, kt, :], hL[:, kt, :],
                               kt == 0, kt == KT - 1)
                last.then_inc(panel_done, 1)
            npan[0] += 8
            norm()
            gemm_loop(12, 24)
            pe.wait_ge(wf_ready, 1)
            for kt in range(KT):
                last = mm3(bank[4][0:H, :], wfH[:, kt * H:(kt + 1) * H], wfL[:, kt * H:(kt + 1) * H],
                           hH[:, kt, :], hL[:, kt, :], kt == 0, kt == KT - 1)
            last.then_inc(f_ready, 1)
            pe.wait_ge(zT_ready, 1)
            for tb in range(TB):
                last = mm(bank[5][:, tb * H:(tb + 1) * H], zT[:, tb * P:(tb + 1) * P], ident[0:H, 0:H],
                          start=True, stop=True)
            last.then_inc(f_ready, 1)
            gemm_loop(8)
            values()
            pe.wait_ge(logf_ready, 1)
            pe.wait_ge(two_const, 1)
            for tc in range(TB):
                last = mm(bank[5][0:H, :], z[:, 2, tc * H:(tc + 1) * H], tri[:, tc, :], start=(tc == 0), stop=(tc == TB - 1))
            last.then_inc(fT_mm, 1)
            for qb in range(TB):
                for tc in range(TB):
                    last = mm(bank[4][:, qb * H:(qb + 1) * H], tri[:, tc, qb * P:(qb + 1) * P],
                              z[:, 2, tc * H:(tc + 1) * H], start=(tc == 0), stop=(tc == TB - 1))
            last.then_inc(fT_mm, 1)
            pe.wait_ge(fT_ready, 2)
            for h in range(H):
                if h >= 2:
                    pe.wait_ge(nfk_ready, h - 1)
                mm(bank[6 + h % 2][:, :], negsel[:, h, :], fT[:, :], start=True, stop=True).then_inc(nfk_mm, 1)
            pe.wait_ge(nfk_ready, H)
            pe.wait_ge(out_free, npan[0])
            attend(qk2T, 0, 4, len(UNITS))
            pe.wait_ge(br_split, 2)
            mix(yH, yL, oH, oL)
            pe.wait_ge(mixed_ready, 2)
            residual_gemm()
            gemm_loop(2 * FT, 32)
            n0 = npan[0]
            pe.wait_ge(out_free, n0)
            pe.wait_ge(act_ready, FT)

            def down(s, count, hi, lo, first, last_tile):
                pe.wait_ge(lo_ready, count)
                for nt in range(KT):
                    k = slice(nt * P, (nt + 1) * P)
                    last = mm3(bank[nt][:, :], wH[:, s, k], wL[:, s, k], hi, lo, first, last_tile,
                               skip_group_check=True)
                last.then_inc(panel_done, 1)

            for kt in range(RING):
                down(kt, n0 + kt + 1, actH[:, kt, :], actL[:, kt, :], kt == 0, False)
            with pe.Fori(1, FT // RING) as i:
                for s in range(RING):
                    down(s, i * RING + (n0 + s + 1), actH[:, ds(i * RING + s, 1), :], actL[:, ds(i * RING + s, 1), :],
                         False, False)
            for kt in range(FT // RING * RING, FT):
                down(kt % RING, n0 + kt + 1, actH[:, kt, :], actL[:, kt, :], False, kt == FT - 1)
            norm(0)

        @block.vector
        def _(dve):
            v = nc.vector
            step = Steps(dve, dve_step)
            npan = [0]
            nrt = [0]

            def split(hi, lo, x):
                step(v.tensor_copy(hi, x))
                return v.tensor_tensor(lo, x, hi.bitcast(f32), ALU.subtract)

            def norm_rs():
                dve.wait_ge(rt_ready, nrt[0] + 1)
                v.reciprocal(rs[:, :], rt[:, nrt[0] % 2, :]).then_inc(rt_used, 1)
                nrt[0] += 1
                dve.wait_ge(rt_used, nrt[0])

            def norm(k):
                norm_rs()
                for c in range(KT):
                    if k == 5:
                        last = v.scalar_tensor_tensor(xT[:, c, :], xT[:, c, :], V(NORMS[k], c), rs[:, :],
                                                      ALU.mult, ALU.mult)
                    else:
                        if c >= 2:
                            dve.wait_ge(h_ready, 8 * k + c - 1)
                        v.scalar_tensor_tensor(sq[:, c % 2, :], xT[:, c, :], V(NORMS[k], c), rs[:, :],
                                               ALU.mult, ALU.mult).then_inc(norm_ready, 1)
                        if c:
                            norm_rest(k, c - 1)
                if k != 5:
                    norm_rest(k, KT - 1)
                    return None
                return last

            def norm_rest(k, c):
                dve.wait_ge(norm_ready, 8 * k + c + 1)
                dve.wait_ge(norm_hi, 8 * k + c + 1)
                v.tensor_tensor(hL[:, c, :], sq[:, c % 2, :], hH[:, c, :].bitcast(f32), ALU.subtract).then_inc(h_ready, 1)
                if c + 2 >= KT:
                    dve.wait_ge(h_ready, 8 * k + c + 1)

            def mix_evac(gates0):
                for n in range(8):
                    dve.wait_ge(panel_done, npan[0] + 1)
                    dve.wait_ge(gate_sig, gates0 + 2 * (n + 1))
                    step(v.tensor_tensor(rs[:, :], bank[2 * (n % 2) + 1][:, :], gates[:, 8 + n, :], ALU.mult))
                    m = sq[:, n % 2, :]
                    v.tensor_tensor(m, bank[2 * (n % 2)][:, :], gates[:, n, :], ALU.mult).then_inc(out_free, 1)
                    npan[0] += 1
                    dve.wait_ge(out_free, npan[0])
                    step(v.tensor_tensor(m, m, rs[:, :], ALU.add))
                    step(split(hH[:, n, :], hL[:, n, :], m))
                dve.sem_inc(mixed_ready, 1)

            def add_to_x():
                n0 = npan[0]
                with dve.Fori(0, KT // RING) as i:
                    for s in range(RING):
                        dve.wait_ge(panel_done, i * RING + (n0 + s + 1))
                        x = xT[:, ds(i * RING + s, 1), :]
                        v.tensor_tensor(x, x, bank[s][:, :].rearrange("p (a n) -> p a n", a=1), ALU.add)\
                         .then_inc(out_free, 1)
                npan[0] += KT
                dve.wait_ge(out_free, npan[0])
                dve.sem_inc(x_ready, 1)

            def attend(first, logits, meanwhile):
                m = len(UNITS)
                for i in range(m + 2):
                    if i < m:
                        qb, h = UNITS[i]
                        n = P * (qb + 1)
                        dve.wait_ge(lg_ready, first + i + 1)
                        if i >= 2:
                            dve.wait_ge(ex_ready, first + i - 1)
                        logits(i, qb, h, n)
                    if 1 <= i <= m:
                        j = i - 1
                        dve.wait_ge(ex_ready, first + j + 1)
                        if first + j >= 4:
                            dve.wait_ge(prob_ready, first + j - 3)
                        v.reciprocal(rsum[:, j % 4:j % 4 + 1], esum[:, j % 4:j % 4 + 1]).then_inc(rsum_ready, 1)
                    meanwhile(i)
                    if i >= 2:
                        j = i - 2
                        qb, h = UNITS[j]
                        r = 64 * (h % 2)
                        dve.wait_ge(pv_ready, first + j + 1)
                        v.tensor_copy(oT[r:r + 64, h // 2, qb * P:(qb + 1) * P], bank[j % 2][r:r + 64, 0:P])\
                         .then_inc(pv_used, 1)

            dve.wait_ge(vec_in, 16)
            dve.wait_ge(x_in, 32)
            dve.wait_ge(small_in, 80)
            split(wkiH[:, :, :], wkiL[:, :, :], wki2[:, :, :])
            step(split(wwiH[:, :], wwiL[:, :], wwi[:, :]))
            dve.sem_inc(small_ready, 1)
            norm(0)
            dve.wait_ge(ki_copied, 3)
            j = 0
            for qb in range(1, TB):
                n = P * (qb + 1)
                score = scores[:, qb - 1, 0:n]
                for h in range(H):
                    dve.wait_ge(relu_ready, j + 1)
                    w = wi[:, qb * H + h:qb * H + h + 1]
                    if h == 0:
                        v.tensor_scalar(score, lg[:, j % 2, 0:n], w, None, ALU.mult).then_inc(relu_used, 1)
                    else:
                        v.scalar_tensor_tensor(score, lg[:, j % 2, 0:n], w, score, ALU.mult, ALU.add)\
                         .then_inc(relu_used, 1)
                    j += 1
                    dve.wait_ge(relu_used, j)
                step(v.memset(score[0:64, n - 64:n], MASKED))
            blocks = [(qb, scores[:, qb - 1, 0:P * (qb + 1)], top8[:, 8 * qb:8 * qb + 8]) for qb in range(1, TB)]
            for rnd in range(TOPK // 8):
                for qb, score, best in blocks:
                    last = v.max(out=best, in_=score)
                step(last)
                for qb, score, best in blocks:
                    last = v.match_replace(out=score, in_to_replace=best, in_values=score, imm_value=TAKEN)
                step(last)
            for qb, score, best in blocks:
                last = v.tensor_scalar(mask[:, MOFF[qb]:MOFF[qb] + P * (qb + 1)], score, TAKEN / 2, MASKED,
                                       ALU.is_gt, ALU.mult)
            step(last)
            npan[0] += 4 + 8 + 4
            for c in range(CT):
                dve.wait_ge(u_sig, c + 1)
                npan[0] += 2
                v.tensor_tensor(upad[:, c, TAPS - 1:TAPS - 1 + S], bank[(2 * c) % 4][:, :], lg[:, c % 2, :], ALU.mult)\
                 .then_inc(out_free, 2)
                for e in (2 * c, 2 * c + 1):
                    norm_rs()
                    step(v.scalar_tensor_tensor(qkiT[:, 4 + e, :], qkiT[:, 4 + e, :], V("q_g" if e < 4 else "k_g"),
                                                rs[:, :], ALU.mult, ALU.mult))
                    dve.sem_inc(qk_ready, 1)
            npan[0] += 16
            dve.wait_ge(out_free, FIRST["gates"])
            dve.wait_ge(const_ready, 1)

            def conv_tap(k):
                for c in range(CT if k < TAPS else 0):
                    w = V("conv_w", c * TAPS + k)
                    src = upad[:, c, k:k + S]
                    if k == 0:
                        v.tensor_scalar(ybr[:, c, :], src, w, V("conv_b", c), ALU.mult, ALU.add).then_inc(cv, 1)
                    else:
                        dve.wait_ge(cv, (k - 1) * CT + c + 1)
                        v.scalar_tensor_tensor(ybr[:, c, :], src, w, ybr[:, c, :], ALU.mult, ALU.add).then_inc(cv, 1)
            dve.wait_ge(rel_in, 16)
            dve.wait_ge(const_ready, 1)

            def logits_one(i, qb, h, n):
                step(v.scalar_tensor_tensor(lg[:, i % 2, 0:n], bank[4 + i % 2][:, 0:n], HD ** -0.5,
                                            bias[:, h, 0:n][:, ::-1], ALU.mult, ALU.add))
                step(v.tensor_tensor(lg[:, i % 2, 0:n], lg[:, i % 2, 0:n], mask[:, MOFF[qb]:MOFF[qb] + n], ALU.add))
                v.tensor_reduce(nmax[:, i % 4:i % 4 + 1], lg[:, i % 2, 0:n], axis=AX.X, op=ALU.max, negate=True)\
                 .then_inc(lg_done, 1)

            attend(0, logits_one, conv_tap)
            dve.wait_ge(cm_ready, 1)
            for c in range(CT):
                v.tensor_tensor(ybr[:, c, :], ybr[:, c, :], bank[4][:, :], ALU.subtract).then_inc(cx_ready, 1)
            dve.wait_ge(pv_used, len(UNITS))
            v.tensor_copy(oH[:, :, :], oT[:, :, :])
            dve.wait_ge(csd_ready, 1)
            step(v.reciprocal(rs[:, :], rt[:, 0, :]))
            for c in range(CT):
                v.tensor_tensor(ybr[:, c, :], ybr[:, c, :], rs[:, :], ALU.mult).then_inc(cn_ready, 1)
            for c in range(CT):
                dve.wait_ge(br_ready, c + 1)
                last = split(yH[:, c, :], yL[:, c, :], ybr[:, c, :])
            step(last)
            v.tensor_tensor(oL[:, :, :], oT[:, :, :], oH[:, :, :].bitcast(f32), ALU.subtract).then_inc(br_split, 1)
            mix_evac(0)
            add_to_x()
            norm(1)
            npan[0] += 16
            dve.wait_ge(peer_free, 1)

            def route(tb):
                for hc in range(16):
                    half, col = hc // 8, (hc % 8) * P
                    src = sc[:, half, col:col + P]
                    dve.wait_ge(sc_ready, tb * 4 + hc // 4 + 1)
                    step(v.max(out=sv[:, hc, 0:8], in_=src))
                    v.max_index(out=si[:, hc, 0:8], in_max=sv[:, hc, 0:8], in_values=src)
                    step(v.match_replace(out=sc2, in_to_replace=sv[:, hc, 0:8], in_values=src, imm_value=TAKEN))
                    step(v.max(out=sv[:, hc, 8:16], in_=sc2))
                    step(v.max_index(out=si[:, hc, 8:16], in_max=sv[:, hc, 8:16], in_values=sc2))
                v.tensor_copy(sif[:, :, :], si[:, :, :])
                s4 = sv[:, :, :].rearrange("p (h c) k -> p h c k", c=2)
                step(v.tensor_tensor(cand[:, :, :].rearrange("p h (a b) -> p h a b", a=PK),
                                     s4[:, :, 0, :].unsqueeze(3).to_broadcast([P, PH, PK, PK]),
                                     s4[:, :, 1, :].unsqueeze(2).to_broadcast([P, PH, PK, PK]), ALU.add))
                for h in range(PH):
                    step(v.max(out=tops[:, h, 0:8], in_=cand[:, h, :]))
                    v.max_index(out=topj[:, h, 0:8], in_max=tops[:, h, 0:8], in_values=cand[:, h, :])
                    step(v.match_replace(out=cand2[:, :], in_to_replace=tops[:, h, 0:8], in_values=cand[:, h, :],
                                         imm_value=TAKEN))
                    step(v.max(out=tops[:, h, 8:16], in_=cand2[:, :]))
                    step(v.max_index(out=topj[:, h, 8:16], in_max=tops[:, h, 8:16], in_values=cand2[:, :]))
                gt = gate[:, :].rearrange("p (h k) -> p h k", h=PH)
                v.tensor_tensor(gt, tops[:, :, :], tops[:, :, 0:1].to_broadcast([P, PH, PK]), ALU.subtract)\
                 .then_inc(g_shift, 1)
                tj = topj[:, :, :].rearrange("p h k -> p (h k)")
                v.tensor_scalar(tja[:, 0, :], tj, 4, None, ALU.logical_shift_right)
                step(v.tensor_scalar(tja[:, 1, :], tj, 15, None, ALU.bitwise_and))
                step(v.tensor_copy(tjf[:, :, :], tja))
                e4 = eqv[:, :, :].rearrange("p h (k a) -> p h k a", k=PK)
                i4 = sif[:, :, :].rearrange("p (h c) a -> p h c a", c=2)
                for c in range(2):
                    t3 = tjf[:, c, :].rearrange("p (h k) -> p h k", h=PH)
                    step(v.tensor_tensor(e4, t3.unsqueeze(3).to_broadcast([P, PH, PK, PK]),
                                         iota16[:, :].unsqueeze(1).unsqueeze(1).to_broadcast([P, PH, PK, PK]),
                                         ALU.is_equal))
                    step(v.tensor_tensor(e4, e4, i4[:, :, c, :].unsqueeze(2).to_broadcast([P, PH, PK, PK]), ALU.mult))
                    step(v.tensor_reduce(eij[:, c, :].rearrange("p (h k) -> p h k", h=PH), e4, axis=AX.X, op=ALU.add))
                dve.sem_inc(sc_used, 1)
                dve.wait_ge(g_exp, tb + 1)
                step(v.tensor_reduce(gsum[:, 0, :], gt, axis=AX.X, op=ALU.add))
                step(v.reciprocal(gsum[:, 1, :], gsum[:, 0, :]))
                step(v.tensor_tensor(gt, gt, gsum[:, 1, :].unsqueeze(2).to_broadcast([P, PH, PK]), ALU.mult))

            def one_hots(tb):
                dve.wait_ge(keys_tr, tb + 1)
                step(v.tensor_copy(chosen[:, :, :], bank[4][:, 0:3 * P].rearrange("p (a n) -> p a n", a=3)))
                t0 = tb * P

                def tokens(i, first):
                    for b in range(2):
                        if not first:
                            dve.wait_ge(spread_mm, i * 8 + (t0 + 4 * b - 4))
                        v.tensor_tensor(hot2[:, 4 * b:4 * b + 4, :], iota[:, :].unsqueeze(1).to_broadcast([P, 4, P]),
                                        chosen[:, 2, ds(i * 8 + 4 * b, 4)].unsqueeze(2).to_broadcast([P, 4, P]),
                                        ALU.is_equal)
                        for u in range(4 * b, 4 * b + 4):
                            v.tensor_scalar(hot1[:, u, :], iota[:, :], chosen[:, 1, ds(i * 8 + u, 1)],
                                            chosen[:, 0, ds(i * 8 + u, 1)], ALU.is_equal, ALU.mult).then_inc(hot_ready, 1)

                if tb == 0:
                    tokens(0, True)
                with dve.Fori(1 if tb == 0 else 0, P // 8) as i:
                    tokens(i, False)

            for tb in range(TB):
                route(tb)
                dve.sem_inc(keys_ready, 1)
                one_hots(tb)
            n0 = FIRST["peer_v"]

            def weights(i, first):
                for b in range(2):
                    for s in range(4):
                        if s == 0:
                            dve.wait_ge(pair_in[b], i * 32 + 32)
                        n = i * 8 + (4 * b + s + 1)
                        if not (first and b == 0):
                            dve.wait_ge(panel_done, i * 8 + (n0 + 4 * b + s - 3))
                        x = gin[:, b, s, :]
                        step(v.tensor_tensor(x.rearrange("p (g t) -> p g t", t=GT), x.rearrange("p (g t) -> p g t", t=GT),
                                             din[:, b, :, s, :], ALU.mult))
                        v.tensor_copy(wgtH[:, s, :], x).then_inc(wgt_hi, 1)
                        dve.wait_ge(wgt_hi, n)
                        v.tensor_tensor(wgtL[:, s, :], x, wgtH[:, s, :].bitcast(f32), ALU.subtract).then_inc(wgt_ready, 1)

            weights(0, True)
            base = step.n
            with dve.Fori(1, GV // 2) as i:
                step.n = i * 8 + (base - 8)
                weights(i, False)
            step.n = base + 8 * (GV // 2 - 1)
            npan[0] += 2 * NEXP
            dve.wait_ge(panel_done, npan[0])
            for nt in range(KT):
                v.tensor_tensor(xT[:, nt, :], xT[:, nt, :], bank[nt][:, :], ALU.add).then_inc(out_free, NEXP // KT)
            dve.wait_ge(out_free, npan[0])
            dve.sem_inc(x_ready, 1)
            norm(2)
            for n in range(8):
                dve.wait_ge(sg_ready, n + 1)
                npan[0] += 1
                v.tensor_tensor(sg[:, n % 2, :], sg[:, n % 2, :], bank[2 * (n % 2) + 1][:, :], ALU.mult).then_inc(out_free, 1)
                dve.wait_ge(out_free, npan[0])
                step(v.tensor_tensor(xT[:, n, :], xT[:, n, :], sg[:, n % 2, :], ALU.add))
                dve.sem_inc(sg_used, 1)
            dve.sem_inc(x_ready, 1)
            dve.wait_ge(two_in, 16)
            step(split(wfH[:, :], wfL[:, :], wf[:, :]))
            dve.sem_inc(wf_ready, 1)
            norm(3)
            npan[0] += 4
            dve.wait_ge(out_free, npan[0])
            dve.wait_ge(two_const, 1)
            for c in range(CT):
                dve.wait_ge(panel_done, npan[0] + 1)
                v.tensor_tensor(zpad[:, c, 2:S + 2], bank[c][:, :], ccT[:, c, :], ALU.mult).then_inc(out_free, 1)
                npan[0] += 1
                dve.wait_ge(out_free, npan[0])
                step(v.tensor_scalar(ybr2[:, c, :], zpad[:, c, 2:S + 2], V("conv_mix_w", c * 3 + 2), None, ALU.mult))
                for k in range(2):
                    step(v.scalar_tensor_tensor(ybr2[:, c, :], zpad[:, c, k:k + S], V("conv_mix_w", c * 3 + k),
                                                ybr2[:, c, :], ALU.mult, ALU.add))
            for c in range(CT):
                dve.wait_ge(panel_done, npan[0] + 1)
                v.tensor_tensor(ybr2[:, c, :], ybr2[:, c, :], bank[c][:, :], ALU.mult).then_inc(out_free, 1)
                npan[0] += 1
            dve.wait_ge(f_ready, 2)
            step(v.tensor_tensor(z[:, 0, :], bank[5][:, 0:TB * H], V("b_f", 0, TB * H), ALU.add))
            dve.sem_inc(z_ready, 1)
            step(v.tensor_scalar(z[:, 2, :], z[:, 0, :], 0.0, None, ALU.min))
            dve.wait_ge(sp_ready, 1)
            v.tensor_tensor(z[:, 2, :], z[:, 2, :], z[:, 1, :], ALU.subtract).then_inc(logf_ready, 1)
            dve.wait_ge(fT_mm, 2)
            v.tensor_copy(fq[:, :], bank[4][:, 0:TB * H]).then_inc(fT_ready, 1)
            dve.wait_ge(nfk_ready, H)
            dve.wait_ge(fT_ready, 2)
            npan[0] += 8 + 4 + 16

            def logits_two(i, qb, h, n):
                step(v.scalar_tensor_tensor(lg[:, i % 2, 0:n], bank[4 + i % 2][:, 0:n], fq[:, qb * H + h:qb * H + h + 1],
                                            nfk[:, h, 0:n], ALU.add, ALU.add))
                step(v.tensor_tensor(lg[:, i % 2, n - P:n], lg[:, i % 2, n - P:n], causal[:, :], ALU.add))
                v.tensor_reduce(nmax[:, i % 4:i % 4 + 1], lg[:, i % 2, 0:n], axis=AX.X, op=ALU.max, negate=True)\
                 .then_inc(lg_done, 1)

            attend(len(UNITS), logits_two, lambda i: None)
            dve.wait_ge(pv_used, 2 * len(UNITS))
            dve.wait_ge(out_free, FIRST["q2"])
            step(split(yH[:, :, :], yL[:, :, :], ybr2[:, :, :]))
            step(split(oH[:, :, :], oL[:, :, :], oT[:, :, :]))
            dve.sem_inc(br_split, 1)
            mix_evac(16)
            add_to_x()
            norm(4)
            n0 = npan[0]
            base = step.n
            with dve.Fori(0, 2 * FT // RING) as i:
                step.n = i * 10 + base
                for s in range(RING):
                    dve.wait_ge(out_free, i * RING + (n0 + s + 1))
                    step(v.tensor_scalar(upc[s], uppad[:, s, 2:S + 2], V("conv_ffn_w", i * 12 + (3 * s + 2)), None,
                                         ALU.mult))
                    step(v.scalar_tensor_tensor(upc[s], uppad[:, s, 0:S], V("conv_ffn_w", i * 12 + 3 * s),
                                                upc[s], ALU.mult, ALU.add))
                    v.scalar_tensor_tensor(upc[s], uppad[:, s, 1:S + 1], V("conv_ffn_w", i * 12 + (3 * s + 1)),
                                           upc[s], ALU.mult, ALU.add).then_inc(up_conv, 1)
                for s in (0, 2):
                    dve.wait_ge(up_conv, i * RING + (s + 2))
                    dve.wait_ge(up_silu, i * 2 + (s // 2 + 1))
                    step(v.tensor_tensor(upc[s], upc[s], upc[s + 1], ALU.mult))
                    tile = ds(i * 2 + s // 2, 1)
                    hi = actH[:, tile, :].rearrange("p a n -> p (a n)")
                    v.tensor_copy(hi, upc[s]).then_inc(act_hi, 1)
                    dve.wait_ge(act_hi, i * 2 + (s // 2 + 1))
                    v.tensor_tensor(actL[:, tile, :].rearrange("p a n -> p (a n)"), upc[s], hi.bitcast(f32), ALU.subtract)\
                     .then_inc(act_ready, 1)
                dve.wait_ge(act_ready, i * 2 + 2)
            step.n = base + 10 * (2 * FT // RING)
            npan[0] += 2 * FT + FT
            dve.wait_ge(panel_done, NPANEL)
            for nt in range(KT):
                v.tensor_tensor(xT[:, nt, :], xT[:, nt, :], bank[nt][:, :], ALU.add).then_inc(y_tile, 1)
            dve.wait_ge(y_tile, KT)
            norm(5).then_inc(y_ready, 1)


def kernel(**inputs):
    import concourse.bacc as bacc
    from concourse.bass_utils import run_bass_kernel_spmd

    a = {k: np.asarray(v) for k, v in inputs.items()}

    def tiles(w):
        kt, n = w.shape[0] // P, w.shape[1] // P
        return w.reshape(kt, P, n, P).transpose(2, 1, 0, 3).reshape(n, P, kt * P)

    def values(w):
        return w.reshape(4, 2, P, 512).transpose(0, 2, 1, 3).reshape(4, P, 2 * 512)

    def pairs(x, y):
        return np.stack([x, y], 1).reshape(-1, *x.shape[1:])

    w1, w2 = a["w_in"][0], a["w_in_2"][0]
    wq, wk, wv, wqi, wki, wwi, wglu, wgates = np.split(w1, np.cumsum([512, 512, 512, 512, 64, 8, 1024]), axis=1)
    cb, cc, cin, q2, k2, v2, wf, gates2 = np.split(w2, np.cumsum([512, 512, 512, 512, 512, 512, 8]), axis=1)
    up = tiles(a["w_up_2"][0])
    panels = np.concatenate([
        tiles(wqi), tiles(wq), tiles(wk), values(wv), pairs(tiles(wglu[:, :512]), tiles(wglu[:, 512:])), tiles(wgates),
        tiles(np.concatenate([a["w_att_out"][0], a["w_conv_out"][0]], 0)), tiles(a["w_out"][0]),
        tiles(a["w_peer_q"][0]), tiles(a["peer_u"][0].T), a["peer_v"][0].reshape(NEXP, P, D), tiles(a["w_ple_gate"][0]),
        tiles(cc), tiles(cin), tiles(cb), tiles(q2), tiles(k2), values(v2), tiles(gates2),
        tiles(np.concatenate([a["w_out_conv_2"][0], a["w_out_attn_2"][0]], 0)), tiles(a["w_o_2"][0]),
        pairs(up[:FT], up[FT:]), a["w_down_2"][0].reshape(FT, P, D)], 0)

    def col(v):
        v = v.reshape(-1, P, *v.shape[1:])
        return np.moveaxis(v, 1, 0).reshape(P, -1)

    ffn_w = col(a["conv_ffn_w_2"][0].T).reshape(P, 2, FT, 3).transpose(0, 2, 1, 3).reshape(P, -1)
    vecs = np.concatenate([
        col(a["attn_norm_g"][0]), col(a["b_gate"][0]), np.tile(a["q_norm_g"][0], 2)[:, None],
        np.tile(a["k_norm_g"][0], 2)[:, None], col(a["conv_w"][0, :, 0, :].T), col(a["conv_b"][0]),
        col(a["conv_ln_g"][0]), col(a["conv_ln_b"][0]), col(a["ffn_norm_g"][0]), col(a["ple_norm_g"][0]),
        col(a["norm_mix_g_2"][0]), col(a["b_gate_2"][0]), col(a["conv_mix_w_2"][0].T), col(a["norm_ffn_g_2"][0]),
        ffn_w, col(a["norm_f_g_2"]), np.tile(a["b_f_2"][0], (P, TB))], 1)

    rel = P - np.arange(REL)
    n = np.abs(rel)
    large = 8 + (np.log(np.maximum(n, 1).astype(np.float32) / np.float32(8)) / np.float32(np.log(1024 / 8)) * 8).astype(np.int32)
    bucket = np.where(rel > 0, 16, 0) + np.where(n < 8, n, np.minimum(large, 15))
    onehot = (bucket[None, :] == np.arange(32)[:, None]).astype(np.float32)

    args = dict(
        xT=np.ascontiguousarray(a["x"][0].T.reshape(KT, P, S).transpose(1, 0, 2)),
        pT=np.ascontiguousarray(a["p"][0, 0].T.reshape(2, P, S).transpose(1, 0, 2)),
        panels=panels, vecs=vecs,
        wki=np.ascontiguousarray(wki.reshape(KT, P, 64).transpose(1, 0, 2).reshape(P, -1)),
        wwi=np.ascontiguousarray(wwi.reshape(KT, P, H).transpose(1, 0, 2).reshape(P, -1)),
        wf=np.ascontiguousarray(wf.reshape(KT, P, H).transpose(1, 0, 2).reshape(P, -1)),
        wpp=np.ascontiguousarray(a["w_ple_proj"][0].reshape(2, P, D).transpose(1, 0, 2)),
        subk=np.ascontiguousarray(a["peer_sub_keys"][0].transpose(3, 0, 1, 2).reshape(P, 16, P)),
        relb=a["rel_bias"], onehot=onehot)
    args = {k: np.ascontiguousarray(v) for k, v in args.items()}
    nc = bacc.Bacc("TRN2", target_bir_lowering=False, num_devices=1)
    aps = [nc.dram_tensor("in_" + k, v.shape, mybir.dt.float32, kind="ExternalInput").ap() for k, v in args.items()]
    out = nc.dram_tensor("y", (P, KT, S), mybir.dt.float32, kind="ExternalOutput").ap()
    build(nc, *aps, out)
    r = run_bass_kernel_spmd(nc, [{"in_" + k: v for k, v in args.items()}], core_ids=[0])
    y = r.results[0]["y"]
    return y.transpose(1, 0, 2).reshape(D, S).T.reshape(1, S, D)
```
